# Optimizing a Trainium2 kernel written in Bass

```python
import math
import jax, jax.numpy as jnp
from jax import lax
import numpy as np

D_MODEL = 1024
BATCH = 1
SEQ = 1024
DEPTH = 1
DEC_BATCH = 8
DEC_SEQ = 16
PAST_LEN = 256

CHUNK = 64
ROPE_THETA = 10000.0
NORM_EPS = 1e-6
DA_HEADS = 4
DA_HEAD_DIM = 64
DA_V_DIM = 2 * DA_HEAD_DIM
DA_Q_BLOCK = 128
SW_HEADS = 8
SW_KV_HEADS = 2
SW_GROUP = SW_HEADS // SW_KV_HEADS
SW_HEAD_DIM = 64
WINDOW = 128
WINDOW_CHUNKS = WINDOW // CHUNK
MEM_TOKENS = 256
MEM_HEADS = 4
MEM_HEAD_DIM = 128
MEM_WIDTH = MEM_HEADS * MEM_HEAD_DIM
PEER_HEADS = 8
PEER_N_KEYS = 128
PEER_N_EXPERTS = PEER_N_KEYS * PEER_N_KEYS
PEER_KEY_DIM = 128
PEER_TOPK = 16
PEER_BLOCK = 256
DA_Q_COLS = DA_HEADS * 2 * DA_HEAD_DIM
DA_K_COLS = DA_HEADS * 2 * DA_HEAD_DIM
DA_V_COLS = DA_HEADS * DA_V_DIM
SW_Q_COLS = SW_HEADS * SW_HEAD_DIM
SW_KV_COLS = SW_KV_HEADS * SW_HEAD_DIM
GATE_COLS = 2 * D_MODEL
IN_COLS = DA_Q_COLS + DA_K_COLS + DA_V_COLS + SW_Q_COLS + 2 * SW_KV_COLS + GATE_COLS

kernel_name = "hybrid_diffattn_swa_peer_stream_step"

def rms_norm(x, g):
    xf = x.astype(jnp.float32)
    y = xf * lax.rsqrt(jnp.mean(xf * xf, axis=-1, keepdims=True) + NORM_EPS)
    return (y * g.astype(jnp.float32)).astype(x.dtype)

def rope(x, pos):
    half = x.shape[-1] // 2
    inv = ROPE_THETA ** (-jnp.arange(half, dtype=jnp.float32) / half)
    ang = pos.astype(jnp.float32)[:, None] * inv[None, :]
    ang = ang.reshape(ang.shape[:1] + (1,) * (x.ndim - 3) + (half,))
    cos, sin = jnp.cos(ang), jnp.sin(ang)
    xf = x.astype(jnp.float32)
    x1, x2 = xf[..., :half], xf[..., half:]
    return jnp.concatenate([x1 * cos - x2 * sin, x2 * cos + x1 * sin], axis=-1).astype(x.dtype)

def project_in(xn, w_in, pos):
    B, T = xn.shape[:2]
    z = xn @ w_in
    sizes = (DA_Q_COLS, DA_K_COLS, DA_V_COLS, SW_Q_COLS, SW_KV_COLS, SW_KV_COLS, GATE_COLS)
    parts, off = [], 0
    for s in sizes:
        parts.append(z[..., off:off + s])
        off += s
    dq, dk, dv, sq, sk, sv, gates = parts
    dq = rope(dq.reshape(B, T, DA_HEADS, 2, DA_HEAD_DIM), pos)
    dk = rope(dk.reshape(B, T, DA_HEADS, 2, DA_HEAD_DIM), pos)
    dv = dv.reshape(B, T, DA_HEADS, DA_V_DIM)
    sq = rope(sq.reshape(B, T, SW_KV_HEADS, SW_GROUP, SW_HEAD_DIM), pos)
    sk = rope(sk.reshape(B, T, SW_KV_HEADS, SW_HEAD_DIM), pos)
    sv = sv.reshape(B, T, SW_KV_HEADS, SW_HEAD_DIM)
    g = jax.nn.sigmoid(gates.astype(jnp.float32)).astype(xn.dtype)
    return dq, dk, dv, sq, sk, sv, g[..., :D_MODEL], g[..., D_MODEL:]

def diff_attn_core(q, k, v, q_pos, k_pos, lam):
    scale = q.shape[-1] ** -0.5
    s = jnp.einsum('bqhmd,bkhmd->bhmqk', q, k).astype(jnp.float32) * scale
    visible = (k_pos[None, :] // CHUNK) <= (q_pos[:, None] // CHUNK)
    s = jnp.where(visible, s, -jnp.inf)
    p = jax.nn.softmax(s, axis=-1)
    w = p[:, :, 0] - lam * p[:, :, 1]
    return jnp.einsum('bhqk,bkhe->bqhe', w.astype(v.dtype), v)

def diff_attn_prompt(q, k, v, lam):
    B, T = q.shape[:2]
    nb = T // DA_Q_BLOCK
    k_pos = jnp.arange(T)
    qb = q.reshape((B, nb, DA_Q_BLOCK) + q.shape[2:]).swapaxes(0, 1)

    def one(args):
        q_blk, i = args
        q_pos = i * DA_Q_BLOCK + jnp.arange(DA_Q_BLOCK)
        return diff_attn_core(q_blk, k, v, q_pos, k_pos, lam)

    out = lax.map(one, (qb, jnp.arange(nb)))
    return out.swapaxes(0, 1).reshape(B, T, DA_HEADS, DA_V_DIM)

def swa_core(q, k, v, q_pos, k_pos, sinks):
    scale = q.shape[-1] ** -0.5
    s = jnp.einsum('bcqhgd,bckhd->bchgqk', q, k).astype(jnp.float32) * scale
    qc = q_pos[:, :, None] // CHUNK
    kc = k_pos[:, None, :] // CHUNK
    visible = (k_pos[:, None, :] >= 0) & (kc <= qc) & (kc >= qc - WINDOW_CHUNKS)
    s = jnp.where(visible[None, :, None, None], s, -jnp.inf)
    sink = sinks.astype(jnp.float32).reshape(SW_KV_HEADS, SW_GROUP)[None, None, :, :, None, None]
    m = jnp.maximum(jnp.max(s, axis=-1, keepdims=True), sink)
    p = jnp.exp(s - m)
    p = p / (jnp.sum(p, axis=-1, keepdims=True) + jnp.exp(sink - m))
    return jnp.einsum('bchgqk,bckhd->bcqhgd', p.astype(v.dtype), v)

def swa_prompt(q, k, v, sinks):
    B, T = q.shape[:2]
    nC = T // CHUNK
    pad = WINDOW_CHUNKS * CHUNK

    def band(a):
        ap = jnp.pad(a, ((0, 0), (pad, 0)) + ((0, 0),) * (a.ndim - 2))
        blocks = ap.reshape((B, nC + WINDOW_CHUNKS, CHUNK) + a.shape[2:])
        return jnp.concatenate([blocks[:, j:j + nC] for j in range(WINDOW_CHUNKS + 1)], axis=2)

    pos_blocks = jnp.arange(-pad, T).reshape(nC + WINDOW_CHUNKS, CHUNK)
    k_pos = jnp.concatenate([pos_blocks[j:j + nC] for j in range(WINDOW_CHUNKS + 1)], axis=1)
    q_pos = jnp.arange(T).reshape(nC, CHUNK)
    qb = q.reshape((B, nC, CHUNK) + q.shape[2:])
    out = swa_core(qb, band(k), band(v), q_pos, k_pos, sinks)
    return out.reshape(B, T, SW_HEADS * SW_HEAD_DIM)

def swa_sample(q, k_all, v_all, q_pos, k_pos, sinks):
    B, Tn = q.shape[:2]
    out = swa_core(q[:, None], k_all[:, None], v_all[:, None], q_pos[None], k_pos[None], sinks)
    return out.reshape(B, Tn, SW_HEADS * SW_HEAD_DIM)

def merge_out(oa, ob, ga, gb, subln_g, lam_init, w_a, w_b, w_out):
    B, T = oa.shape[:2]
    oa = rms_norm(oa, subln_g) * (1.0 - lam_init)
    ya = oa.reshape(B, T, -1) @ w_a
    yb = ob @ w_b
    return (ga * ya + gb * yb) @ w_out

def mem_kv(mem, g, w_k, w_v):
    B, M = mem.shape[:2]
    mn = rms_norm(mem, g)
    return ((mn @ w_k).reshape(B, M, MEM_HEADS, MEM_HEAD_DIM),
            (mn @ w_v).reshape(B, M, MEM_HEADS, MEM_HEAD_DIM))

def mem_attn(xn, mk, mv, w_q, w_o):
    B, T = xn.shape[:2]
    q = (xn @ w_q).reshape(B, T, MEM_HEADS, MEM_HEAD_DIM)
    s = jnp.einsum('bqhd,bkhd->bhqk', q, mk).astype(jnp.float32) * (MEM_HEAD_DIM ** -0.5)
    p = jax.nn.softmax(s, axis=-1)
    o = jnp.einsum('bhqk,bkhd->bqhd', p.astype(mv.dtype), mv)
    return o.reshape(B, T, MEM_WIDTH) @ w_o

def peer(xn, w_q, keys1, keys2, u, v):
    shp = xn.shape
    xt = xn.reshape(-1, shp[-1])
    n = xt.shape[0]
    blk = min(PEER_BLOCK, n)
    xt = jnp.pad(xt, ((0, (-n) % blk), (0, 0)))

    def one(xb):
        nb = xb.shape[0]
        q = (xb @ w_q).reshape(nb, PEER_HEADS, 2, PEER_KEY_DIM // 2)
        s1 = jnp.einsum('nhd,hkd->nhk', q[:, :, 0], keys1).astype(jnp.float32)
        s2 = jnp.einsum('nhd,hkd->nhk', q[:, :, 1], keys2).astype(jnp.float32)
        v1, i1 = lax.top_k(s1, PEER_TOPK)
        v2, i2 = lax.top_k(s2, PEER_TOPK)
        cand = (v1[..., :, None] + v2[..., None, :]).reshape(nb, PEER_HEADS, PEER_TOPK * PEER_TOPK)
        cidx = (i1[..., :, None] * PEER_N_KEYS + i2[..., None, :]).reshape(nb, PEER_HEADS, PEER_TOPK * PEER_TOPK)
        sc, sel = lax.top_k(cand, PEER_TOPK)
        idx = jnp.take_along_axis(cidx, sel, axis=-1)
        g = jax.nn.softmax(sc, axis=-1)
        h = jnp.einsum('nd,nhkd->nhk', xb, u[idx]).astype(jnp.float32)
        a = (jax.nn.gelu(h) * g).astype(xb.dtype)
        return jnp.einsum('nhk,nhkd->nd', a, v[idx])

    out = lax.map(one, xt.reshape(-1, blk, shp[-1]))
    return out.reshape(-1, shp[-1])[:n].reshape(shp)

def setup_inputs(seed: int = 0) -> dict:
    key = jax.random.key(seed)
    ks = iter(jax.random.split(key, 48))

    def nrm(shape, scale):
        return jax.random.normal(next(ks), shape, jnp.float32) * scale

    L, D = DEPTH, D_MODEL
    sw_rows = min(WINDOW, PAST_LEN)
    return {
        "x_prompt": nrm((BATCH, SEQ, D), 1.0),
        "mem_prompt": nrm((BATCH, MEM_TOKENS, D), 1.0),
        "x_sample": nrm((DEC_BATCH, DEC_SEQ, D), 1.0),
        "cache_diff_k": nrm((L, DEC_BATCH, PAST_LEN, DA_HEADS, 2, DA_HEAD_DIM), 1.0),
        "cache_diff_v": nrm((L, DEC_BATCH, PAST_LEN, DA_HEADS, DA_V_DIM), 1.0),
        "cache_swa_k": nrm((L, DEC_BATCH, sw_rows, SW_KV_HEADS, SW_HEAD_DIM), 1.0),
        "cache_swa_v": nrm((L, DEC_BATCH, sw_rows, SW_KV_HEADS, SW_HEAD_DIM), 1.0),
        "cache_mem_k": nrm((L, DEC_BATCH, MEM_TOKENS, MEM_HEADS, MEM_HEAD_DIM), 1.0),
        "cache_mem_v": nrm((L, DEC_BATCH, MEM_TOKENS, MEM_HEADS, MEM_HEAD_DIM), 1.0),
        "norm_mix_g": 1.0 + nrm((L, D), 0.02),
        "w_in": nrm((L, D, IN_COLS), D ** -0.5),
        "lambda_q1": nrm((L, DA_HEAD_DIM), 0.1),
        "lambda_k1": nrm((L, DA_HEAD_DIM), 0.1),
        "lambda_q2": nrm((L, DA_HEAD_DIM), 0.1),
        "lambda_k2": nrm((L, DA_HEAD_DIM), 0.1),
        "diff_subln_g": 1.0 + nrm((L, DA_V_DIM), 0.02),
        "swa_sinks": nrm((L, SW_HEADS), 0.5),
        "w_branch_a": nrm((L, DA_V_COLS, D), DA_V_COLS ** -0.5),
        "w_branch_b": nrm((L, SW_Q_COLS, D), SW_Q_COLS ** -0.5),
        "w_out": nrm((L, D, D), D ** -0.5),
        "norm_mem_g": 1.0 + nrm((L, D), 0.02),
        "norm_memkv_g": 1.0 + nrm((L, D), 0.02),
        "w_mem_q": nrm((L, D, MEM_WIDTH), D ** -0.5),
        "w_mem_k": nrm((L, D, MEM_WIDTH), D ** -0.5),
        "w_mem_v": nrm((L, D, MEM_WIDTH), D ** -0.5),
        "w_mem_o": nrm((L, MEM_WIDTH, D), MEM_WIDTH ** -0.5),
        "norm_ffn_g": 1.0 + nrm((L, D), 0.02),
        "w_peer_q": nrm((L, D, PEER_HEADS * PEER_KEY_DIM), D ** -0.5),
        "peer_keys1": nrm((L, PEER_HEADS, PEER_N_KEYS, PEER_KEY_DIM // 2), (PEER_KEY_DIM // 2) ** -0.5),
        "peer_keys2": nrm((L, PEER_HEADS, PEER_N_KEYS, PEER_KEY_DIM // 2), (PEER_KEY_DIM // 2) ** -0.5),
        "peer_u": nrm((L, PEER_N_EXPERTS, D), D ** -0.5),
        "peer_v": nrm((L, PEER_N_EXPERTS, D), 0.3),
        "final_norm_g": 1.0 + nrm((D,), 0.02),
    }

def reference(x_prompt, mem_prompt, x_sample, cache_diff_k, cache_diff_v, cache_swa_k, cache_swa_v,
              cache_mem_k, cache_mem_v, norm_mix_g, w_in, lambda_q1, lambda_k1, lambda_q2, lambda_k2,
              diff_subln_g, swa_sinks, w_branch_a, w_branch_b, w_out, norm_mem_g, norm_memkv_g,
              w_mem_q, w_mem_k, w_mem_v, w_mem_o, norm_ffn_g, w_peer_q, peer_keys1, peer_keys2,
              peer_u, peer_v, final_norm_g):
    T = x_prompt.shape[1]
    Tn = x_sample.shape[1]
    past = cache_diff_k.shape[2]
    sw_rows_s = cache_swa_k.shape[2]
    sw_rows_p = min(WINDOW, T)
    pos_p = jnp.arange(T)
    pos_s = past + jnp.arange(Tn)
    hp, hs = x_prompt, x_sample
    dkp, dvp, skp, svp, mkp, mvp, dks, dvs, sks, svs = ([] for _ in range(10))
    for l in range(DEPTH):
        lam_init = 0.8 - 0.6 * math.exp(-0.3 * l)
        f32 = jnp.float32
        lam = (jnp.exp(jnp.sum(lambda_q1[l].astype(f32) * lambda_k1[l].astype(f32)))
               - jnp.exp(jnp.sum(lambda_q2[l].astype(f32) * lambda_k2[l].astype(f32))) + lam_init)
        xn = rms_norm(hp, norm_mix_g[l])
        dq, dk, dv, sq, sk, sv, ga, gb = project_in(xn, w_in[l], pos_p)
        oa = diff_attn_prompt(dq, dk, dv, lam)
        ob = swa_prompt(sq, sk, sv, swa_sinks[l])
        hp = hp + merge_out(oa, ob, ga, gb, diff_subln_g[l], lam_init, w_branch_a[l], w_branch_b[l], w_out[l])
        mk, mv = mem_kv(mem_prompt, norm_memkv_g[l], w_mem_k[l], w_mem_v[l])
        hp = hp + mem_attn(rms_norm(hp, norm_mem_g[l]), mk, mv, w_mem_q[l], w_mem_o[l])
        hp = hp + peer(rms_norm(hp, norm_ffn_g[l]), w_peer_q[l], peer_keys1[l], peer_keys2[l], peer_u[l], peer_v[l])
        dkp.append(dk)
        dvp.append(dv)
        skp.append(sk[:, T - sw_rows_p:])
        svp.append(sv[:, T - sw_rows_p:])
        mkp.append(mk)
        mvp.append(mv)
        xn = rms_norm(hs, norm_mix_g[l])
        dq, dk, dv, sq, sk, sv, ga, gb = project_in(xn, w_in[l], pos_s)
        k_all = jnp.concatenate([cache_diff_k[l], dk], axis=1)
        v_all = jnp.concatenate([cache_diff_v[l], dv], axis=1)
        oa = diff_attn_core(dq, k_all, v_all, pos_s, jnp.arange(past + Tn), lam)
        swk_all = jnp.concatenate([cache_swa_k[l], sk], axis=1)
        swv_all = jnp.concatenate([cache_swa_v[l], sv], axis=1)
        sw_pos = jnp.concatenate([past - sw_rows_s + jnp.arange(sw_rows_s), pos_s])
        ob = swa_sample(sq, swk_all, swv_all, pos_s, sw_pos, swa_sinks[l])
        hs = hs + merge_out(oa, ob, ga, gb, diff_subln_g[l], lam_init, w_branch_a[l], w_branch_b[l], w_out[l])
        hs = hs + mem_attn(rms_norm(hs, norm_mem_g[l]), cache_mem_k[l], cache_mem_v[l], w_mem_q[l], w_mem_o[l])
        hs = hs + peer(rms_norm(hs, norm_ffn_g[l]), w_peer_q[l], peer_keys1[l], peer_keys2[l], peer_u[l], peer_v[l])
        dks.append(dk)
        dvs.append(dv)
        sks.append(swk_all[:, swk_all.shape[1] - sw_rows_s:])
        svs.append(swv_all[:, swv_all.shape[1] - sw_rows_s:])
    y_prompt = rms_norm(hp, final_norm_g)
    y_sample = rms_norm(hs, final_norm_g)
    diff_k_prompt = jnp.stack(dkp)
    diff_v_prompt = jnp.stack(dvp)
    swa_k_prompt = jnp.stack(skp)
    swa_v_prompt = jnp.stack(svp)
    mem_k_prompt = jnp.stack(mkp)
    mem_v_prompt = jnp.stack(mvp)
    diff_k_sample = jnp.stack(dks)
    diff_v_sample = jnp.stack(dvs)
    swa_k_sample = jnp.stack(sks)
    swa_v_sample = jnp.stack(svs)
    return (y_prompt, y_sample, diff_k_prompt, diff_v_prompt, swa_k_prompt, swa_v_prompt,
            mem_k_prompt, mem_v_prompt, diff_k_sample, diff_v_sample, swa_k_sample, swa_v_sample)


_drawn_inputs = setup_inputs


def setup_inputs(seed=0):
    import zlib

    import numpy as np

    out = dict(_drawn_inputs(seed))
    spreads = {}
    factors = {'diff_subln_g': 3.386,
     'swa_sinks': 8.0,
     'norm_mem_g': 7.316,
     'norm_memkv_g': 2.736,
     'norm_ffn_g': 2.731,
     'final_norm_g': 2.746}
    for name, (base, spread) in spreads.items():
        noise = np.random.default_rng([zlib.crc32(name.encode()), seed]).standard_normal(out[name].shape)
        drawn = base * np.exp(spread * noise) if base else spread * noise
        out[name] = __import__('jax').numpy.asarray(drawn.astype(out[name].dtype))
    for name, factor in factors.items():
        out[name] = (out[name] * factor).astype(out[name].dtype)
    return out
```

```python
from contextlib import ExitStack

import numpy as np

import concourse.bass as bass
from concourse import mybir

F32 = mybir.dt.float32
U32 = mybir.dt.uint32
ALU = mybir.AluOpType
ACT = mybir.ActivationFunctionType
AXX = mybir.AxisListType.X

P = 128
D = 1024
KD = D // P
TP = 1024
NB, TS = 8, 16
NT = 9
N = NT * P
EPS = 1e-6
CW = 512
ROPED, PLAIN = 3, 5


def along(ap, n):
    return ap.unsqueeze(2).to_broadcast([ap.shape[0], ap.shape[1], n])


def over(ap, n):
    return ap.unsqueeze(1).to_broadcast([ap.shape[0], n, ap.shape[1]])


def open_phase(nc, ctx, name):
    def sb(label, shape, dt=F32):
        return ctx.enter_context(nc.sbuf_tensor(f"{name}_{label}", shape, dt))

    def ps(label, shape, dt=F32):
        return ctx.enter_context(nc.psum_tensor(f"{name}_{label}", shape, dt))
    return sb, ps


def phase_project(nc, sem, K, I, S):
    with ExitStack() as ctx:
        sb, ps = open_phase(nc, ctx, "proj")
        xn = sb("xn", [P, D])
        xt = sb("xt", [P, KD, N])
        g = sb("g", [P, KD])
        w = sb("w", [P, 2, KD * CW])
        cos = sb("cos", [P, NT, 64])
        sin = sb("sin", [P, NT, 64])
        turned = sb("turned", [P, 3, CW])
        straight = sb("straight", [P, 3, CW])
        zs = sb("zs", [P, 3, CW])
        zt = sb("zt", [P, 3, CW])
        junk = sb("junk", [P, D])
        std = sb("std", [P, NT])
        zp = [ps(f"z{n}", [P, CW]) for n in range(3)]
        tp = [ps(f"t{n}", [P, CW]) for n in range(3)]
        xp = ps("x", [P, D])

        x_in, g_in, tab_in = sem("x_in"), sem("g_in"), sem("tab_in")
        squared, rooted, factor = sem("squared"), sem("rooted"), sem("factor")
        xn_ready, x_turned, xt_ready = sem("xn_ready"), sem("x_turned"), sem("xt_ready")
        w_in = sem("w_in")
        z_ready = sem("z_ready")
        roped, plain, small = sem("roped_rows"), sem("plain_rows"), sem("window_rows")
        zs_out = [sem(f"zs_out{n}") for n in range(3)]
        t_ready = sem("t_ready")
        zt_ready = sem("zt_ready")
        zt_out = [sem(f"zt_out{n}") for n in range(3)]
        sk_out, copies = sem("sk_out"), sem("copies")
        H, ident = K["H"], K["ident"]

        with nc.Block() as block:

            @block.sync
            def _(sp):
                sp.dma_start(H[:, 0:8, :], I["x_prompt"].rearrange("(t p) d -> p t d", p=P)).then_inc(x_in, 16)
                sp.dma_start(H[:, 8, :], I["x_sample"]).then_inc(x_in, 16)
                sp.dma_start(g[:, :], I["norm_mix_g"]).then_inc(g_in, 16)
                sp.dma_start(cos[:, :, :], I["rope_cos"].rearrange("(t p) d -> p t d", p=P)).then_inc(tab_in, 16)
                sp.dma_start(sin[:, :, :], I["rope_sin"].rearrange("(t p) d -> p t d", p=P)).then_inc(tab_in, 16)
                sp.dma_start(w[:, 0, :].rearrange("p (k n) -> p k n", k=KD),
                             I["w_in"][:, 0:CW].rearrange("(k p) n -> p k n", p=P)).then_inc(w_in, 16)

                sp.wait_ge(w_in, 16)
                sp.dma_start(w[:, 1, :].rearrange("p (k n) -> p k n", k=KD),
                             I["w_in"][:, CW:2 * CW].rearrange("(k p) n -> p k n", p=P)).then_inc(w_in, 16)

                def store_rows(c, ready, first):
                    for t in range(NT):
                        sp.wait_ge(ready, (c - first) * NT + t + 1 + 3)
                        sp.dma_start(S["z"][bass.ds(c * N + t * P, P), :], zs[:, t % 3, :]).then_inc(zs_out[t % 3], 16)

                def load_after(c):
                    sp.wait_ge(w_in, 16 * (c + 2))
                    sp.wait_ge(z_ready, (c + 1) * NT)
                    sp.dma_start(w[:, bass.ds(c % 2, 1), :].rearrange("p a (k n) -> p (a k) n", k=KD),
                                 I["w_in"][:, bass.ds((c + 2) * CW, CW)].rearrange("(k p) n -> p k n", p=P))\
                      .then_inc(w_in, 16)

                with sp.Fori(0, ROPED) as c:
                    store_rows(c, roped, 0)
                    load_after(c)
                with sp.Fori(ROPED, ROPED + PLAIN - 2) as c:
                    store_rows(c, plain, ROPED)
                    load_after(c)
                for c in range(ROPED + PLAIN - 2, ROPED + PLAIN):
                    store_rows(c, plain, ROPED)
                    if c == ROPED + PLAIN - 2:
                        sp.wait_ge(w_in, 16 * (c + 2))
                        sp.dma_start(w[:, 0, 0:KD * 256].rearrange("p (k n) -> p k n", k=KD),
                                     I["w_in"][:, 8 * CW:8 * CW + 256].rearrange("(k p) n -> p k n", p=P)).then_inc(w_in, 16)
                for t in range(NT):
                    sp.wait_ge(small, t + 1 + 3)
                    sp.dma_start(S["skv"][t * P:t * P + P, :], zs[:, t % 3, 0:256]).then_inc(zs_out[t % 3], 16)
                for n in range(3):
                    sp.wait_ge(zs_out[n], 16 * (3 * (ROPED + PLAIN + 1) + 1))

            @block.gpsimd
            def _(pool):
                pool.dma_start(S["swa_k_sample"][:, 0:P - TS, :], I["cache_swa_k"][:, TS:P, :]).then_inc(copies, 16)
                pool.dma_start(S["swa_v_sample"][:, 0:P - TS, :], I["cache_swa_v"][:, TS:P, :]).then_inc(copies, 16)
                pool.wait_ge(copies, 32)

            @block.scalar
            def _(act):
                act.sem_inc(zt_ready, 3)
                act.sem_inc(plain, 3)
                for n in range(3):
                    act.sem_inc(zt_out[n], 16)
                act.wait_ge(x_in, 32)
                with act.Fori(0, NT) as t:
                    act.drain()
                    act.activation(junk[:, :], H[:, bass.ds(t, 1), :].rearrange("p a d -> p (a d)"), ACT.Square,
                                   accum_out=K["ss"][:, bass.ds(t, 1)])
                act.drain()
                act.activation(std[:, :], K["ss"][:, 0:NT], ACT.Sqrt, scale=1.0 / D, bias=K["eps"][:, 0:1]).then_inc(rooted, 1)

                def store_turned(c, t):
                    act.wait_ge(t_ready, c * NT + t + 1)
                    act.wait_ge(zt_out[t % 3], 16 * (c * 3 + t // 3 + 1))
                    act.activation(zt[:, t % 3, :], tp[t % 3][:, :], ACT.Copy).then_inc(zt_ready, 1)
                    act.wait_ge(zt_ready, c * NT + t + 1 + 3)
                    act.dma_start(S["zt"][bass.ds(c * 4, 4), :, t * P:t * P + P].rearrange("j p n -> p j n"),
                                  zt[:, t % 3, :].rearrange("p (j n) -> p j n", j=4)).then_inc(zt_out[t % 3], 16)

                with act.Fori(0, ROPED) as c:
                    for t in range(NT):
                        store_turned(c, t)
                with act.Fori(ROPED, ROPED + PLAIN) as c:
                    for t in range(NT):
                        act.wait_ge(z_ready, c * NT + t + 1)
                        act.wait_ge(zs_out[t % 3], 16 * (c * 3 + t // 3 + 1))
                        act.activation(zs[:, t % 3, :], zp[t % 3][:, :], ACT.Copy).then_inc(plain, 1)
                for t in range(NT):
                    c = ROPED
                    act.wait_ge(t_ready, c * NT + t + 1)
                    act.wait_ge(zt_out[t % 3], 16 * (c * 3 + 1) + 64 * (t // 3))
                    act.activation(zt[:, t % 3, 0:P], tp[t % 3][:, 0:P], ACT.Copy).then_inc(zt_ready, 1)
                    act.wait_ge(zt_ready, c * NT + t + 1 + 3)
                    for kv in range(2):
                        for half in range(2):
                            act.dma_start(S["skt"][2 * kv:2 * kv + 2, 64 * half:64 * half + 64, t * P:t * P + P]
                                          .rearrange("j p n -> p j n"),
                                          zt[64 * kv:64 * kv + 64, t % 3, 0:P].unsqueeze(1).to_broadcast([64, 2, P]))\
                               .then_inc(zt_out[t % 3], 16)
                for n in range(3):
                    act.wait_ge(zt_out[n], 16 * (ROPED * 3 + 1) + 64 * 3)

            @block.vector
            def _(dve):
                dve.sem_inc(roped, 3)
                dve.sem_inc(small, 3)
                dve.sem_inc(xt_ready, 1)
                for n in range(3):
                    dve.sem_inc(zs_out[n], 16)
                dve.wait_ge(g_in, 16)
                dve.wait_ge(rooted, 1)
                dve.reciprocal(K["rstd"][:, 0:NT], std[:, :])
                with dve.Fori(0, NT) as t:
                    dve.drain()
                    dve.wait_ge(x_turned, t + 1)
                    dve.tensor_scalar(xn[:, :], H[:, bass.ds(t, 1), :].rearrange("p a d -> p (a d)"),
                                      K["rstd"][:, bass.ds(t, 1)], None, ALU.mult).then_inc(xn_ready, 1)
                    dve.wait_ge(x_turned, t + 2)
                    dve.tensor_tensor(xt[:, :, bass.ds(t * P, P)], xp[:, :].rearrange("p (k n) -> p k n", k=KD),
                                      along(g[:, :], P), ALU.mult).then_inc(xt_ready, 1)
                dve.wait_ge(tab_in, 32)

                def rope(c, t, heads, ready):
                    n, width = t % 3, heads * 64
                    z3 = zp[n][:, 0:width].rearrange("p (h d) -> p h d", d=64)
                    r3 = turned[:, n, 0:width].rearrange("p (h d) -> p h d", d=64)
                    s3 = straight[:, n, 0:width].rearrange("p (h d) -> p h d", d=64)
                    dve.wait_ge(z_ready, c * NT + t + 1)
                    dve.tensor_tensor(s3, z3, over(cos[:, t, :], heads), ALU.mult)
                    dve.tensor_tensor(r3[:, :, 0:32], z3[:, :, 32:64], over(sin[:, t, 0:32], heads), ALU.mult)
                    dve.tensor_tensor(r3[:, :, 32:64], z3[:, :, 0:32], over(sin[:, t, 32:64], heads), ALU.mult)
                    dve.drain()
                    dve.wait_ge(zs_out[n], 16 * (c * 3 + t // 3 + 1))
                    if width < CW:
                        dve.tensor_copy(zs[:, n, width:2 * width], zp[n][:, width:2 * width])
                        dve.drain()
                    dve.tensor_tensor(zs[:, n, 0:width], straight[:, n, 0:width], turned[:, n, 0:width], ALU.add)\
                       .then_inc(ready, 1)

                with dve.Fori(0, ROPED) as c:
                    dve.drain()
                    for t in range(NT):
                        rope(c, t, 8, roped)
                dve.drain()
                for t in range(NT):
                    rope(ROPED + PLAIN, t, 2, small)

            @block.tensor
            def _(pe):
                pe.sem_inc(x_turned, 1)
                with pe.Fori(0, NT) as t:
                    pe.wait_ge(xn_ready, t + 1)
                    pe.wait_ge(xt_ready, t + 1)
                    for k in range(KD):
                        last = pe.transpose(xp[:, k * P:(k + 1) * P], xn[:, k * P:(k + 1) * P], ident[:, :])
                    last.then_inc(x_turned, 1)
                pe.wait_ge(xt_ready, NT + 1)

                def turn(c, t, blocks):
                    if blocks == 1:
                        pe.wait_ge(small, t + 1 + 3)
                    else:
                        pe.wait_ge(roped, c * NT + t + 1 + 3)
                    pe.wait_ge(zt_ready, c * NT + t + 1)
                    for j in range(blocks):
                        last = pe.transpose(tp[t % 3][:, j * P:(j + 1) * P], zs[:, t % 3, j * P:(j + 1) * P], ident[:, :])
                    last.then_inc(t_ready, 1)

                def project(c, t, width, slot, ready):
                    pe.wait_ge(ready, c * NT + t + 1)
                    for k in range(KD):
                        if slot is None:
                            rhs = w[:, 0, k * width:(k + 1) * width]
                        else:
                            rhs = w[:, bass.ds(slot, 1), k * width:(k + 1) * width].rearrange("p a n -> p (a n)")
                        last = pe.matmul(zp[t % 3][:, 0:width], xt[:, k, t * P:(t + 1) * P], rhs,
                                         start=(k == 0), stop=(k == KD - 1))
                    last.then_inc(z_ready, 1)

                with pe.Fori(0, ROPED) as c:
                    pe.wait_ge(w_in, 16 * (c + 1))
                    for t in range(NT):
                        project(c, t, CW, c % 2, roped)
                        if t > 0:
                            turn(c, t - 1, 4)
                    turn(c, NT - 1, 4)
                with pe.Fori(ROPED, ROPED + PLAIN) as c:
                    pe.wait_ge(w_in, 16 * (c + 1))
                    for t in range(NT):
                        project(c - ROPED, t, CW, c % 2, plain)
                pe.wait_ge(w_in, 16 * (ROPED + PLAIN + 1))
                pe.wait_ge(plain, PLAIN * NT + 3)
                for t in range(NT):
                    project(0, t, 256, None, small)
                    if t > 0:
                        turn(ROPED, t - 1, 1)
                turn(ROPED, NT - 1, 1)


NH = 4
PAST = 256
NKS = PAST + TS
HALF = 64
SCALE = HALF ** -0.5
FAR = -1e30
LAM0 = 0.8 - 0.6


def phase_diff(nc, sem, K, I, S):
    with ExitStack() as ctx:
        sb, ps = open_phase(nc, ctx, "diff")
        q = [sb(f"q{s}", [P, N]) for s in range(2)]
        k = [sb(f"k{s}", [P, N]) for s in range(2)]
        v = [sb(f"v{s}", [P, NT, P]) for s in range(2)]
        ck = [sb(f"ck{s}", [P, NB, NKS]) for s in range(2)]
        cv = [sb(f"cv{s}", [P, 2 * NB, P]) for s in range(2)]
        nv = [sb(f"nv{s}", [TS, NB, P]) for s in range(2)]
        qpad = sb("qpad", [P, NB * P + P])
        wpad = sb("wpad", [P, 3, NB * P + P])
        lam = sb("lam", [P, 4, HALF])
        lprod = sb("lprod", [P, 2, HALF])
        lsum = sb("lsum", [P, 2])
        lexp = sb("lexp", [P, 2])
        neglam = sb("neglam", [P, 1])
        far = sb("far", [1, HALF])
        early = sb("early", [1, P])
        pr = [[sb(f"p{a}{m}", [P, TP]) for m in range(2)] for a in range(2)]
        wt = [sb(f"wt{a}", [P, TP]) for a in range(2)]
        mx = sb("mx", [P, 2, 2])
        negm = sb("negm", [P, 2, 2])
        den = sb("den", [P, 2, 2])
        rden = sb("rden", [P, 2, 2])
        ratio = sb("ratio", [P, 2])
        junk = sb("junk", [P, P])
        sp_ = [ps(f"s{m}", [P, TP]) for m in range(2)]
        tp = [ps(f"t{a}", [P, 4, P]) for a in range(2)]
        op = [ps(f"o{a}", [P, P]) for a in range(2)]

        loaded = [sem("diff_loaded0"), sem("diff_loaded1")]
        lam_in, lam_sum, lam_exp = sem("lam_in"), sem("lam_sum"), sem("lam_exp")
        constants, samples_in = sem("diff_constants"), sem("diff_samples_in")
        s_ready, m_ready = sem("diff_s_ready"), sem("diff_m_ready")
        p_ready = sem("diff_p_ready")
        w_ready, t_ready = sem("diff_w_ready"), sem("diff_t_ready")
        t_copied = sem("diff_t_copied")
        o_ready = sem("diff_o_ready")
        o_done = sem("diff_o_done")
        OA = K["OA"]
        groups = [1, 1, 1, 1, 2, 2, 2, 2, 1]
        NG = sum(groups)

        def diag(ap):
            return ap[:, 0:NB * (P + TS)].rearrange("p (b n) -> p b n", b=NB)[:, :, 0:TS]

        with nc.Block() as block:

            @block.sync
            def _(sp):
                def load(h, s):
                    col = h * P
                    for dst, src in (
                        (q[s][:, :], S["zt"][h, :, :]),
                        (k[s][:, :], S["zt"][4 + h, :, :]),
                        (ck[s][:, :, 0:PAST], I["cache_diff_kt"][h].rearrange("p (b n) -> p b n", b=NB)),
                        (v[s][:, :, :], S["z"][3 * N:4 * N, col:col + P].rearrange("(t p) e -> p t e", p=P)),
                        (cv[s][:, :, :], I["cache_diff_v"][:, col:col + P].rearrange("(b p) e -> p b e", p=P)),
                        (nv[s][:, :, :], S["z"][3 * N + TP:4 * N, col:col + P].rearrange("(b p) e -> p b e", p=TS)),
                    ):
                        sp.dma_start(dst, src).then_inc(loaded[s], 16)

                sp.dma_start(lam[:, :, :], I["lambdas"].partition_broadcast(P)).then_inc(lam_in, 16)
                load(0, 0)
                load(1, 1)
                for s in range(2):
                    sp.wait_ge(o_ready, NT * (s + 1) + 2)
                    load(2 + s, s)

            @block.gpsimd
            def _(pool):
                pool.memset(qpad[:, :], 0.0).then_inc(constants, 1)
                pool.memset(wpad[:, :, :], 0.0).then_inc(constants, 1)
                pool.memset(far[:, :], FAR).then_inc(constants, 1)
                pool.memset(early[:, 0:HALF], 1.0).then_inc(constants, 1)
                pool.memset(early[:, HALF:P], 0.0).then_inc(constants, 1)

            @block.scalar
            def _(act):
                act.sem_inc(p_ready, 2)
                act.sem_inc(t_copied, 2)
                act.wait_ge(constants, 5)
                act.wait_ge(lam_sum, 1)
                act.activation(lexp[:, :], lsum[:, :], ACT.Exp).then_inc(lam_exp, 1)

                def exponents(h, s, i):
                    n, a = h * NT + i, (s * NT + i) % 2
                    width = (i + 1) * P if i < 8 else NKS
                    for m in range(2):
                        act.wait_ge(m_ready, 2 * n + m + 1)
                        act.activation(pr[a][m][:, 0:width], sp_[m][:, 0:width], ACT.Exp, scale=SCALE,
                                       bias=negm[:, a, m:m + 1], accum_out=den[:, a, m:m + 1]).then_inc(p_ready, 1)

                def copy_turned(h, s, i):
                    n, a = h * NT + i, (s * NT + i) % 2
                    first = sum(groups[:i])
                    act.wait_ge(o_ready, n + 1)
                    for c in range(groups[i]):
                        g = first + c
                        bank = tp[(s * NG + g) % 2]
                        act.wait_ge(t_ready, h * NG + g + 1)
                        if i < 8:
                            w = min(4, i + 1 - 4 * c) * P
                            act.activation(wt[a][:, c * 4 * P:c * 4 * P + w],
                                           bank[:, :, :].rearrange("p j n -> p (j n)")[:, 0:w], ACT.Copy)\
                               .then_inc(t_copied, 1)
                        else:
                            for j in range(3):
                                rows = P if j < 2 else TS
                                last = act.activation(diag(wpad[0:rows, j, :]),
                                                      bank[0:rows, j, :].rearrange("p (b n) -> p b n", b=NB), ACT.Copy)
                            last.then_inc(t_copied, 1)

                def squares(h, s, i):
                    act.wait_ge(o_done, h * NT + i + 1 + 2)
                    act.activation(junk[:, :], OA[:, i, bass.ds(h * P, P)], ACT.Square,
                                   accum_out=K["sso"][:, bass.ds(h + NH * i, 1)])
                    act.drain()

                with act.Fori(0, 2) as pair:
                    for s in range(2):
                        h = pair * 2 + s
                        for i in range(NT + 1):
                            if i < NT:
                                exponents(h, s, i)
                            if i >= 1:
                                copy_turned(h, s, i - 1)
                            if i >= 2:
                                squares(h, s, i - 2)
                        squares(h, s, NT - 1)

            @block.vector
            def _(dve):
                dve.sem_inc(o_done, 2)
                dve.wait_ge(lam_in, 16)
                dve.tensor_tensor(lprod[:, :, :], lam[:, 0:2, :], lam[:, 2:4, :], ALU.mult)
                dve.drain()
                dve.tensor_reduce(lsum[:, :], lprod[:, :, :], AXX, ALU.add).then_inc(lam_sum, 1)
                dve.wait_ge(lam_exp, 1)
                dve.scalar_tensor_tensor(out=neglam[:, :], in0=lexp[:, 1:2], scalar=-LAM0, in1=lexp[:, 0:1],
                                         op0=ALU.add, op1=ALU.subtract)
                dve.wait_ge(constants, 5)

                def maxima(h, s, i):
                    n, a = h * NT + i, (s * NT + i) % 2
                    width = (i + 1) * P if i < 8 else NKS
                    for m in range(2):
                        dve.wait_ge(s_ready, 2 * n + m + 1)
                        dve.tensor_reduce(mx[:, a, m:m + 1], sp_[m][:, 0:width], AXX, ALU.max)
                        dve.drain()
                        dve.tensor_scalar(negm[:, a, m:m + 1], mx[:, a, m:m + 1], -SCALE, None, ALU.mult)\
                           .then_inc(m_ready, 1)

                def combine(h, s, i):
                    n, a = h * NT + i, (s * NT + i) % 2
                    width = (i + 1) * P if i < 8 else NKS
                    dve.wait_ge(p_ready, 2 * n + 2 + 2)
                    dve.reciprocal(rden[:, a, :], den[:, a, :])
                    dve.drain()
                    dve.tensor_scalar(ratio[:, a:a + 1], den[:, a, 0:1], rden[:, a, 1:2], neglam[:, :], ALU.mult, ALU.mult)
                    dve.drain()
                    dve.scalar_tensor_tensor(out=pr[a][0][:, 0:width], in0=pr[a][1][:, 0:width], scalar=ratio[:, a:a + 1],
                                             in1=pr[a][0][:, 0:width], op0=ALU.mult, op1=ALU.add).then_inc(w_ready, 1)

                def finish(h, s, i):
                    n, a = h * NT + i, (s * NT + i) % 2
                    dve.wait_ge(o_ready, n + 1 + 2)
                    dve.tensor_scalar(OA[:, i, bass.ds(h * P, P)], op[a][:, :], rden[:, a, 0:1], None, ALU.mult)\
                       .then_inc(o_done, 1)

                with dve.Fori(0, 2) as pair:
                    for s in range(2):
                        h = pair * 2 + s
                        dve.drain()
                        dve.wait_ge(loaded[s], (pair + 1) * 96)
                        dve.tensor_copy(diag(qpad[:, :]), q[s][:, TP:N].rearrange("p (b n) -> p b n", b=NB))
                        dve.tensor_copy(ck[s][:, :, PAST:NKS], k[s][:, TP:N].rearrange("p (b n) -> p b n", b=NB))\
                           .then_inc(samples_in, 1)
                        for i in range(NT + 1):
                            if i < NT:
                                maxima(h, s, i)
                                combine(h, s, i)
                            if i >= 1:
                                finish(h, s, i - 1)

            @block.tensor
            def _(pe):
                pe.sem_inc(o_ready, 2)

                def scores(h, s, i):
                    n = h * NT + i
                    for m in range(2):
                        lo = HALF * m
                        pe.wait_ge(p_ready, 2 * n + m + 1)
                        if i == NT - 1:
                            if m == 0:
                                pe.wait_ge(samples_in, h + 1)
                            for b in range(NB):
                                last = pe.matmul(sp_[m][:, 0:NKS], qpad[lo:lo + HALF, b * P:(b + 1) * P],
                                                 ck[s][lo:lo + HALF, b, :], start=(b == 0), stop=(b == NB - 1))
                            last.then_inc(s_ready, 1)
                            continue
                        width = (i + 1) * P
                        for c in range(0, width, 512):
                            w = min(512, width - c)
                            pe.matmul(sp_[m][:, c:c + w], q[s][lo:lo + HALF, i * P:(i + 1) * P],
                                      k[s][lo:lo + HALF, c:c + w], start=True, stop=(c + w < width))
                        pe.matmul(sp_[m][:, width - HALF:width], early[:, :], far[:, :], start=False, stop=True)\
                          .then_inc(s_ready, 1)

                def turn(h, s, i):
                    n, a = h * NT + i, (s * NT + i) % 2
                    first = sum(groups[:i])
                    pe.wait_ge(w_ready, n + 1)
                    for c in range(groups[i]):
                        g = first + c
                        pe.wait_ge(t_copied, h * NG + g + 1)
                        bank = tp[(s * NG + g) % 2]
                        blocks = 3 if i == NT - 1 else min(4, i + 1 - 4 * c)
                        for j in range(blocks):
                            at = (4 * c + j) * P
                            w = TS if i == NT - 1 and j == 2 else P
                            last = pe.transpose(bank[0:w, j, :], pr[a][0][:, at:at + w], K["ident"][:, :])
                        last.then_inc(t_ready, 1)

                def values(h, s, i):
                    n, a = h * NT + i, (s * NT + i) % 2
                    pe.wait_ge(o_done, n + 1)
                    pe.wait_ge(t_copied, h * NG + sum(groups[:i + 1]) + 2)
                    if i < NT - 1:
                        for j in range(i + 1):
                            last = pe.matmul(op[a][:, :], wt[a][:, j * P:(j + 1) * P], v[s][:, j, :],
                                             start=(j == 0), stop=(j == i))
                    else:
                        for b in range(NB):
                            for j in range(3):
                                rows = P if j < 2 else TS
                                rhs = cv[s][:, 2 * b + j, :] if j < 2 else nv[s][:, b, :]
                                last = pe.matmul(op[a][:, :], wpad[0:rows, j, b * P:(b + 1) * P], rhs,
                                                 start=(b == 0 and j == 0), stop=(b == NB - 1 and j == 2))
                    last.then_inc(o_ready, 1)

                pe.wait_ge(constants, 5)
                with pe.Fori(0, 2) as pair:
                    for s in range(2):
                        h = pair * 2 + s
                        pe.wait_ge(loaded[s], (pair + 1) * 96)
                        for i in range(NT + 1):
                            if i < NT:
                                scores(h, s, i)
                            if i >= 1:
                                turn(h, s, i - 1)
                                values(h, s, i - 1)


NPAIR = 4
NKW = P + TS


def phase_window(nc, sem, K, I, S):
    with ExitStack() as ctx:
        sb, ps = open_phase(nc, ctx, "win")
        q = [sb(f"q{s}", [P, N]) for s in range(2)]
        k = [sb(f"k{s}", [P, N]) for s in range(2)]
        v = [sb(f"v{s}", [P, NT, HALF]) for s in range(2)]
        ck = [sb(f"ck{s}", [P, NB, NKW]) for s in range(2)]
        cv = [sb(f"cv{s}", [P, NB, HALF]) for s in range(2)]
        nv = [sb(f"nv{s}", [TS, NB, HALF]) for s in range(2)]
        qpad = sb("qpad", [P, NB * P + P])
        wpad = sb("wpad", [P, 4, NB * P + P])
        sink = sb("sink", [P, 8])
        nsink = sb("nsink", [P, 8])
        far = sb("far", [1, HALF])
        seen = sb("seen", [1, 2, P])
        pr = [sb(f"p{a}", [P, 2, 2 * P]) for a in range(2)]
        wt = [sb(f"wt{a}", [P, 4, P]) for a in range(2)]
        mx = sb("mx", [P, 2, 2])
        negm = sb("negm", [P, 2, 2])
        gap = sb("gap", [P, 2, 2])
        den = sb("den", [P, 2, 3, 2])
        rden = sb("rden", [P, 2, 2])
        sp_ = [ps(f"s{a}", [P, 2, 4 * P]) for a in range(2)]
        tp = [ps(f"t{a}", [P, 4, P]) for a in range(2)]
        op = [ps(f"o{a}", [P, 2, HALF]) for a in range(2)]

        loaded = [sem("win_loaded0"), sem("win_loaded1")]
        sink_in, constants, samples_in = sem("win_sink_in"), sem("win_constants"), sem("win_samples_in")
        s_ready, m_ready = sem("win_s_ready"), sem("win_m_ready")
        p_ready = sem("win_p_ready")
        t_ready = sem("win_t_ready")
        t_copied = sem("win_t_copied")
        o_ready = sem("win_o_ready")
        o_done = sem("win_o_done")
        new_rows = sem("win_new_rows")
        OB = K["OB"]

        def diag(ap):
            return ap[:, 0:NB * (P + TS)].rearrange("p (b n) -> p b n", b=NB)[:, :, 0:TS]

        with nc.Block() as block:

            @block.sync
            def _(sp):
                def load(j, kv, s):
                    for dst, src in (
                        (q[s][:, :], S["zt"][8 + j, :, :]),
                        (k[s][:, :], S["skt"][j, :, :]),
                        (ck[s][:, :, 0:P], I["cache_swa_kt"][kv].rearrange("p (b n) -> p b n", b=NB)),
                        (v[s][:, :, :], S["skv"][:, P + kv * HALF:P + (kv + 1) * HALF].rearrange("(t p) e -> p t e", p=P)),
                        (cv[s][:, :, :], I["cache_swa_v"][:, :, kv * HALF:(kv + 1) * HALF].rearrange("b p e -> p b e")),
                        (nv[s][:, :, :], S["skv"][TP:N, P + kv * HALF:P + (kv + 1) * HALF].rearrange("(b p) e -> p b e", p=TS)),
                    ):
                        sp.dma_start(dst, src).then_inc(loaded[s], 16)

                sp.dma_start(sink[:, :], I["swa_sinks"].partition_broadcast(P)).then_inc(sink_in, 16)
                load(0, 0, 0)
                load(1, 0, 1)
                for out, col in (("swa_k_sample", 0), ("swa_v_sample", P)):
                    sp.dma_start(S[out][:, P - TS:P, :], S["skv"][TP:N, col:col + P].rearrange("(b n) e -> b n e", n=TS))\
                      .then_inc(new_rows, 16)
                for s in range(2):
                    sp.wait_ge(o_ready, NT * (s + 1) + 2)
                    load(2 + s, 1, s)
                sp.wait_ge(new_rows, 32)

            @block.gpsimd
            def _(pool):
                pool.memset(qpad[:, :], 0.0).then_inc(constants, 1)
                pool.memset(wpad[:, :, :], 0.0).then_inc(constants, 1)
                pool.memset(far[:, :], FAR).then_inc(constants, 1)
                for a in range(2):
                    pool.memset(seen[:, a, 0:HALF], 1.0 - a).then_inc(constants, 1)
                    pool.memset(seen[:, a, HALF:P], float(a)).then_inc(constants, 1)

            @block.scalar
            def _(act):
                act.sem_inc(p_ready, 2)
                act.sem_inc(t_copied, 2)
                act.wait_ge(constants, 7)

                def exponents(j, s, i):
                    n, a = j * NT + i, (s * NT + i) % 2
                    width = P if i == 0 else 2 * P if i < 8 else NKW
                    act.wait_ge(m_ready, n + 1)
                    for r in range(2):
                        act.activation(pr[a][:, r, 0:width], sp_[a][:, r, 0:width], ACT.Exp, scale=SCALE,
                                       bias=negm[:, a, r:r + 1], accum_out=den[:, a, 0, r:r + 1])
                    act.activation(den[:, a, 1, :], gap[:, a, :], ACT.Exp).then_inc(p_ready, 1)

                def copy_turned(j, s, i):
                    n, a = j * NT + i, (s * NT + i) % 2
                    act.wait_ge(o_ready, n + 1)
                    act.wait_ge(t_ready, n + 1)
                    if i < NT - 1:
                        w = 2 if i == 0 else 4
                        act.activation(wt[a][:, 0:w, :], tp[a][:, 0:w, :], ACT.Copy).then_inc(t_copied, 1)
                    else:
                        for x in range(4):
                            rows = P if x % 2 == 0 else TS
                            last = act.activation(diag(wpad[0:rows, x, :]),
                                                  tp[a][0:rows, x, :].rearrange("p (b n) -> p b n", b=NB), ACT.Copy)
                        last.then_inc(t_copied, 1)

                with act.Fori(0, 2) as kv:
                    for s in range(2):
                        j = kv * 2 + s
                        for i in range(NT + 1):
                            if i < NT:
                                exponents(j, s, i)
                            if i >= 1:
                                copy_turned(j, s, i - 1)

            @block.vector
            def _(dve):
                dve.sem_inc(o_done, 2)
                dve.wait_ge(sink_in, 16)
                dve.tensor_scalar(nsink[:, :], sink[:, :], -1.0, None, ALU.mult)
                dve.wait_ge(constants, 7)

                def maxima(j, s, i):
                    n, a = j * NT + i, (s * NT + i) % 2
                    width = P if i == 0 else 2 * P if i < 8 else NKW
                    dve.wait_ge(s_ready, n + 1)
                    dve.tensor_reduce(mx[:, a, :], sp_[a][:, :, 0:width], AXX, ALU.max)
                    dve.drain()
                    dve.scalar_tensor_tensor(out=negm[:, a, :], in0=mx[:, a, :], scalar=-SCALE,
                                             in1=nsink[:, bass.ds(j * 2, 2)], op0=ALU.mult, op1=ALU.min)
                    dve.drain()
                    dve.tensor_tensor(gap[:, a, :], negm[:, a, :], nsink[:, bass.ds(j * 2, 2)], ALU.subtract)\
                       .then_inc(m_ready, 1)

                def finish(j, s, i):
                    n, a = j * NT + i, (s * NT + i) % 2
                    dve.tensor_tensor(den[:, a, 2, :], den[:, a, 0, :], den[:, a, 1, :], ALU.add)
                    dve.drain()
                    dve.reciprocal(rden[:, a, :], den[:, a, 2, :])
                    dve.drain()
                    dve.wait_ge(o_ready, n + 1 + 2)
                    dve.tensor_tensor(OB[:, i, bass.ds(j * P, P)].rearrange("p (r e) -> p r e", r=2), op[a][:, :, :],
                                      along(rden[:, a, :], HALF), ALU.mult).then_inc(o_done, 1)

                with dve.Fori(0, 2) as kv:
                    for s in range(2):
                        j = kv * 2 + s
                        dve.drain()
                        dve.wait_ge(loaded[s], (kv + 1) * 96)
                        dve.tensor_copy(diag(qpad[:, :]), q[s][:, TP:N].rearrange("p (b n) -> p b n", b=NB))
                        dve.tensor_copy(ck[s][:, :, P:NKW], k[s][:, TP:N].rearrange("p (b n) -> p b n", b=NB))\
                           .then_inc(samples_in, 1)
                        for i in range(NT + 1):
                            if i < NT:
                                maxima(j, s, i)
                            if i >= 1:
                                dve.wait_ge(p_ready, j * NT + i - 1 + 1 + 2)
                                finish(j, s, i - 1)

            @block.tensor
            def _(pe):
                pe.sem_inc(o_ready, 2)

                def scores(j, s, i):
                    n, a = j * NT + i, (s * NT + i) % 2
                    pe.wait_ge(p_ready, n + 1)
                    if i == NT - 1:
                        pe.wait_ge(samples_in, j + 1)
                    for r in range(2):
                        lo = HALF * r
                        if i == NT - 1:
                            for b in range(NB):
                                last = pe.matmul(sp_[a][:, r, 0:NKW], qpad[lo:lo + HALF, b * P:(b + 1) * P],
                                                 ck[s][lo:lo + HALF, b, :], start=(b == 0), stop=(b == NB - 1))
                            continue
                        first = max(i - 1, 0) * P
                        width = (i + 1) * P - first
                        pe.matmul(sp_[a][:, r, 0:width], q[s][lo:lo + HALF, i * P:(i + 1) * P],
                                  k[s][lo:lo + HALF, first:first + width], start=True, stop=False)
                        if i > 0:
                            pe.matmul(sp_[a][:, r, 0:HALF], seen[:, 1, :], far[:, :], start=False, stop=False)
                        last = pe.matmul(sp_[a][:, r, width - HALF:width], seen[:, 0, :], far[:, :], start=False, stop=True)
                    last.then_inc(s_ready, 1)

                def turn(j, s, i):
                    n, a = j * NT + i, (s * NT + i) % 2
                    pe.wait_ge(p_ready, n + 1 + 2)
                    pe.wait_ge(t_copied, n + 1)
                    x = 0
                    for r in range(2):
                        for c in range(1 if i == 0 else 2):
                            w = TS if i == NT - 1 and c == 1 else P
                            last = pe.transpose(tp[a][0:w, x, :], pr[a][:, r, c * P:c * P + w], K["ident"][:, :])
                            x += 1
                    last.then_inc(t_ready, 1)

                def values(j, s, i):
                    n, a = j * NT + i, (s * NT + i) % 2
                    pe.wait_ge(o_done, n + 1)
                    pe.wait_ge(t_copied, n + 1 + 2)
                    for r in range(2):
                        if i < NT - 1:
                            tiles = range(max(i - 1, 0), i + 1)
                            for c, t in enumerate(tiles):
                                last = pe.matmul(op[a][:, r, :], wt[a][:, r * len(tiles) + c, :], v[s][:, t, :],
                                                 start=(c == 0), stop=(t == i))
                            continue
                        for b in range(NB):
                            pe.matmul(op[a][:, r, :], wpad[:, 2 * r, b * P:(b + 1) * P], cv[s][:, b, :],
                                      start=(b == 0), stop=False)
                            last = pe.matmul(op[a][:, r, :], wpad[0:TS, 2 * r + 1, b * P:(b + 1) * P], nv[s][:, b, :],
                                             start=False, stop=(b == NB - 1))
                    last.then_inc(o_ready, 1)

                pe.wait_ge(constants, 7)
                with pe.Fori(0, 2) as kv:
                    for s in range(2):
                        j = kv * 2 + s
                        pe.wait_ge(loaded[s], (kv + 1) * 96)
                        for i in range(NT + 1):
                            if i < NT:
                                scores(j, s, i)
                            if i >= 1:
                                turn(j, s, i - 1)
                                values(j, s, i - 1)


def tile_of(ap, t):
    return ap[:, bass.ds(t, 1), :].rearrange("p a d -> p (a d)")


def phase_merge(nc, sem, K, I, S):
    with ExitStack() as ctx:
        sb, ps = open_phase(nc, ctx, "merge")
        wa = sb("wa", [P, 4, D])
        wb = sb("wb", [P, 4, D])
        wo = sb("wo", [P, KD, D])
        gates = sb("gates", [P, 4, CW])
        gsub = sb("gsub", [P, 1])
        gsub1 = sb("gsub1", [P, 1])
        std = sb("std", [P, NH * NT])
        rso = sb("rso", [P, NH * NT])
        oan = sb("oan", [P, CW])
        obn = sb("obn", [P, CW])
        oat = sb("oat", [P, 4, P])
        obt = sb("obt", [P, 4, P])
        ma = sb("ma", [P, D])
        mb = sb("mb", [P, D])
        m = sb("m", [P, D])
        mt = sb("mt", [P, KD, P])
        junk = sb("junk", [P, D])
        tp = [ps(f"t{a}", [P, 4, P]) for a in range(2)]
        ya, yb, yo = ps("ya", [P, D]), ps("yb", [P, D]), ps("yo", [P, D])

        w_in, gsub_in, gates_in = sem("merge_w_in"), sem("gsub_in"), sem("gates_in")
        rooted, gates_open = sem("merge_rooted"), sem("gates_open")
        gsub_ready = sem("gsub_ready")
        oan_ready, obn_ready = sem("oan_ready"), sem("obn_ready")
        t_ready = sem("merge_t_ready")
        t_copied = sem("merge_t_copied")
        y_ready, m_ready = sem("merge_y_ready"), sem("merge_m_ready")
        out_ready = sem("merge_out_ready")
        h_added = sem("merge_h_added")
        H, OA, OB = K["H"], K["OA"], K["OB"]

        with nc.Block() as block:

            @block.sync
            def _(sp):
                sp.dma_start(gsub[:, :], I["diff_subln_g"]).then_inc(gsub_in, 16)
                sp.dma_start(wa[:, :, :], I["w_branch_a"].rearrange("(k p) n -> p k n", p=P)).then_inc(w_in, 16)
                sp.dma_start(wb[:, :, :], I["w_branch_b"].rearrange("(k p) n -> p k n", p=P)).then_inc(w_in, 16)
                sp.dma_start(wo[:, :, :], I["w_out"].rearrange("(k p) n -> p k n", p=P)).then_inc(w_in, 16)
                zg = S["z"][4 * N:8 * N, :].rearrange("(c t p) n -> t p c n", c=4, p=P)
                sp.dma_start(gates[:, :, :], zg[0]).then_inc(gates_in, 16)
                with sp.Fori(1, NT) as t:
                    sp.wait_ge(m_ready, t)
                    sp.dma_start(gates[:, :, :], zg[bass.ds(t, 1)].rearrange("a p c n -> (a p) c n")).then_inc(gates_in, 16)

            @block.scalar
            def _(act):
                act.sem_inc(t_copied, 2)
                act.activation(std[:, :], K["sso"][:, :], ACT.Sqrt, scale=1.0 / P, bias=K["eps"][:, 0:1]).then_inc(rooted, 1)
                act.wait_ge(gsub_ready, 1)
                act.activation(obn[:, :], OB[:, 0, :], ACT.Copy).then_inc(obn_ready, 1)

                def copy_branches(t, first):
                    at = 0 if first else 4 * t - 2
                    if not first:
                        act.wait_ge(y_ready, t)
                    act.wait_ge(t_ready, at + 1)
                    act.activation(oat[:, :, :], tp[0][:, :, :], ACT.Copy, scale=gsub1[:, 0:1]).then_inc(t_copied, 1)
                    act.wait_ge(t_ready, at + 2)
                    act.activation(obt[:, :, :], tp[1][:, :, :], ACT.Copy).then_inc(t_copied, 1)

                def open_gates(t):
                    act.wait_ge(gates_in, 16 * (t + 1))
                    act.activation(gates[:, :, :], gates[:, :, :], ACT.Sigmoid).then_inc(gates_open, 1)

                def copy_merged(t, last_tile=False):
                    at = 4 * t + (2 if last_tile else 4)
                    act.wait_ge(out_ready, t + 1)
                    for x in range(2):
                        act.wait_ge(t_ready, at + x + 1)
                        act.activation(mt[:, 4 * x:4 * x + 4, :], tp[x][:, :, :], ACT.Copy).then_inc(t_copied, 1)

                def squares(t):
                    act.wait_ge(h_added, t + 1 + 1)
                    act.activation(junk[:, :], tile_of(H, t), ACT.Square, accum_out=K["ss"][:, bass.ds(t, 1)])
                    act.drain()

                copy_branches(0, True)
                open_gates(0)
                act.activation(obn[:, :], OB[:, 1, :], ACT.Copy).then_inc(obn_ready, 1)
                with act.Fori(1, NT - 1) as t:
                    copy_branches(t, False)
                    open_gates(t)
                    act.activation(obn[:, :], tile_of(OB, t + 1), ACT.Copy).then_inc(obn_ready, 1)
                    copy_merged(t - 1)
                    squares(t - 1)
                t = NT - 1
                copy_branches(t, False)
                open_gates(t)
                copy_merged(t - 1)
                squares(t - 1)
                copy_merged(t, last_tile=True)
                squares(t)

            @block.vector
            def _(dve):
                dve.sem_inc(h_added, 1)
                dve.wait_ge(gsub_in, 16)
                dve.tensor_scalar(gsub1[:, :], gsub[:, :], 1.0 - LAM0, None, ALU.mult).then_inc(gsub_ready, 1)
                dve.wait_ge(rooted, 1)
                dve.reciprocal(rso[:, :], std[:, :])
                dve.drain()

                def normed(t):
                    dve.tensor_tensor(oan[:, :].rearrange("p (h e) -> p h e", h=NH),
                                      tile_of(OA, t).rearrange("p (h e) -> p h e", h=NH),
                                      along(rso[:, bass.ds(t * NH, NH)], P), ALU.mult).then_inc(oan_ready, 1)

                def merged(t, first):
                    dve.wait_ge(y_ready, t + 1)
                    dve.wait_ge(gates_open, t + 1)
                    dve.tensor_tensor(ma[:, :], ya[:, :], gates[:, 0:2, :].rearrange("p c n -> p (c n)"), ALU.mult)
                    dve.tensor_tensor(mb[:, :], yb[:, :], gates[:, 2:4, :].rearrange("p c n -> p (c n)"), ALU.mult)
                    dve.drain()
                    if not first:
                        dve.wait_ge(t_ready, 4 * t + 2)
                    dve.tensor_tensor(m[:, :], ma[:, :], mb[:, :], ALU.add).then_inc(m_ready, 1)

                def residual(t):
                    dve.wait_ge(out_ready, t + 1 + 1)
                    dve.tensor_tensor(tile_of(H, t), tile_of(H, t), yo[:, :], ALU.add).then_inc(h_added, 1)

                normed(0)
                merged(0, True)
                normed(1)
                with dve.Fori(1, NT - 1) as t:
                    dve.drain()
                    merged(t, False)
                    normed(t + 1)
                    residual(t - 1)
                dve.drain()
                merged(NT - 1, False)
                residual(NT - 2)
                residual(NT - 1)

            @block.tensor
            def _(pe):
                pe.sem_inc(out_ready, 1)
                pe.wait_ge(w_in, 48)

                def branches(t, first):
                    at = 0 if first else 4 * t - 2
                    pe.wait_ge(oan_ready, t + 1)
                    pe.wait_ge(t_copied, at + 1)
                    for j in range(4):
                        last = pe.transpose(tp[0][:, j, :], oan[:, j * P:(j + 1) * P], K["ident"][:, :])
                    last.then_inc(t_ready, 1)
                    pe.wait_ge(obn_ready, t + 1)
                    pe.wait_ge(t_copied, at + 2)
                    for j in range(4):
                        last = pe.transpose(tp[1][:, j, :], obn[:, j * P:(j + 1) * P], K["ident"][:, :])
                    last.then_inc(t_ready, 1)
                    if not first:
                        pe.wait_ge(m_ready, t)
                    pe.wait_ge(t_copied, at + 2 + 2)
                    for w, src, y in ((wa, oat, ya), (wb, obt, yb)):
                        for half in range(2):
                            for j in range(4):
                                last = pe.matmul(y[:, half * CW:(half + 1) * CW], src[:, j, :],
                                                 w[:, j, half * CW:(half + 1) * CW], start=(j == 0), stop=(j == 3))
                    last.then_inc(y_ready, 1)

                def output(t, last_tile=False):
                    at = 4 * t + (2 if last_tile else 4)
                    pe.wait_ge(m_ready, t + 1)
                    for x in range(2):
                        pe.wait_ge(t_copied, at + x + 1)
                        for j in range(4 * x, 4 * x + 4):
                            last = pe.transpose(tp[x][:, j % 4, :], m[:, j * P:(j + 1) * P], K["ident"][:, :])
                        last.then_inc(t_ready, 1)
                    pe.wait_ge(h_added, t + 1)
                    pe.wait_ge(t_copied, at + 2 + 2)
                    for half in range(2):
                        for j in range(KD):
                            last = pe.matmul(yo[:, half * CW:(half + 1) * CW], mt[:, j, :],
                                             wo[:, j, half * CW:(half + 1) * CW], start=(j == 0), stop=(j == KD - 1))
                    last.then_inc(out_ready, 1)

                branches(0, True)
                with pe.Fori(1, NT) as t:
                    branches(t, False)
                    output(t - 1)
                output(NT - 1, last_tile=True)


NM = 256
MSCALE = P ** -0.5


def phase_memory(nc, sem, K, I, S):
    with ExitStack() as ctx:
        sb, ps = open_phase(nc, ctx, "mem")
        wq = sb("wq", [P, KD, CW])
        wkv = sb("wkv", [P, 2, KD, CW])
        wo = sb("wo", [P, 4, D])
        g = sb("g", [P, KD])
        gkv = sb("gkv", [P, KD])
        mem = sb("mem", [P, 2, D])
        mss = sb("mss", [P, 2])
        mstd = sb("mstd", [P, 2])
        mrstd = sb("mrstd", [P, 2])
        std = sb("std", [P, NT])
        mkv = sb("mkv", [P, 2, 2, CW])
        mkt = sb("mkt", [P, 4, NM])
        ckt = sb("ckt", [P, 4, NB * NM])
        cv = wkv[:, :, :, :].rearrange("p c k n -> p (c k) n")
        xn = sb("xn", [P, D])
        xt = sb("xt", [P, KD, P])
        qt = sb("qt", [P, 4, P])
        qpad = sb("qpad", [P, 4, NB * P + P])
        pr = sb("pr", [P, 4, NM])
        pt = sb("pt", [P, KD, P])
        ot = sb("ot", [P, 4, P])
        mx = sb("mx", [P, 4])
        negm = sb("negm", [P, 4])
        den = sb("den", [P, 4])
        rden = sb("rden", [P, 4])
        junk = sb("junk", [P, D])
        tp = ps("t", [P, KD, P])
        qp = ps("q", [P, 4, P])
        op = ps("o", [P, 4, P])
        sp_ = ps("s", [P, 4, NM])
        yo = ps("y", [P, D])

        m_in, w_in, g_in, cache_in = sem("mem_in"), sem("mem_w_in"), sem("mem_g_in"), sem("mem_cache_in")
        squared, rooted, padded = sem("mem_squared"), sem("mem_rooted"), sem("mem_padded")
        x_ready = sem("mem_x_ready")
        x_turned, xt_ready = sem("mem_x_turned"), sem("mem_xt_ready")
        kv_ready, kv_copied = sem("mem_kv_ready"), sem("mem_kv_copied")
        k_turned, k_copied, kv_out = sem("mem_k_turned"), sem("mem_k_copied"), sem("mem_kv_out")
        q_ready, q_copied = sem("mem_q_ready"), sem("mem_q_copied")
        s_ready, m_ready, p_ready, p_normed = sem("mem_s_ready"), sem("mem_m_ready"), sem("mem_p_ready"), sem("mem_p_normed")
        p_turned, pt_ready = sem("mem_p_turned"), sem("mem_pt_ready")
        o_ready, o_copied = sem("mem_o_ready"), sem("mem_o_copied")
        out_ready, h_added = sem("mem_out_ready"), sem("mem_h_added")
        H, ident = K["H"], K["ident"]

        def diag(ap):
            return ap[:, 0:NB * (P + TS)].rearrange("p (b n) -> p b n", b=NB)[:, :, 0:TS]

        with nc.Block() as block:

            @block.sync
            def _(sp):
                sp.dma_start(mem[:, :, :], I["mem_prompt"].rearrange("(t p) d -> p t d", p=P)).then_inc(m_in, 16)
                sp.dma_start(gkv[:, :], I["norm_memkv_g"]).then_inc(g_in, 16)
                sp.dma_start(g[:, :], I["norm_mem_g"]).then_inc(g_in, 16)
                for c, name in enumerate(("w_mem_k", "w_mem_v")):
                    sp.dma_start(wkv[:, c, :, :], I[name].rearrange("(k p) n -> p k n", p=P)).then_inc(w_in, 16)
                sp.dma_start(wq[:, :, :], I["w_mem_q"].rearrange("(k p) n -> p k n", p=P)).then_inc(w_in, 16)
                sp.dma_start(wo[:, :, :], I["w_mem_o"].rearrange("(k p) n -> p k n", p=P)).then_inc(w_in, 16)
                sp.dma_start(ckt[:, :, :], I["cache_mem_kt"].rearrange("h p n -> p h n")).then_inc(cache_in, 16)
                sp.wait_ge(kv_ready, 4)
                sp.dma_start(cv, I["cache_mem_v"].rearrange("(b p) n -> p b n", p=P)).then_inc(cache_in, 16)
                sp.wait_ge(kv_copied, 4)
                for c, out in enumerate(("mk", "mv")):
                    sp.dma_start(S[out].rearrange("(t p) n -> p t n", p=P), mkv[:, :, c, :]).then_inc(kv_out, 16)
                sp.wait_ge(kv_out, 32)

            @block.gpsimd
            def _(pool):
                pool.memset(qpad[:, :, :], 0.0).then_inc(padded, 1)

            @block.scalar
            def _(act):
                act.wait_ge(m_in, 16)
                for t in range(2):
                    act.activation(junk[:, :], mem[:, t, :], ACT.Square, accum_out=mss[:, t:t + 1])
                    act.drain()
                act.activation(mstd[:, :], mss[:, :], ACT.Sqrt, scale=1.0 / D, bias=K["eps"][:, 0:1])
                act.activation(std[:, :], K["ss"][:, :], ACT.Sqrt, scale=1.0 / D, bias=K["eps"][:, 0:1]).then_inc(rooted, 1)
                for n in range(4):
                    t, c = n // 2, n % 2
                    act.wait_ge(kv_ready, n + 1)
                    act.activation(mkv[:, t, c, :], (qp, op)[c][:, :, :].rearrange("p h n -> p (h n)"), ACT.Copy)\
                       .then_inc(kv_copied, 1)
                for t in range(2):
                    act.wait_ge(k_turned, t + 1)
                    act.activation(mkt[:, :, t * P:(t + 1) * P], tp[:, 4 * t:4 * t + 4, :], ACT.Copy).then_inc(k_copied, 1)

                def copy_queries(t):
                    act.wait_ge(q_ready, t + 1)
                    act.activation(qt[:, :, :], qp[:, :, :], ACT.Copy).then_inc(q_copied, 1)

                def exponents(t):
                    act.wait_ge(m_ready, t + 1)
                    for h in range(4):
                        last = act.activation(pr[:, h, :], sp_[:, h, :], ACT.Exp, scale=MSCALE, bias=negm[:, h:h + 1],
                                              accum_out=den[:, h:h + 1])
                    last.then_inc(p_ready, 1)

                def copy_probs(t):
                    act.wait_ge(p_turned, t + 1)
                    act.activation(pt[:, :, :], tp[:, :, :], ACT.Copy).then_inc(pt_ready, 1)

                def copy_outputs(t):
                    act.wait_ge(o_ready, t + 1)
                    act.activation(ot[:, :, :], op[:, :, :], ACT.Copy).then_inc(o_copied, 1)

                def squares(t):
                    act.wait_ge(h_added, t + 1)
                    act.activation(junk[:, :], tile_of(H, t), ACT.Square, accum_out=K["ss"][:, bass.ds(t, 1)])
                    act.drain()

                copy_queries(0)
                exponents(0)
                with act.Fori(1, NT - 1) as t:
                    copy_probs(t - 1)
                    copy_queries(t)
                    copy_outputs(t - 1)
                    exponents(t)
                    squares(t - 1)
                t = NT - 1
                act.wait_ge(padded, 1)
                copy_probs(t - 1)
                act.wait_ge(q_ready, t + 1)
                for h in range(4):
                    last = act.activation(diag(qpad[:, h, :]), qp[:, h, :].rearrange("p (b n) -> p b n", b=NB), ACT.Copy)
                last.then_inc(q_copied, 1)
                copy_outputs(t - 1)
                exponents(t)
                squares(t - 1)
                copy_probs(t)
                copy_outputs(t)
                squares(t)

            @block.vector
            def _(dve):
                dve.wait_ge(g_in, 32)
                dve.wait_ge(rooted, 1)
                dve.reciprocal(mrstd[:, :], mstd[:, :])
                dve.reciprocal(K["rstd"][:, :], std[:, :])
                dve.drain()
                mnt = [xt, pt]
                for t in range(2):
                    if t:
                        dve.wait_ge(x_turned, t)
                    dve.tensor_scalar(xn[:, :], mem[:, t, :], mrstd[:, t:t + 1], None, ALU.mult).then_inc(x_ready, 1)
                    dve.wait_ge(x_turned, t + 1)
                    dve.tensor_tensor(mnt[t][:, :, :], tp[:, :, :], along(gkv[:, :], P), ALU.mult).then_inc(xt_ready, 1)

                def normed(t):
                    dve.tensor_scalar(xn[:, :], tile_of(H, t), K["rstd"][:, bass.ds(t, 1)], None, ALU.mult)\
                       .then_inc(x_ready, 1)

                def scaled(t):
                    dve.wait_ge(x_turned, t + 1 + 2)
                    dve.tensor_tensor(xt[:, :, :], tp[:, :, :], along(g[:, :], P), ALU.mult).then_inc(xt_ready, 1)

                def maxima(t):
                    dve.wait_ge(s_ready, t + 1)
                    dve.tensor_reduce(mx[:, :], sp_[:, :, :], AXX, ALU.max)
                    dve.drain()
                    dve.tensor_scalar(negm[:, :], mx[:, :], -MSCALE, None, ALU.mult).then_inc(m_ready, 1)

                def divided(t):
                    dve.wait_ge(p_ready, t + 1)
                    dve.reciprocal(rden[:, :], den[:, :])
                    dve.drain()
                    dve.tensor_tensor(pr[:, :, :], pr[:, :, :], along(rden[:, :], NM), ALU.mult).then_inc(p_normed, 1)

                def residual(t):
                    dve.wait_ge(out_ready, t + 1)
                    dve.tensor_tensor(tile_of(H, t), tile_of(H, t), yo[:, :], ALU.add).then_inc(h_added, 1)

                normed(0)
                scaled(0)
                normed(1)
                maxima(0)
                with dve.Fori(1, NT - 1) as t:
                    divided(t - 1)
                    scaled(t)
                    dve.drain()
                    normed(t + 1)
                    maxima(t)
                    residual(t - 1)
                t = NT - 1
                divided(t - 1)
                scaled(t)
                maxima(t)
                residual(t - 1)
                divided(t)
                residual(t)

            @block.tensor
            def _(pe):
                mnt = [xt, pt]

                def turn(n):
                    pe.wait_ge(x_ready, n + 1)
                    for k in range(KD):
                        last = pe.transpose(tp[:, k, :], xn[:, k * P:(k + 1) * P], ident[:, :])
                    last.then_inc(x_turned, 1)

                turn(0)
                pe.wait_ge(xt_ready, 1)
                turn(1)
                pe.wait_ge(w_in, 64)
                for t in range(2):
                    pe.wait_ge(xt_ready, t + 1)
                    for c in range(2):
                        if t:
                            pe.wait_ge(kv_copied, c + 1)
                        for k in range(KD):
                            last = pe.matmul((qp, op)[c][:, :, :].rearrange("p h n -> p (h n)"), mnt[t][:, k, :],
                                             wkv[:, c, k, :], start=(k == 0), stop=(k == KD - 1))
                        last.then_inc(kv_ready, 1)
                for t in range(2):
                    pe.wait_ge(kv_copied, 2 * t + 1)
                    for h in range(4):
                        last = pe.transpose(tp[:, 4 * t + h, :], mkv[:, t, 0, h * P:(h + 1) * P], ident[:, :])
                    last.then_inc(k_turned, 1)
                pe.wait_ge(k_copied, 2)
                pe.wait_ge(kv_copied, 4)

                def queries(t):
                    pe.wait_ge(xt_ready, t + 1 + 2)
                    for h in range(4):
                        for k in range(KD):
                            last = pe.matmul(qp[:, h, :], wq[:, k, h * P:(h + 1) * P], xt[:, k, :],
                                             start=(k == 0), stop=(k == KD - 1))
                    last.then_inc(q_ready, 1)

                def scores(t, first=False, samples=False):
                    pe.wait_ge(q_copied, t + 1)
                    if not first:
                        pe.wait_ge(p_ready, t)
                    for h in range(4):
                        if samples:
                            for b in range(NB):
                                last = pe.matmul(sp_[:, h, :], qpad[:, h, b * P:(b + 1) * P],
                                                 ckt[:, h, b * NM:(b + 1) * NM], start=(b == 0), stop=(b == NB - 1))
                        else:
                            last = pe.matmul(sp_[:, h, :], qt[:, h, :], mkt[:, h, :], start=True, stop=True)
                    last.then_inc(s_ready, 1)

                def turn_probs(t):
                    pe.wait_ge(p_normed, t + 1)
                    pe.wait_ge(xt_ready, min(t + 2, NT) + 2 if isinstance(t, int) else t + 2 + 2)
                    for h in range(4):
                        for j in range(2):
                            last = pe.transpose(tp[:, 2 * h + j, :], pr[:, h, j * P:(j + 1) * P], ident[:, :])
                    last.then_inc(p_turned, 1)

                def values(t, samples=False):
                    pe.wait_ge(pt_ready, t + 1)
                    for h in range(4):
                        if samples:
                            for b in range(NB):
                                for j in range(2):
                                    last = pe.matmul(op[:, h, b * TS:(b + 1) * TS], cv[:, 2 * b + j, h * P:(h + 1) * P],
                                                     pt[:, 2 * h + j, b * TS:(b + 1) * TS], start=(j == 0), stop=(j == 1))
                        else:
                            for j in range(2):
                                last = pe.matmul(op[:, h, :], mkv[:, j, 1, h * P:(h + 1) * P], pt[:, 2 * h + j, :],
                                                 start=(j == 0), stop=(j == 1))
                    last.then_inc(o_ready, 1)

                def output(t, first=False):
                    pe.wait_ge(o_copied, t + 1)
                    if not first:
                        pe.wait_ge(h_added, t)
                    for half in range(2):
                        for h in range(4):
                            last = pe.matmul(yo[:, half * CW:(half + 1) * CW], ot[:, h, :],
                                             wo[:, h, half * CW:(half + 1) * CW], start=(h == 0), stop=(h == 3))
                    last.then_inc(out_ready, 1)

                turn(2)
                queries(0)
                scores(0, first=True)
                turn(3)
                turn_probs(0)
                queries(1)
                values(0)
                scores(1)
                output(0, first=True)
                with pe.Fori(2, NT - 1) as t:
                    pe.wait_ge(pt_ready, t - 1)
                    turn(t + 2)
                    turn_probs(t - 1)
                    queries(t)
                    values(t - 1)
                    scores(t)
                    output(t - 1)
                t = NT - 1
                pe.wait_ge(cache_in, 32)
                pe.wait_ge(pt_ready, t - 1)
                turn(t + 2)
                turn_probs(t - 1)
                queries(t)
                values(t - 1)
                scores(t, samples=True)
                output(t - 1)
                turn_probs(t)
                values(t, samples=True)
                output(t)


PH = 8
NKEY = 128
TOP = 16
LOW = -3.0e38


def phase_retrieve(nc, sem, K, I, S):
    with ExitStack() as ctx:
        sb, ps = open_phase(nc, ctx, "top")
        wq = sb("wq", [P, KD, D])
        keys = sb("keys", [P, PH, NKEY])
        g = sb("g", [P, KD])
        std = sb("std", [P, NT])
        first_place = sb("first_place", [P, 2 * PH * NKEY])
        second_place = sb("second_place", [P, 2 * PH * NKEY])
        sc = first_place[:, :].rearrange("p (a h n) -> p a h n", a=2, h=PH)
        cand = first_place[:, :].rearrange("p (h n) -> p h n", h=PH)
        xn = second_place[:, 0:D]
        qt = second_place[:, D:2 * D].rearrange("p (h n) -> p h n", h=PH)
        sc2 = second_place[:, :].rearrange("p (a h n) -> p a h n", a=2, h=PH)
        cand2 = second_place[:, :].rearrange("p (h n) -> p h n", h=PH)
        hot = second_place[:, :].rearrange("p (c j) -> p c j", j=TOP)
        val = sb("val", [P, 2, PH, TOP])
        ind = sb("ind", [P, 2, PH, TOP], U32)
        indf = sb("indf", [P, 2, PH, TOP])
        best = sb("best", [P, PH, TOP])
        pos = sb("pos", [P, PH, TOP], U32)
        part = sb("part", [P, 2, PH * TOP], U32)
        partf = sb("partf", [P, 2, PH * TOP])
        picked = sb("picked", [P, 3, PH * TOP])
        above = sb("above", [P, PH, TOP])
        mass = sb("mass", [P, PH])
        rmass = sb("rmass", [P, PH])
        carrier = sb("carrier", [P, 1])
        iota16 = sb("iota16", [P, TOP])
        iota = sb("iota", [P, NKEY])
        turned = sb("turned", [P, 3, P])
        left = sb("left", [P, 8, NKEY])
        right = sb("right", [P, 8, NKEY])
        tile_w = sb("tile_w", [P, NKEY, P])
        tp = ps("t", [P, KD, P])
        qp = ps("q", [P, PH, P])
        kp = [ps(f"k{x}", [P, CW]) for x in range(4)]

        w_in, g_in, iotas = sem("top_w_in"), sem("top_g_in"), sem("top_iotas")
        rooted, x_ready, x_turned, xt_ready = sem("top_rooted"), sem("top_x_ready"), sem("top_x_turned"), sem("top_xt_ready")
        q_ready, q_copied = sem("top_q_ready"), sem("top_q_copied")
        s_ready, s_copied = sem("top_s_ready"), sem("top_s_copied")
        above_ready, e_ready = sem("above_ready"), sem("above_e_ready")
        picked_ready, p_turned, turned_ready = sem("picked_ready"), sem("picked_turned"), sem("turned_ready")
        hot_ready = sem("hot_ready")
        w_made = sem("w_made")
        w_copied = sem("w_copied")
        w_stored = sem("w_stored")
        H, XT, ident = K["H"], K["XT"], K["ident"]

        with nc.Block() as block:

            @block.sync
            def _(sp):
                sp.dma_start(g[:, :], I["norm_ffn_g"]).then_inc(g_in, 16)
                sp.dma_start(wq[:, :, :], I["w_peer_q"].rearrange("(k p) n -> p k n", p=P)).then_inc(w_in, 16)
                sp.dma_start(keys[:, :, :], I["peer_keys"].rearrange("h p n -> p h n")).then_inc(w_in, 16)
                with sp.Fori(0, NT) as t:
                    sp.wait_ge(w_copied, 32 * (t + 1) + 4)
                    sp.dma_start(S["w"][:, bass.ds(t, 1), :, :].rearrange("p a j n -> p (a j n)"),
                                 tile_w[:, :, :].rearrange("p j n -> p (j n)")).then_inc(w_stored, 16)
                sp.wait_ge(w_stored, 16 * (NT + 1))

            @block.gpsimd
            def _(pool):
                pool.iota(iota16[:, :], pattern=[[1, TOP]], base=0, channel_multiplier=0,
                          allow_small_or_imprecise_dtypes=True).then_inc(iotas, 1)
                pool.iota(iota[:, :], pattern=[[1, NKEY]], base=0, channel_multiplier=0,
                          allow_small_or_imprecise_dtypes=True).then_inc(iotas, 1)

            @block.scalar
            def _(act):
                act.sem_inc(w_copied, 4)
                act.sem_inc(w_stored, 16)
                act.activation(std[:, :], K["ss"][:, :], ACT.Sqrt, scale=1.0 / D, bias=K["eps"][:, 0:1]).then_inc(rooted, 1)
                with act.Fori(0, NT) as t:
                    act.wait_ge(q_ready, t + 1)
                    act.activation(qt[:, :, :], qp[:, :, :], ACT.Copy).then_inc(q_copied, 1)
                    act.wait_ge(s_ready, t + 1)
                    for x in range(4):
                        last = act.activation(sc[:, x // 2, 4 * (x % 2):4 * (x % 2) + 4, :].rearrange("p h n -> p (h n)"),
                                              kp[x][:, :], ACT.Copy)
                    last.then_inc(s_copied, 1)
                    act.wait_ge(above_ready, t + 1)
                    act.activation(above[:, :, :], above[:, :, :], ACT.Exp).then_inc(e_ready, 1)
                    act.wait_ge(p_turned, t + 1)
                    act.activation(turned[:, :, :], tp[:, 0:3, :], ACT.Copy).then_inc(turned_ready, 1)
                    act.wait_ge(w_stored, 16 * (t + 1))
                    with act.Fori(0, 8) as i:
                        for b in range(4):
                            act.wait_ge(w_made, 32 * t + 4 * i + b + 1 + 2)
                            act.activation(tile_w[:, :, bass.ds(16 * i + 4 * b, 4)].rearrange("p j n -> p n j"),
                                           kp[b][:, :].rearrange("p (n j) -> p n j", n=4), ACT.Copy)\
                               .then_inc(w_copied, 1)

            @block.vector
            def _(dve):
                dve.wait_ge(g_in, 16)
                dve.wait_ge(iotas, 2)
                dve.wait_ge(rooted, 1)
                dve.reciprocal(K["rstd"][:, :], std[:, :])

                def halves(f):
                    for a in range(2):
                        for h in range(PH):
                            f(a, h)
                    dve.drain()

                def heads(f):
                    for h in range(PH):
                        f(h)
                    dve.drain()

                with dve.Fori(0, NT) as t:
                    dve.drain()
                    dve.tensor_scalar(xn, tile_of(H, t), K["rstd"][:, bass.ds(t, 1)], None, ALU.mult)\
                       .then_inc(x_ready, 1)
                    dve.wait_ge(x_turned, t + 1)
                    dve.tensor_tensor(XT[:, :, bass.ds(t * P, P)], tp[:, :, :], along(g[:, :], P), ALU.mult)\
                       .then_inc(xt_ready, 1)
                    dve.wait_ge(s_copied, t + 1)
                    dve.memset(carrier[:, :], 0.0)
                    halves(lambda a, h: dve.max(val[:, a, h, 0:8], sc[:, a, h, :]))
                    halves(lambda a, h: dve.max_index(ind[:, a, h, 0:8], val[:, a, h, 0:8], sc[:, a, h, :]))
                    halves(lambda a, h: dve.match_replace(sc2[:, a, h, :], val[:, a, h, 0:8], sc[:, a, h, :], LOW))
                    halves(lambda a, h: dve.max(val[:, a, h, 8:16], sc2[:, a, h, :]))
                    halves(lambda a, h: dve.max_index(ind[:, a, h, 8:16], val[:, a, h, 8:16], sc2[:, a, h, :]))
                    for h in range(PH):
                        dve.tensor_tensor(cand[:, h, :].rearrange("p (a b) -> p a b", a=TOP), along(val[:, 0, h, :], TOP),
                                          over(val[:, 1, h, :], TOP), ALU.add)
                    dve.tensor_copy(indf[:, :, :, :], ind[:, :, :, :])
                    dve.drain()
                    heads(lambda h: dve.max(best[:, h, 0:8], cand[:, h, :]))
                    heads(lambda h: dve.max_index(pos[:, h, 0:8], best[:, h, 0:8], cand[:, h, :]))
                    heads(lambda h: dve.match_replace(cand2[:, h, :], best[:, h, 0:8], cand[:, h, :], LOW))
                    heads(lambda h: dve.max(best[:, h, 8:16], cand2[:, h, :]))
                    heads(lambda h: dve.max_index(pos[:, h, 8:16], best[:, h, 8:16], cand2[:, h, :]))
                    dve.tensor_tensor(above[:, :, :], best[:, :, :], best[:, :, 0:1].to_broadcast([P, PH, TOP]), ALU.subtract)\
                       .then_inc(above_ready, 1)
                    flat = pos[:, :, :].rearrange("p h k -> p (h k)")
                    dve.tensor_scalar(part[:, 0, :], flat, 4, None, ALU.logical_shift_right)
                    dve.tensor_scalar(part[:, 1, :], flat, 15, None, ALU.bitwise_and)
                    dve.drain()
                    dve.tensor_copy(partf[:, :, :], part[:, :, :])
                    for a in range(2):
                        dve.drain()
                        dve.tensor_tensor(hot[:, :, :], along(partf[:, a, :], TOP), over(iota16[:, :], PH * TOP), ALU.is_equal)
                        dve.drain()
                        for h in range(PH):
                            hh = hot[:, h * TOP:(h + 1) * TOP, :]
                            dve.tensor_tensor(hh, hh, over(indf[:, a, h, :], TOP), ALU.mult)
                        dve.drain()
                        dve.tensor_reduce(picked[:, a, :], hot[:, :, :], AXX, ALU.add)
                    dve.wait_ge(e_ready, t + 1)
                    dve.tensor_reduce(mass[:, :], above[:, :, :], AXX, ALU.add)
                    dve.drain()
                    dve.reciprocal(rmass[:, :], mass[:, :])
                    dve.drain()
                    dve.tensor_tensor(picked[:, 2, :].rearrange("p (h k) -> p h k", h=PH), above[:, :, :],
                                      along(rmass[:, :], TOP), ALU.mult).then_inc(picked_ready, 1)
                    dve.wait_ge(turned_ready, t + 1)
                    dve.memset(carrier[:, :], 0.0)
                    with dve.Fori(0, 8) as i:
                        dve.drain()
                        for n in range(16):
                            col = i * 16 + n
                            if n % 4 == 0:
                                dve.wait_ge(w_made, 32 * t + 4 * i + n // 4 + 1)
                            dve.tensor_scalar(left[:, n % 8, :], iota[:, :], turned[:, 0, bass.ds(col, 1)], None, ALU.is_equal)
                            dve.tensor_scalar(right[:, n % 8, :], iota[:, :], turned[:, 1, bass.ds(col, 1)],
                                              turned[:, 2, bass.ds(col, 1)], ALU.is_equal, ALU.mult).then_inc(hot_ready, 1)

            @block.tensor
            def _(pe):
                pe.sem_inc(w_made, 2)
                pe.wait_ge(w_in, 32)
                with pe.Fori(0, NT) as t:
                    pe.wait_ge(x_ready, t + 1)
                    for k in range(KD):
                        last = pe.transpose(tp[:, k, :], xn[:, k * P:(k + 1) * P], ident[:, :])
                    last.then_inc(x_turned, 1)
                    pe.wait_ge(xt_ready, t + 1)
                    for h in range(PH):
                        for k in range(KD):
                            last = pe.matmul(qp[:, h, :], wq[:, k, h * P:(h + 1) * P], XT[:, k, bass.ds(t * P, P)],
                                             start=(k == 0), stop=(k == KD - 1))
                    last.then_inc(q_ready, 1)
                    pe.wait_ge(q_copied, t + 1)
                    pe.wait_ge(w_copied, 32 * t + 4)
                    for x in range(4):
                        lo = 64 * (x // 2)
                        for h in range(4):
                            hh = 4 * (x % 2) + h
                            last = pe.matmul(kp[x][:, h * P:(h + 1) * P], qt[lo:lo + 64, hh, :], keys[lo:lo + 64, hh, :],
                                             start=True, stop=True)
                    last.then_inc(s_ready, 1)
                    pe.wait_ge(picked_ready, t + 1)
                    for x in range(3):
                        last = pe.transpose(tp[:, x, :], picked[:, x, :], ident[:, :])
                    last.then_inc(p_turned, 1)
                    with pe.Fori(0, 8) as i:
                        for n in range(16):
                            if n % 4 == 0:
                                pe.wait_ge(w_copied, 32 * t + 4 * i + n // 4 + 1)
                            pe.wait_ge(hot_ready, P * t + 16 * i + n + 1)
                            last = pe.matmul(kp[n // 4][:, (n % 4) * P:(n % 4 + 1) * P], left[:, n % 8, :], right[:, n % 8, :],
                                             start=True, stop=True)
                            if n % 4 == 3:
                                last.then_inc(w_made, 1)


NE = 4
NGRP = NKEY // NE
CT = 3
TC = N // CT


def phase_experts(nc, sem, K, I, S):
    with ExitStack() as ctx:
        sb, ps = open_phase(nc, ctx, "exp")
        u = [sb(f"u{s}", [P, NE, D]) for s in range(2)]
        v = [sb(f"v{s}", [P, NE, D]) for s in range(2)]
        w = [sb(f"w{s}", [P, NT, NE * P]) for s in range(2)]
        act_out = sb("act_out", [P, 4, TC])
        hp = [ps(f"h{x}", [P, CW]) for x in range(4)]
        yp = [ps(f"y{x}", [P, CW]) for x in range(4)]
        u_in = [sem("u_in0"), sem("u_in1")]
        v_in = [sem("v_in0"), sem("v_in1")]
        w_in = [sem("ew_in0"), sem("ew_in1")]
        h_ready = sem("h_ready")
        h_taken = sem("h_taken")
        a_ready = sem("a_ready")
        y_ready = sem("y_ready")
        y_added = sem("y_added")
        H, XT = K["H"], K["XT"]
        NH3, NY = NE * CT, 2 * NT

        def tokens(s, e, first, count):
            return w[s][:, first:first + count, e * P:(e + 1) * P]

        with nc.Block() as block:

            @block.sync
            def _(sp):
                def load_u(g, s):
                    sp.dma_start(u[s][:, :, :], I["peer_u"][bass.ds(g * NE, NE)].rearrange("j p n -> p j n")).then_inc(u_in[s], 16)

                def load_v(g, s):
                    sp.dma_start(w[s][:, :, :], S["w"][:, :, bass.ds(g * NE, NE), :].rearrange("p t j n -> p t (j n)"))\
                      .then_inc(w_in[s], 16)
                    sp.dma_start(v[s][:, :, :], I["peer_v"][:, bass.ds(g * NE, NE), :]).then_inc(v_in[s], 16)

                load_u(0, 0)
                load_v(0, 0)
                load_u(1, 1)
                load_v(1, 1)
                with sp.Fori(0, NGRP // 2 - 1) as i:
                    for s in range(2):
                        g = i * 2 + s
                        sp.wait_ge(h_ready, NH3 * (g + 1))
                        load_u(g + 2, s)
                        sp.wait_ge(y_ready, NY * (g + 1))
                        load_v(g + 2, s)

            @block.scalar
            def _(act):
                with act.Fori(0, NGRP) as g:
                    for x in range(NH3):
                        act.wait_ge(h_ready, NH3 * g + x + 1)
                        act.wait_ge(a_ready, NH3 * g + x + 1)
                        act.activation(act_out[:, x % 4, :], hp[x % 4][:, 0:TC], ACT.Gelu_apprx_tanh).then_inc(h_taken, 1)

            @block.vector
            def _(dve):
                dve.sem_inc(a_ready, 4)
                dve.sem_inc(y_added, 4)

                def weigh(g, s, pair):
                    dve.wait_ge(w_in[s], 16 * (pair + 1))
                    for x in range(NH3):
                        e, c = x // CT, x % CT
                        nb = TC // P
                        dve.wait_ge(h_taken, NH3 * g + x + 1 + 4)
                        dst = tokens(s, e, c * nb, nb)
                        dve.tensor_tensor(dst, dst, act_out[:, x % 4, :].rearrange("p (b n) -> p b n", n=P), ALU.mult)\
                           .then_inc(a_ready, 1)

                def add_up(g, s):
                    dve.drain()
                    for x in range(NY):
                        dst = H[:, x // 2, (x % 2) * CW:(x % 2 + 1) * CW]
                        dve.wait_ge(y_ready, NY * g + x + 1)
                        dve.tensor_tensor(dst, dst, yp[(s * NY + x) % 4][:, :], ALU.add).then_inc(y_added, 1)

                weigh(0, 0, 0)
                with dve.Fori(0, NGRP // 2 - 1) as i:
                    weigh(i * 2 + 1, 1, i)
                    add_up(i * 2, 0)
                    weigh(i * 2 + 2, 0, i + 1)
                    add_up(i * 2 + 1, 1)
                weigh(NGRP - 1, 1, NGRP // 2 - 1)
                add_up(NGRP - 2, 0)
                add_up(NGRP - 1, 1)

            @block.tensor
            def _(pe):
                pe.sem_inc(h_taken, 4)

                def hidden(g, s, pair):
                    pe.wait_ge(u_in[s], 16 * (pair + 1))
                    for x in range(NH3):
                        e, c = x // CT, x % CT
                        pe.wait_ge(h_taken, NH3 * g + x + 1)
                        for k in range(KD):
                            last = pe.matmul(hp[x % 4][:, 0:TC], u[s][:, e, k * P:(k + 1) * P],
                                             XT[:, k, c * TC:(c + 1) * TC], start=(k == 0), stop=(k == KD - 1))
                        last.then_inc(h_ready, 1)

                def output(g, s, pair):
                    pe.wait_ge(v_in[s], 16 * (pair + 1))
                    pe.wait_ge(a_ready, NH3 * (g + 1) + 4)
                    for x in range(NY):
                        t, half = x // 2, x % 2
                        pe.wait_ge(y_added, NY * g + x + 1)
                        for e in range(NE):
                            last = pe.matmul(yp[(s * NY + x) % 4][:, :], w[s][:, t, e * P:(e + 1) * P],
                                             v[s][:, e, half * CW:(half + 1) * CW], start=(e == 0), stop=(e == NE - 1))
                        last.then_inc(y_ready, 1)

                hidden(0, 0, 0)
                with pe.Fori(0, NGRP // 2 - 1) as i:
                    hidden(i * 2 + 1, 1, i)
                    output(i * 2, 0, i)
                    hidden(i * 2 + 2, 0, i + 1)
                    output(i * 2 + 1, 1, i)
                hidden(NGRP - 1, 1, NGRP // 2 - 1)
                output(NGRP - 2, 0, NGRP // 2 - 1)
                output(NGRP - 1, 1, NGRP // 2 - 1)


def phase_final(nc, sem, K, I, S):
    with ExitStack() as ctx:
        sb, ps = open_phase(nc, ctx, "fin")
        g = sb("g", [P, D])
        std = sb("std", [P, NT])
        y = sb("y", [P, 3, D])
        junk = sb("junk", [P, D])
        g_in, rooted, y_ready = sem("fin_g_in"), sem("fin_rooted"), sem("fin_y_ready")
        stored = [sem(f"fin_stored{x}") for x in range(3)]
        H = K["H"]

        with nc.Block() as block:

            @block.sync
            def _(sp):
                sp.dma_start(g[:, :], I["final_norm_g"].partition_broadcast(P)).then_inc(g_in, 16)
                for x in range(3):
                    sp.sem_inc(stored[x], 16)
                with sp.Fori(0, 3) as i:
                    for x in range(3):
                        sp.wait_ge(y_ready, i * 3 + x + 1)
                        sp.dma_start(S["y"][bass.ds((i * 3 + x) * P, P), :], y[:, x, :]).then_inc(stored[x], 16)
                for x in range(3):
                    sp.wait_ge(stored[x], 64)

            @block.scalar
            def _(act):
                with act.Fori(0, NT) as t:
                    act.drain()
                    act.activation(junk[:, :], tile_of(H, t), ACT.Square, accum_out=K["ss"][:, bass.ds(t, 1)])
                act.drain()
                act.activation(std[:, :], K["ss"][:, :], ACT.Sqrt, scale=1.0 / D, bias=K["eps"][:, 0:1]).then_inc(rooted, 1)

            @block.vector
            def _(dve):
                dve.wait_ge(g_in, 16)
                dve.wait_ge(rooted, 1)
                dve.reciprocal(K["rstd"][:, :], std[:, :])
                dve.drain()
                with dve.Fori(0, 3) as i:
                    for x in range(3):
                        t = i * 3 + x
                        dve.wait_ge(stored[x], 16 * (i + 1))
                        dve.scalar_tensor_tensor(out=y[:, x, :], in0=tile_of(H, t), scalar=K["rstd"][:, bass.ds(t, 1)],
                                                 in1=g[:, :], op0=ALU.mult, op1=ALU.mult).then_inc(y_ready, 1)


def load_constants(nc, sem, K, I):
    with nc.Block() as block:
        cleared = sem("cleared")

        @block.gpsimd
        def _(pool):
            pool.memset(K["ident"][:, :], 0.0).then_inc(cleared, 1)
            pool.memset(K["eps"][:, :], EPS).then_inc(cleared, 1)
            pool.wait_ge(cleared, 2)
            pool.affine_select(out=K["ident"][:, :], in_=K["ident"][:, :], compare_op=ALU.not_equal, fill=1.0,
                               base=0, pattern=[[-1, P]], channel_multiplier=1)


def build(nc, I, O):
    with ExitStack() as ctx:
        def sem(name):
            return ctx.enter_context(nc.semaphore(name))

        def keep(name, shape, dt=F32):
            return ctx.enter_context(nc.sbuf_tensor(name, shape, dt))

        K = {
            "H": keep("H", [P, NT, D]),
            "ident": keep("ident", [P, P]),
            "eps": keep("eps", [P, 1]),
            "ss": keep("ss", [P, NT]),
            "rstd": keep("rstd", [P, NT]),
        }
        S = {n: nc.dram_tensor(f"s_{n}", shape, F32).ap() for n, shape in SCRATCH.items()}
        S.update(O)
        load_constants(nc, sem, K, I)
        for kept, phases in PHASES:
            with ExitStack() as scope:
                for name, shape in kept.items():
                    K[name] = scope.enter_context(nc.sbuf_tensor(name, shape, F32))
                for phase in phases:
                    phase(nc, sem, K, I, S)


SCRATCH = {
    "w": (P, NT, NKEY, P),
    "zt": (ROPED * 4, P, N),
    "skt": (4, P, N),
}
OUTS = {
    "y": (N, D),
    "z": ((ROPED + PLAIN) * N, CW), "skv": (N, 256),
    "mk": (2 * P, CW), "mv": (2 * P, CW),
    "swa_k_sample": (NB, P, P), "swa_v_sample": (NB, P, P),
}


def kernel(**inputs):
    import numpy as _np
    import concourse.bacc as _bacc
    from concourse import mybir as _mybir
    from concourse.bass_utils import run_bass_kernel_spmd as _run

    a = {k: _np.asarray(v) for k, v in inputs.items()}
    arrays = lay_out(a, _np)
    nc = _bacc.Bacc("TRN2", target_bir_lowering=False, num_devices=1)
    ins, feed = {}, {}
    for name, x in arrays.items():
        x = _np.ascontiguousarray(x)
        ins[name] = nc.dram_tensor(f"in_{name}", x.shape, _mybir.dt.from_np(x.dtype), kind="ExternalInput").ap()
        feed[f"in_{name}"] = x
    outs = {n: nc.dram_tensor(f"out_{n}", shape, _mybir.dt.float32, kind="ExternalOutput").ap() for n, shape in OUTS.items()}
    build(nc, ins, outs)
    r = _run(nc, [feed], core_ids=[0]).results[0]
    return give_back({n: r[f"out_{n}"] for n in OUTS})


def rope_tables(np):
    pos = np.concatenate([np.arange(TP), 256 + np.arange(NB * TS) % TS]).astype(np.float32)
    inv = np.float32(10000.0) ** (-np.arange(32, dtype=np.float32) / np.float32(32))
    angle = (pos[:, None] * inv[None, :]).astype(np.float32)
    cos, sin = np.cos(angle), np.sin(angle)
    return np.concatenate([cos, cos], 1).astype(np.float32), np.concatenate([-sin, sin], 1).astype(np.float32)


def lay_out(a, np):
    cols = a["w_in"][0]
    cos, sin = rope_tables(np)
    return {
        "x_prompt": a["x_prompt"][0], "x_sample": a["x_sample"].reshape(N - TP, D),
        "norm_mix_g": a["norm_mix_g"][0].reshape(KD, P).T,
        "w_in": np.concatenate([cols[:, 0:1024], cols[:, 1536:2048], cols[:, 1024:1536], cols[:, 2304:4352],
                                cols[:, 2048:2304]], axis=1),
        "rope_cos": cos, "rope_sin": sin,
        "cache_diff_kt": a["cache_diff_k"][0].reshape(NB, PAST, NH, P).transpose(2, 3, 0, 1).reshape(NH, P, NB * PAST),
        "cache_diff_v": a["cache_diff_v"][0].reshape(NB * PAST, NH * P),
        "lambdas": np.stack([a[f"lambda_{x}"][0] for x in ("q1", "q2", "k1", "k2")]),
        "cache_swa_kt": np.concatenate([a["cache_swa_k"][0].transpose(2, 3, 0, 1).reshape(2, HALF, NB * P)] * 2, axis=1),
        "diff_subln_g": a["diff_subln_g"][0].reshape(P, 1),
        "w_branch_a": a["w_branch_a"][0], "w_branch_b": a["w_branch_b"][0], "w_out": a["w_out"][0],
        "mem_prompt": a["mem_prompt"][0],
        "norm_memkv_g": a["norm_memkv_g"][0].reshape(KD, P).T, "norm_mem_g": a["norm_mem_g"][0].reshape(KD, P).T,
        "w_mem_q": a["w_mem_q"][0], "w_mem_k": a["w_mem_k"][0], "w_mem_v": a["w_mem_v"][0], "w_mem_o": a["w_mem_o"][0],
        "cache_mem_kt": a["cache_mem_k"][0].transpose(2, 3, 0, 1).reshape(4, P, NB * NM),
        "cache_mem_v": a["cache_mem_v"][0].reshape(NB * NM, CW),
        "norm_ffn_g": a["norm_ffn_g"][0].reshape(KD, P).T, "w_peer_q": a["w_peer_q"][0],
        "peer_keys": np.concatenate([a[f"peer_keys{x}"][0].transpose(0, 2, 1) for x in (1, 2)], axis=1),
        "peer_u": a["peer_u"][0].reshape(NKEY, NKEY, KD, P).transpose(1, 3, 2, 0).reshape(NKEY, P, D),
        "peer_v": a["peer_v"][0].reshape(NKEY, NKEY, D),
        "final_norm_g": a["final_norm_g"],
        "swa_sinks": a["swa_sinks"][0],
        "cache_swa_k": a["cache_swa_k"][0].reshape(NB, P, P), "cache_swa_v": a["cache_swa_v"][0].reshape(NB, P, P),
    }



def give_back(o):
    z = o["z"].reshape(ROPED + PLAIN, N, CW)
    dk, dv, skv = z[1], z[3], o["skv"]
    return (
        o["y"][:TP].reshape(1, TP, D), o["y"][TP:].reshape(NB, TS, D),
        dk[:TP].reshape(1, 1, TP, NH, 2, HALF), dv[:TP].reshape(1, 1, TP, NH, P),
        skv[TP - P:TP, 0:P].reshape(1, 1, P, 2, HALF), skv[TP - P:TP, P:2 * P].reshape(1, 1, P, 2, HALF),
        o["mk"].reshape(1, 1, NM, 4, P), o["mv"].reshape(1, 1, NM, 4, P),
        dk[TP:].reshape(1, NB, TS, NH, 2, HALF), dv[TP:].reshape(1, NB, TS, NH, P),
        o["swa_k_sample"].reshape(1, NB, P, 2, HALF), o["swa_v_sample"].reshape(1, NB, P, 2, HALF),
    )


PHASES = [
    ({"OA": [P, NT, CW], "OB": [P, NT, CW], "sso": [P, NH * NT]},
     [phase_project, phase_diff, phase_window, phase_merge]),
    ({}, [phase_memory]),
    ({"XT": [P, KD, N]}, [phase_retrieve, phase_experts]),
    ({}, [phase_final]),
]
```

```python
from contextlib import ExitStack

import numpy as np

import concourse.bass as bass
from concourse import mybir

F32 = mybir.dt.float32
F32R = mybir.dt.float32r
BF16 = mybir.dt.bfloat16
U32 = mybir.dt.uint32
ALU = mybir.AluOpType
ACT = mybir.ActivationFunctionType
AXX = mybir.AxisListType.X

P = 128
D = 1024
KD = D // P
TP = 1024
NB, TS = 8, 16
NT = 9
N = NT * P
EPS = 1e-6
CW = 512
ROPED, PLAIN = 3, 5


def along(ap, n):
    return ap.unsqueeze(2).to_broadcast([ap.shape[0], ap.shape[1], n])


def over(ap, n):
    return ap.unsqueeze(1).to_broadcast([ap.shape[0], n, ap.shape[1]])


def open_phase(nc, ctx, name):
    def sb(label, shape, dt=F32):
        return ctx.enter_context(nc.sbuf_tensor(f"{name}_{label}", shape, dt))

    def ps(label, shape, dt=F32):
        return ctx.enter_context(nc.psum_tensor(f"{name}_{label}", shape, dt))
    return sb, ps


def phase_project(nc, sem, K, I, S):
    with ExitStack() as ctx:
        sb, ps = open_phase(nc, ctx, "proj")
        xn = sb("xn", [P, D])
        xt = sb("xt", [P, KD, N])
        g = sb("g", [P, KD])
        w = sb("w", [P, 2, KD * CW])
        cos = sb("cos", [P, NT, 64])
        sin = sb("sin", [P, NT, 64])
        turned = sb("turned", [P, 3, CW])
        straight = sb("straight", [P, 3, CW])
        zs = sb("zs", [P, 3, CW])
        zt = sb("zt", [P, 3, CW])
        junk = sb("junk", [P, D])
        std = sb("std", [P, NT])
        zp = [ps(f"z{n}", [P, CW]) for n in range(3)]
        tp = [ps(f"t{n}", [P, CW]) for n in range(3)]
        xp = ps("x", [P, D])

        x_in, g_in, tab_in = sem("x_in"), sem("g_in"), sem("tab_in")
        squared, rooted, factor = sem("squared"), sem("rooted"), sem("factor")
        xn_ready, x_turned, xt_ready = sem("xn_ready"), sem("x_turned"), sem("xt_ready")
        w_in = sem("w_in")
        z_ready = sem("z_ready")
        roped, plain, small = sem("roped_rows"), sem("plain_rows"), sem("window_rows")
        zs_out = [sem(f"zs_out{n}") for n in range(3)]
        t_ready = sem("t_ready")
        zt_ready = sem("zt_ready")
        zt_out = [sem(f"zt_out{n}") for n in range(3)]
        sk_out, copies = sem("sk_out"), sem("copies")
        H, ident = K["H"], K["ident"]

        with nc.Block() as block:

            @block.sync
            def _(sp):
                sp.dma_start(H[:, 0:8, :], I["x_prompt"].rearrange("(t p) d -> p t d", p=P)).then_inc(x_in, 16)
                sp.dma_start(H[:, 8, :], I["x_sample"]).then_inc(x_in, 16)
                sp.dma_start(g[:, :], I["norm_mix_g"]).then_inc(g_in, 16)
                sp.dma_start(cos[:, :, :], I["rope_cos"].rearrange("(t p) d -> p t d", p=P)).then_inc(tab_in, 16)
                sp.dma_start(sin[:, :, :], I["rope_sin"].rearrange("(t p) d -> p t d", p=P)).then_inc(tab_in, 16)
                sp.dma_start(w[:, 0, :].rearrange("p (k n) -> p k n", k=KD),
                             I["w_in"][:, 0:CW].rearrange("(k p) n -> p k n", p=P)).then_inc(w_in, 16)

                sp.wait_ge(w_in, 16)
                sp.dma_start(w[:, 1, :].rearrange("p (k n) -> p k n", k=KD),
                             I["w_in"][:, CW:2 * CW].rearrange("(k p) n -> p k n", p=P)).then_inc(w_in, 16)

                def store_rows(c, ready, first):
                    for t in range(NT):
                        sp.wait_ge(ready, (c - first) * NT + t + 1 + 3)
                        sp.dma_start(S["z"][bass.ds(c * N + t * P, P), :], zs[:, t % 3, :]).then_inc(zs_out[t % 3], 16)

                def load_after(c):
                    sp.wait_ge(w_in, 16 * (c + 2))
                    sp.wait_ge(z_ready, (c + 1) * NT)
                    sp.dma_start(w[:, bass.ds(c % 2, 1), :].rearrange("p a (k n) -> p (a k) n", k=KD),
                                 I["w_in"][:, bass.ds((c + 2) * CW, CW)].rearrange("(k p) n -> p k n", p=P))\
                      .then_inc(w_in, 16)

                with sp.Fori(0, ROPED) as c:
                    store_rows(c, roped, 0)
                    load_after(c)
                with sp.Fori(ROPED, ROPED + PLAIN - 2) as c:
                    store_rows(c, plain, ROPED)
                    load_after(c)
                for c in range(ROPED + PLAIN - 2, ROPED + PLAIN):
                    store_rows(c, plain, ROPED)
                    if c == ROPED + PLAIN - 2:
                        sp.wait_ge(w_in, 16 * (c + 2))
                        sp.dma_start(w[:, 0, 0:KD * 256].rearrange("p (k n) -> p k n", k=KD),
                                     I["w_in"][:, 8 * CW:8 * CW + 256].rearrange("(k p) n -> p k n", p=P)).then_inc(w_in, 16)
                for t in range(NT):
                    sp.wait_ge(small, t + 1 + 3)
                    sp.dma_start(S["skv"][t * P:t * P + P, :], zs[:, t % 3, 0:256]).then_inc(zs_out[t % 3], 16)
                for n in range(3):
                    sp.wait_ge(zs_out[n], 16 * (3 * (ROPED + PLAIN + 1) + 1))

            @block.gpsimd
            def _(pool):
                pool.dma_start(S["swa_k_sample"][:, 0:P - TS, :], I["cache_swa_k"][:, TS:P, :]).then_inc(copies, 16)
                pool.dma_start(S["swa_v_sample"][:, 0:P - TS, :], I["cache_swa_v"][:, TS:P, :]).then_inc(copies, 16)
                pool.wait_ge(copies, 32)

            @block.scalar
            def _(act):
                act.sem_inc(zt_ready, 3)
                act.sem_inc(plain, 3)
                for n in range(3):
                    act.sem_inc(zt_out[n], 16)
                act.wait_ge(x_in, 32)
                with act.Fori(0, NT) as t:
                    act.drain()
                    act.activation(junk[:, :], H[:, bass.ds(t, 1), :].rearrange("p a d -> p (a d)"), ACT.Square,
                                   accum_out=K["ss"][:, bass.ds(t, 1)])
                act.drain()
                act.activation(std[:, :], K["ss"][:, 0:NT], ACT.Sqrt, scale=1.0 / D, bias=K["eps"][:, 0:1]).then_inc(rooted, 1)

                def store_turned(c, t):
                    act.wait_ge(t_ready, c * NT + t + 1)
                    act.wait_ge(zt_out[t % 3], 16 * (c * 3 + t // 3 + 1))
                    act.activation(zt[:, t % 3, :], tp[t % 3][:, :], ACT.Copy).then_inc(zt_ready, 1)
                    act.wait_ge(zt_ready, c * NT + t + 1 + 3)
                    act.dma_start(S["zt"][bass.ds(c * 4, 4), :, t * P:t * P + P].rearrange("j p n -> p j n"),
                                  zt[:, t % 3, :].rearrange("p (j n) -> p j n", j=4)).then_inc(zt_out[t % 3], 16)

                with act.Fori(0, ROPED) as c:
                    for t in range(NT):
                        store_turned(c, t)
                with act.Fori(ROPED, ROPED + PLAIN) as c:
                    for t in range(NT):
                        act.wait_ge(z_ready, c * NT + t + 1)
                        act.wait_ge(zs_out[t % 3], 16 * (c * 3 + t // 3 + 1))
                        act.activation(zs[:, t % 3, :], zp[t % 3][:, :], ACT.Copy).then_inc(plain, 1)
                for t in range(NT):
                    c = ROPED
                    act.wait_ge(t_ready, c * NT + t + 1)
                    act.wait_ge(zt_out[t % 3], 16 * (c * 3 + 1) + 64 * (t // 3))
                    act.activation(zt[:, t % 3, 0:P], tp[t % 3][:, 0:P], ACT.Copy).then_inc(zt_ready, 1)
                    act.wait_ge(zt_ready, c * NT + t + 1 + 3)
                    for kv in range(2):
                        for half in range(2):
                            act.dma_start(S["skt"][2 * kv:2 * kv + 2, 64 * half:64 * half + 64, t * P:t * P + P]
                                          .rearrange("j p n -> p j n"),
                                          zt[64 * kv:64 * kv + 64, t % 3, 0:P].unsqueeze(1).to_broadcast([64, 2, P]))\
                               .then_inc(zt_out[t % 3], 16)
                for n in range(3):
                    act.wait_ge(zt_out[n], 16 * (ROPED * 3 + 1) + 64 * 3)

            @block.vector
            def _(dve):
                dve.sem_inc(roped, 3)
                dve.sem_inc(small, 3)
                dve.sem_inc(xt_ready, 1)
                for n in range(3):
                    dve.sem_inc(zs_out[n], 16)
                dve.wait_ge(g_in, 16)
                dve.wait_ge(rooted, 1)
                dve.reciprocal(K["rstd"][:, 0:NT], std[:, :])
                with dve.Fori(0, NT) as t:
                    dve.drain()
                    dve.wait_ge(x_turned, t + 1)
                    dve.tensor_scalar(xn[:, :], H[:, bass.ds(t, 1), :].rearrange("p a d -> p (a d)"),
                                      K["rstd"][:, bass.ds(t, 1)], None, ALU.mult).then_inc(xn_ready, 1)
                    dve.wait_ge(x_turned, t + 2)
                    dve.tensor_tensor(xt[:, :, bass.ds(t * P, P)], xp[:, :].rearrange("p (k n) -> p k n", k=KD),
                                      along(g[:, :], P), ALU.mult).then_inc(xt_ready, 1)
                dve.wait_ge(tab_in, 32)

                def rope(c, t, heads, ready):
                    n, width = t % 3, heads * 64
                    z3 = zp[n][:, 0:width].rearrange("p (h d) -> p h d", d=64)
                    r3 = turned[:, n, 0:width].rearrange("p (h d) -> p h d", d=64)
                    s3 = straight[:, n, 0:width].rearrange("p (h d) -> p h d", d=64)
                    dve.wait_ge(z_ready, c * NT + t + 1)
                    dve.tensor_tensor(s3, z3, over(cos[:, t, :], heads), ALU.mult)
                    dve.tensor_tensor(r3[:, :, 0:32], z3[:, :, 32:64], over(sin[:, t, 0:32], heads), ALU.mult)
                    dve.tensor_tensor(r3[:, :, 32:64], z3[:, :, 0:32], over(sin[:, t, 32:64], heads), ALU.mult)
                    dve.drain()
                    dve.wait_ge(zs_out[n], 16 * (c * 3 + t // 3 + 1))
                    if width < CW:
                        dve.tensor_copy(zs[:, n, width:2 * width], zp[n][:, width:2 * width])
                        dve.drain()
                    dve.tensor_tensor(zs[:, n, 0:width], straight[:, n, 0:width], turned[:, n, 0:width], ALU.add)\
                       .then_inc(ready, 1)

                with dve.Fori(0, ROPED) as c:
                    dve.drain()
                    for t in range(NT):
                        rope(c, t, 8, roped)
                dve.drain()
                for t in range(NT):
                    rope(ROPED + PLAIN, t, 2, small)

            @block.tensor
            def _(pe):
                pe.sem_inc(x_turned, 1)
                with pe.Fori(0, NT) as t:
                    pe.wait_ge(xn_ready, t + 1)
                    pe.wait_ge(xt_ready, t + 1)
                    for k in range(KD):
                        last = pe.transpose(xp[:, k * P:(k + 1) * P], xn[:, k * P:(k + 1) * P], ident[:, :])
                    last.then_inc(x_turned, 1)
                pe.wait_ge(xt_ready, NT + 1)

                def turn(c, t, blocks):
                    if blocks == 1:
                        pe.wait_ge(small, t + 1 + 3)
                    else:
                        pe.wait_ge(roped, c * NT + t + 1 + 3)
                    pe.wait_ge(zt_ready, c * NT + t + 1)
                    for j in range(blocks):
                        last = pe.transpose(tp[t % 3][:, j * P:(j + 1) * P], zs[:, t % 3, j * P:(j + 1) * P], ident[:, :])
                    last.then_inc(t_ready, 1)

                def project(c, t, width, slot, ready):
                    pe.wait_ge(ready, c * NT + t + 1)
                    for k in range(KD):
                        if slot is None:
                            rhs = w[:, 0, k * width:(k + 1) * width]
                        else:
                            rhs = w[:, bass.ds(slot, 1), k * width:(k + 1) * width].rearrange("p a n -> p (a n)")
                        last = pe.matmul(zp[t % 3][:, 0:width], xt[:, k, t * P:(t + 1) * P], rhs,
                                         start=(k == 0), stop=(k == KD - 1))
                    last.then_inc(z_ready, 1)

                with pe.Fori(0, ROPED) as c:
                    pe.wait_ge(w_in, 16 * (c + 1))
                    for t in range(NT):
                        project(c, t, CW, c % 2, roped)
                        if t > 0:
                            turn(c, t - 1, 4)
                    turn(c, NT - 1, 4)
                with pe.Fori(ROPED, ROPED + PLAIN) as c:
                    pe.wait_ge(w_in, 16 * (c + 1))
                    for t in range(NT):
                        project(c - ROPED, t, CW, c % 2, plain)
                pe.wait_ge(w_in, 16 * (ROPED + PLAIN + 1))
                pe.wait_ge(plain, PLAIN * NT + 3)
                for t in range(NT):
                    project(0, t, 256, None, small)
                    if t > 0:
                        turn(ROPED, t - 1, 1)
                turn(ROPED, NT - 1, 1)


NH = 4
PAST = 256
NKS = PAST + TS
HALF = 64
SCALE = HALF ** -0.5
FAR = -1e30
LAM0 = 0.8 - 0.6


def phase_diff(nc, sem, K, I, S):
    with ExitStack() as ctx:
        sb, ps = open_phase(nc, ctx, "diff")
        q = [sb(f"q{s}", [P, N]) for s in range(2)]
        k = [sb(f"k{s}", [P, N]) for s in range(2)]
        v = [sb(f"v{s}", [P, NT, P]) for s in range(2)]
        ck = [sb(f"ck{s}", [P, NB, NKS]) for s in range(2)]
        cv = [sb(f"cv{s}", [P, 2 * NB, P]) for s in range(2)]
        nv = [sb(f"nv{s}", [TS, NB, P]) for s in range(2)]
        qpad = sb("qpad", [P, NB * P + P])
        wpad = sb("wpad", [P, 3, NB * P + P])
        lam = sb("lam", [P, 4, HALF])
        lprod = sb("lprod", [P, 2, HALF])
        lsum = sb("lsum", [P, 2])
        lexp = sb("lexp", [P, 2])
        neglam = sb("neglam", [P, 1])
        far = sb("far", [1, HALF])
        early = sb("early", [1, P])
        pr = [[sb(f"p{a}{m}", [P, TP]) for m in range(2)] for a in range(2)]
        wt = [sb(f"wt{a}", [P, TP]) for a in range(2)]
        mx = sb("mx", [P, 2, 2])
        negm = sb("negm", [P, 2, 2])
        den = sb("den", [P, 2, 2])
        rden = sb("rden", [P, 2, 2])
        ratio = sb("ratio", [P, 2])
        junk = sb("junk", [P, P])
        sp_ = [ps(f"s{m}", [P, TP]) for m in range(2)]
        tp = [ps(f"t{a}", [P, 4, P]) for a in range(2)]
        op = [ps(f"o{a}", [P, P]) for a in range(2)]

        loaded = [sem("diff_loaded0"), sem("diff_loaded1")]
        lam_in, lam_sum, lam_exp = sem("lam_in"), sem("lam_sum"), sem("lam_exp")
        constants, samples_in = sem("diff_constants"), sem("diff_samples_in")
        s_ready, m_ready = sem("diff_s_ready"), sem("diff_m_ready")
        p_ready = sem("diff_p_ready")
        w_ready, t_ready = sem("diff_w_ready"), sem("diff_t_ready")
        t_copied = sem("diff_t_copied")
        o_ready = sem("diff_o_ready")
        o_done = sem("diff_o_done")
        OA = K["OA"]
        groups = [1, 1, 1, 1, 2, 2, 2, 2, 1]
        NG = sum(groups)

        def diag(ap):
            return ap[:, 0:NB * (P + TS)].rearrange("p (b n) -> p b n", b=NB)[:, :, 0:TS]

        with nc.Block() as block:

            @block.sync
            def _(sp):
                def load(h, s):
                    col = h * P
                    for dst, src in (
                        (q[s][:, :], S["zt"][h, :, :]),
                        (k[s][:, :], S["zt"][4 + h, :, :]),
                        (ck[s][:, :, 0:PAST], I["cache_diff_kt"][h].rearrange("p (b n) -> p b n", b=NB)),
                        (v[s][:, :, :], S["z"][3 * N:4 * N, col:col + P].rearrange("(t p) e -> p t e", p=P)),
                        (cv[s][:, :, :], I["cache_diff_v"][:, col:col + P].rearrange("(b p) e -> p b e", p=P)),
                        (nv[s][:, :, :], S["z"][3 * N + TP:4 * N, col:col + P].rearrange("(b p) e -> p b e", p=TS)),
                    ):
                        sp.dma_start(dst, src).then_inc(loaded[s], 16)

                sp.dma_start(lam[:, :, :], I["lambdas"].partition_broadcast(P)).then_inc(lam_in, 16)
                load(0, 0)
                load(1, 1)
                for s in range(2):
                    sp.wait_ge(o_ready, NT * (s + 1) + 2)
                    load(2 + s, s)

            @block.gpsimd
            def _(pool):
                pool.memset(qpad[:, :], 0.0).then_inc(constants, 1)
                pool.memset(wpad[:, :, :], 0.0).then_inc(constants, 1)
                pool.memset(far[:, :], FAR).then_inc(constants, 1)
                pool.memset(early[:, 0:HALF], 1.0).then_inc(constants, 1)
                pool.memset(early[:, HALF:P], 0.0).then_inc(constants, 1)

            @block.scalar
            def _(act):
                act.sem_inc(p_ready, 2)
                act.sem_inc(t_copied, 2)
                act.wait_ge(constants, 5)
                act.wait_ge(lam_sum, 1)
                act.activation(lexp[:, :], lsum[:, :], ACT.Exp).then_inc(lam_exp, 1)

                def exponents(h, s, i):
                    n, a = h * NT + i, (s * NT + i) % 2
                    width = (i + 1) * P if i < 8 else NKS
                    for m in range(2):
                        act.wait_ge(m_ready, 2 * n + m + 1)
                        act.activation(pr[a][m][:, 0:width], sp_[m][:, 0:width], ACT.Exp, scale=SCALE,
                                       bias=negm[:, a, m:m + 1], accum_out=den[:, a, m:m + 1]).then_inc(p_ready, 1)

                def copy_turned(h, s, i):
                    n, a = h * NT + i, (s * NT + i) % 2
                    first = sum(groups[:i])
                    act.wait_ge(o_ready, n + 1)
                    for c in range(groups[i]):
                        g = first + c
                        bank = tp[(s * NG + g) % 2]
                        act.wait_ge(t_ready, h * NG + g + 1)
                        if i < 8:
                            w = min(4, i + 1 - 4 * c) * P
                            act.activation(wt[a][:, c * 4 * P:c * 4 * P + w],
                                           bank[:, :, :].rearrange("p j n -> p (j n)")[:, 0:w], ACT.Copy)\
                               .then_inc(t_copied, 1)
                        else:
                            for j in range(3):
                                rows = P if j < 2 else TS
                                last = act.activation(diag(wpad[0:rows, j, :]),
                                                      bank[0:rows, j, :].rearrange("p (b n) -> p b n", b=NB), ACT.Copy)
                            last.then_inc(t_copied, 1)

                def squares(h, s, i):
                    act.wait_ge(o_done, h * NT + i + 1 + 2)
                    act.activation(junk[:, :], OA[:, i, bass.ds(h * P, P)], ACT.Square,
                                   accum_out=K["sso"][:, bass.ds(h + NH * i, 1)])
                    act.drain()

                with act.Fori(0, 2) as pair:
                    for s in range(2):
                        h = pair * 2 + s
                        for i in range(NT + 1):
                            if i < NT:
                                exponents(h, s, i)
                            if i >= 1:
                                copy_turned(h, s, i - 1)
                            if i >= 2:
                                squares(h, s, i - 2)
                        squares(h, s, NT - 1)

            @block.vector
            def _(dve):
                dve.sem_inc(o_done, 2)
                dve.wait_ge(lam_in, 16)
                dve.tensor_tensor(lprod[:, :, :], lam[:, 0:2, :], lam[:, 2:4, :], ALU.mult)
                dve.drain()
                dve.tensor_reduce(lsum[:, :], lprod[:, :, :], AXX, ALU.add).then_inc(lam_sum, 1)
                dve.wait_ge(lam_exp, 1)
                dve.scalar_tensor_tensor(out=neglam[:, :], in0=lexp[:, 1:2], scalar=-LAM0, in1=lexp[:, 0:1],
                                         op0=ALU.add, op1=ALU.subtract)
                dve.wait_ge(constants, 5)

                def maxima(h, s, i):
                    n, a = h * NT + i, (s * NT + i) % 2
                    width = (i + 1) * P if i < 8 else NKS
                    for m in range(2):
                        dve.wait_ge(s_ready, 2 * n + m + 1)
                        dve.tensor_reduce(mx[:, a, m:m + 1], sp_[m][:, 0:width], AXX, ALU.max)
                        dve.drain()
                        dve.tensor_scalar(negm[:, a, m:m + 1], mx[:, a, m:m + 1], -SCALE, None, ALU.mult)\
                           .then_inc(m_ready, 1)

                def combine(h, s, i):
                    n, a = h * NT + i, (s * NT + i) % 2
                    width = (i + 1) * P if i < 8 else NKS
                    dve.wait_ge(p_ready, 2 * n + 2 + 2)
                    dve.reciprocal(rden[:, a, :], den[:, a, :])
                    dve.drain()
                    dve.tensor_scalar(ratio[:, a:a + 1], den[:, a, 0:1], rden[:, a, 1:2], neglam[:, :], ALU.mult, ALU.mult)
                    dve.drain()
                    dve.scalar_tensor_tensor(out=pr[a][0][:, 0:width], in0=pr[a][1][:, 0:width], scalar=ratio[:, a:a + 1],
                                             in1=pr[a][0][:, 0:width], op0=ALU.mult, op1=ALU.add).then_inc(w_ready, 1)

                def finish(h, s, i):
                    n, a = h * NT + i, (s * NT + i) % 2
                    dve.wait_ge(o_ready, n + 1 + 2)
                    dve.tensor_scalar(OA[:, i, bass.ds(h * P, P)], op[a][:, :], rden[:, a, 0:1], None, ALU.mult)\
                       .then_inc(o_done, 1)

                with dve.Fori(0, 2) as pair:
                    for s in range(2):
                        h = pair * 2 + s
                        dve.drain()
                        dve.wait_ge(loaded[s], (pair + 1) * 96)
                        dve.tensor_copy(diag(qpad[:, :]), q[s][:, TP:N].rearrange("p (b n) -> p b n", b=NB))
                        dve.tensor_copy(ck[s][:, :, PAST:NKS], k[s][:, TP:N].rearrange("p (b n) -> p b n", b=NB))\
                           .then_inc(samples_in, 1)
                        for i in range(NT + 1):
                            if i < NT:
                                maxima(h, s, i)
                                combine(h, s, i)
                            if i >= 1:
                                finish(h, s, i - 1)

            @block.tensor
            def _(pe):
                pe.sem_inc(o_ready, 2)

                def scores(h, s, i):
                    n = h * NT + i
                    for m in range(2):
                        lo = HALF * m
                        pe.wait_ge(p_ready, 2 * n + m + 1)
                        if i == NT - 1:
                            if m == 0:
                                pe.wait_ge(samples_in, h + 1)
                            for b in range(NB):
                                last = pe.matmul(sp_[m][:, 0:NKS], qpad[lo:lo + HALF, b * P:(b + 1) * P],
                                                 ck[s][lo:lo + HALF, b, :], start=(b == 0), stop=(b == NB - 1))
                            last.then_inc(s_ready, 1)
                            continue
                        width = (i + 1) * P
                        for c in range(0, width, 512):
                            w = min(512, width - c)
                            pe.matmul(sp_[m][:, c:c + w], q[s][lo:lo + HALF, i * P:(i + 1) * P],
                                      k[s][lo:lo + HALF, c:c + w], start=True, stop=(c + w < width))
                        pe.matmul(sp_[m][:, width - HALF:width], early[:, :], far[:, :], start=False, stop=True)\
                          .then_inc(s_ready, 1)

                def turn(h, s, i):
                    n, a = h * NT + i, (s * NT + i) % 2
                    first = sum(groups[:i])
                    pe.wait_ge(w_ready, n + 1)
                    for c in range(groups[i]):
                        g = first + c
                        pe.wait_ge(t_copied, h * NG + g + 1)
                        bank = tp[(s * NG + g) % 2]
                        blocks = 3 if i == NT - 1 else min(4, i + 1 - 4 * c)
                        for j in range(blocks):
                            at = (4 * c + j) * P
                            w = TS if i == NT - 1 and j == 2 else P
                            last = pe.transpose(bank[0:w, j, :], pr[a][0][:, at:at + w], K["ident"][:, :])
                        last.then_inc(t_ready, 1)

                def values(h, s, i):
                    n, a = h * NT + i, (s * NT + i) % 2
                    pe.wait_ge(o_done, n + 1)
                    pe.wait_ge(t_copied, h * NG + sum(groups[:i + 1]) + 2)
                    if i < NT - 1:
                        for j in range(i + 1):
                            last = pe.matmul(op[a][:, :], wt[a][:, j * P:(j + 1) * P], v[s][:, j, :],
                                             start=(j == 0), stop=(j == i))
                    else:
                        for b in range(NB):
                            for j in range(3):
                                rows = P if j < 2 else TS
                                rhs = cv[s][:, 2 * b + j, :] if j < 2 else nv[s][:, b, :]
                                last = pe.matmul(op[a][:, :], wpad[0:rows, j, b * P:(b + 1) * P], rhs,
                                                 start=(b == 0 and j == 0), stop=(b == NB - 1 and j == 2))
                    last.then_inc(o_ready, 1)

                pe.wait_ge(constants, 5)
                with pe.Fori(0, 2) as pair:
                    for s in range(2):
                        h = pair * 2 + s
                        pe.wait_ge(loaded[s], (pair + 1) * 96)
                        for i in range(NT + 1):
                            if i < NT:
                                scores(h, s, i)
                            if i >= 1:
                                turn(h, s, i - 1)
                                values(h, s, i - 1)


NPAIR = 4
NKW = P + TS


def phase_window(nc, sem, K, I, S):
    with ExitStack() as ctx:
        sb, ps = open_phase(nc, ctx, "win")
        q = [sb(f"q{s}", [P, N]) for s in range(2)]
        k = [sb(f"k{s}", [P, N]) for s in range(2)]
        v = [sb(f"v{s}", [P, NT, HALF]) for s in range(2)]
        ck = [sb(f"ck{s}", [P, NB, NKW]) for s in range(2)]
        cv = [sb(f"cv{s}", [P, NB, HALF]) for s in range(2)]
        nv = [sb(f"nv{s}", [TS, NB, HALF]) for s in range(2)]
        qpad = sb("qpad", [P, NB * P + P])
        wpad = sb("wpad", [P, 4, NB * P + P])
        sink = sb("sink", [P, 8])
        nsink = sb("nsink", [P, 8])
        far = sb("far", [1, HALF])
        seen = sb("seen", [1, 2, P])
        pr = [sb(f"p{a}", [P, 2, 2 * P]) for a in range(2)]
        wt = [sb(f"wt{a}", [P, 4, P]) for a in range(2)]
        mx = sb("mx", [P, 2, 2])
        negm = sb("negm", [P, 2, 2])
        gap = sb("gap", [P, 2, 2])
        den = sb("den", [P, 2, 3, 2])
        rden = sb("rden", [P, 2, 2])
        sp_ = [ps(f"s{a}", [P, 2, 4 * P]) for a in range(2)]
        tp = [ps(f"t{a}", [P, 4, P]) for a in range(2)]
        op = [ps(f"o{a}", [P, 2, HALF]) for a in range(2)]

        loaded = [sem("win_loaded0"), sem("win_loaded1")]
        sink_in, constants, samples_in = sem("win_sink_in"), sem("win_constants"), sem("win_samples_in")
        s_ready, m_ready = sem("win_s_ready"), sem("win_m_ready")
        p_ready = sem("win_p_ready")
        t_ready = sem("win_t_ready")
        t_copied = sem("win_t_copied")
        o_ready = sem("win_o_ready")
        o_done = sem("win_o_done")
        new_rows = sem("win_new_rows")
        OB = K["OB"]

        def diag(ap):
            return ap[:, 0:NB * (P + TS)].rearrange("p (b n) -> p b n", b=NB)[:, :, 0:TS]

        with nc.Block() as block:

            @block.sync
            def _(sp):
                def load(j, kv, s):
                    for dst, src in (
                        (q[s][:, :], S["zt"][8 + j, :, :]),
                        (k[s][:, :], S["skt"][j, :, :]),
                        (ck[s][:, :, 0:P], I["cache_swa_kt"][kv].rearrange("p (b n) -> p b n", b=NB)),
                        (v[s][:, :, :], S["skv"][:, P + kv * HALF:P + (kv + 1) * HALF].rearrange("(t p) e -> p t e", p=P)),
                        (cv[s][:, :, :], I["cache_swa_v"][:, :, kv * HALF:(kv + 1) * HALF].rearrange("b p e -> p b e")),
                        (nv[s][:, :, :], S["skv"][TP:N, P + kv * HALF:P + (kv + 1) * HALF].rearrange("(b p) e -> p b e", p=TS)),
                    ):
                        sp.dma_start(dst, src).then_inc(loaded[s], 16)

                sp.dma_start(sink[:, :], I["swa_sinks"].partition_broadcast(P)).then_inc(sink_in, 16)
                load(0, 0, 0)
                load(1, 0, 1)
                for out, col in (("swa_k_sample", 0), ("swa_v_sample", P)):
                    sp.dma_start(S[out][:, P - TS:P, :], S["skv"][TP:N, col:col + P].rearrange("(b n) e -> b n e", n=TS))\
                      .then_inc(new_rows, 16)
                for s in range(2):
                    sp.wait_ge(o_ready, NT * (s + 1) + 2)
                    load(2 + s, 1, s)
                sp.wait_ge(new_rows, 32)

            @block.gpsimd
            def _(pool):
                pool.memset(qpad[:, :], 0.0).then_inc(constants, 1)
                pool.memset(wpad[:, :, :], 0.0).then_inc(constants, 1)
                pool.memset(far[:, :], FAR).then_inc(constants, 1)
                for a in range(2):
                    pool.memset(seen[:, a, 0:HALF], 1.0 - a).then_inc(constants, 1)
                    pool.memset(seen[:, a, HALF:P], float(a)).then_inc(constants, 1)

            @block.scalar
            def _(act):
                act.sem_inc(p_ready, 2)
                act.sem_inc(t_copied, 2)
                act.wait_ge(constants, 7)

                def exponents(j, s, i):
                    n, a = j * NT + i, (s * NT + i) % 2
                    width = P if i == 0 else 2 * P if i < 8 else NKW
                    act.wait_ge(m_ready, n + 1)
                    for r in range(2):
                        act.activation(pr[a][:, r, 0:width], sp_[a][:, r, 0:width], ACT.Exp, scale=SCALE,
                                       bias=negm[:, a, r:r + 1], accum_out=den[:, a, 0, r:r + 1])
                    act.activation(den[:, a, 1, :], gap[:, a, :], ACT.Exp).then_inc(p_ready, 1)

                def copy_turned(j, s, i):
                    n, a = j * NT + i, (s * NT + i) % 2
                    act.wait_ge(o_ready, n + 1)
                    act.wait_ge(t_ready, n + 1)
                    if i < NT - 1:
                        w = 2 if i == 0 else 4
                        act.activation(wt[a][:, 0:w, :], tp[a][:, 0:w, :], ACT.Copy).then_inc(t_copied, 1)
                    else:
                        for x in range(4):
                            rows = P if x % 2 == 0 else TS
                            last = act.activation(diag(wpad[0:rows, x, :]),
                                                  tp[a][0:rows, x, :].rearrange("p (b n) -> p b n", b=NB), ACT.Copy)
                        last.then_inc(t_copied, 1)

                with act.Fori(0, 2) as kv:
                    for s in range(2):
                        j = kv * 2 + s
                        for i in range(NT + 1):
                            if i < NT:
                                exponents(j, s, i)
                            if i >= 1:
                                copy_turned(j, s, i - 1)

            @block.vector
            def _(dve):
                dve.sem_inc(o_done, 2)
                dve.wait_ge(sink_in, 16)
                dve.tensor_scalar(nsink[:, :], sink[:, :], -1.0, None, ALU.mult)
                dve.wait_ge(constants, 7)

                def maxima(j, s, i):
                    n, a = j * NT + i, (s * NT + i) % 2
                    width = P if i == 0 else 2 * P if i < 8 else NKW
                    dve.wait_ge(s_ready, n + 1)
                    dve.tensor_reduce(mx[:, a, :], sp_[a][:, :, 0:width], AXX, ALU.max)
                    dve.drain()
                    dve.scalar_tensor_tensor(out=negm[:, a, :], in0=mx[:, a, :], scalar=-SCALE,
                                             in1=nsink[:, bass.ds(j * 2, 2)], op0=ALU.mult, op1=ALU.min)
                    dve.drain()
                    dve.tensor_tensor(gap[:, a, :], negm[:, a, :], nsink[:, bass.ds(j * 2, 2)], ALU.subtract)\
                       .then_inc(m_ready, 1)

                def finish(j, s, i):
                    n, a = j * NT + i, (s * NT + i) % 2
                    dve.tensor_tensor(den[:, a, 2, :], den[:, a, 0, :], den[:, a, 1, :], ALU.add)
                    dve.drain()
                    dve.reciprocal(rden[:, a, :], den[:, a, 2, :])
                    dve.drain()
                    dve.wait_ge(o_ready, n + 1 + 2)
                    dve.tensor_tensor(OB[:, i, bass.ds(j * P, P)].rearrange("p (r e) -> p r e", r=2), op[a][:, :, :],
                                      along(rden[:, a, :], HALF), ALU.mult).then_inc(o_done, 1)

                with dve.Fori(0, 2) as kv:
                    for s in range(2):
                        j = kv * 2 + s
                        dve.drain()
                        dve.wait_ge(loaded[s], (kv + 1) * 96)
                        dve.tensor_copy(diag(qpad[:, :]), q[s][:, TP:N].rearrange("p (b n) -> p b n", b=NB))
                        dve.tensor_copy(ck[s][:, :, P:NKW], k[s][:, TP:N].rearrange("p (b n) -> p b n", b=NB))\
                           .then_inc(samples_in, 1)
                        for i in range(NT + 1):
                            if i < NT:
                                maxima(j, s, i)
                            if i >= 1:
                                dve.wait_ge(p_ready, j * NT + i - 1 + 1 + 2)
                                finish(j, s, i - 1)

            @block.tensor
            def _(pe):
                pe.sem_inc(o_ready, 2)

                def scores(j, s, i):
                    n, a = j * NT + i, (s * NT + i) % 2
                    pe.wait_ge(p_ready, n + 1)
                    if i == NT - 1:
                        pe.wait_ge(samples_in, j + 1)
                    for r in range(2):
                        lo = HALF * r
                        if i == NT - 1:
                            for b in range(NB):
                                last = pe.matmul(sp_[a][:, r, 0:NKW], qpad[lo:lo + HALF, b * P:(b + 1) * P],
                                                 ck[s][lo:lo + HALF, b, :], start=(b == 0), stop=(b == NB - 1))
                            continue
                        first = max(i - 1, 0) * P
                        width = (i + 1) * P - first
                        pe.matmul(sp_[a][:, r, 0:width], q[s][lo:lo + HALF, i * P:(i + 1) * P],
                                  k[s][lo:lo + HALF, first:first + width], start=True, stop=False)
                        if i > 0:
                            pe.matmul(sp_[a][:, r, 0:HALF], seen[:, 1, :], far[:, :], start=False, stop=False)
                        last = pe.matmul(sp_[a][:, r, width - HALF:width], seen[:, 0, :], far[:, :], start=False, stop=True)
                    last.then_inc(s_ready, 1)

                def turn(j, s, i):
                    n, a = j * NT + i, (s * NT + i) % 2
                    pe.wait_ge(p_ready, n + 1 + 2)
                    pe.wait_ge(t_copied, n + 1)
                    x = 0
                    for r in range(2):
                        for c in range(1 if i == 0 else 2):
                            w = TS if i == NT - 1 and c == 1 else P
                            last = pe.transpose(tp[a][0:w, x, :], pr[a][:, r, c * P:c * P + w], K["ident"][:, :])
                            x += 1
                    last.then_inc(t_ready, 1)

                def values(j, s, i):
                    n, a = j * NT + i, (s * NT + i) % 2
                    pe.wait_ge(o_done, n + 1)
                    pe.wait_ge(t_copied, n + 1 + 2)
                    for r in range(2):
                        if i < NT - 1:
                            tiles = range(max(i - 1, 0), i + 1)
                            for c, t in enumerate(tiles):
                                last = pe.matmul(op[a][:, r, :], wt[a][:, r * len(tiles) + c, :], v[s][:, t, :],
                                                 start=(c == 0), stop=(t == i))
                            continue
                        for b in range(NB):
                            pe.matmul(op[a][:, r, :], wpad[:, 2 * r, b * P:(b + 1) * P], cv[s][:, b, :],
                                      start=(b == 0), stop=False)
                            last = pe.matmul(op[a][:, r, :], wpad[0:TS, 2 * r + 1, b * P:(b + 1) * P], nv[s][:, b, :],
                                             start=False, stop=(b == NB - 1))
                    last.then_inc(o_ready, 1)

                pe.wait_ge(constants, 7)
                with pe.Fori(0, 2) as kv:
                    for s in range(2):
                        j = kv * 2 + s
                        pe.wait_ge(loaded[s], (kv + 1) * 96)
                        for i in range(NT + 1):
                            if i < NT:
                                scores(j, s, i)
                            if i >= 1:
                                turn(j, s, i - 1)
                                values(j, s, i - 1)


def tile_of(ap, t):
    return ap[:, bass.ds(t, 1), :].rearrange("p a d -> p (a d)")


def phase_merge(nc, sem, K, I, S):
    with ExitStack() as ctx:
        sb, ps = open_phase(nc, ctx, "merge")
        wa = sb("wa", [P, 4, D])
        wb = sb("wb", [P, 4, D])
        wo = sb("wo", [P, KD, D])
        gates = sb("gates", [P, 4, CW])
        gsub = sb("gsub", [P, 1])
        gsub1 = sb("gsub1", [P, 1])
        std = sb("std", [P, NH * NT])
        rso = sb("rso", [P, NH * NT])
        oan = sb("oan", [P, CW])
        obn = sb("obn", [P, CW])
        oat = sb("oat", [P, 4, P])
        obt = sb("obt", [P, 4, P])
        ma = sb("ma", [P, D])
        mb = sb("mb", [P, D])
        m = sb("m", [P, D])
        mt = sb("mt", [P, KD, P])
        junk = sb("junk", [P, D])
        tp = [ps(f"t{a}", [P, 4, P]) for a in range(2)]
        ya, yb, yo = ps("ya", [P, D]), ps("yb", [P, D]), ps("yo", [P, D])

        w_in, gsub_in, gates_in = sem("merge_w_in"), sem("gsub_in"), sem("gates_in")
        rooted, gates_open = sem("merge_rooted"), sem("gates_open")
        gsub_ready = sem("gsub_ready")
        oan_ready, obn_ready = sem("oan_ready"), sem("obn_ready")
        t_ready = sem("merge_t_ready")
        t_copied = sem("merge_t_copied")
        y_ready, m_ready = sem("merge_y_ready"), sem("merge_m_ready")
        out_ready = sem("merge_out_ready")
        h_added = sem("merge_h_added")
        H, OA, OB = K["H"], K["OA"], K["OB"]

        with nc.Block() as block:

            @block.sync
            def _(sp):
                sp.dma_start(gsub[:, :], I["diff_subln_g"]).then_inc(gsub_in, 16)
                sp.dma_start(wa[:, :, :], I["w_branch_a"].rearrange("(k p) n -> p k n", p=P)).then_inc(w_in, 16)
                sp.dma_start(wb[:, :, :], I["w_branch_b"].rearrange("(k p) n -> p k n", p=P)).then_inc(w_in, 16)
                sp.dma_start(wo[:, :, :], I["w_out"].rearrange("(k p) n -> p k n", p=P)).then_inc(w_in, 16)
                zg = S["z"][4 * N:8 * N, :].rearrange("(c t p) n -> t p c n", c=4, p=P)
                sp.dma_start(gates[:, :, :], zg[0]).then_inc(gates_in, 16)
                with sp.Fori(1, NT) as t:
                    sp.wait_ge(m_ready, t)
                    sp.dma_start(gates[:, :, :], zg[bass.ds(t, 1)].rearrange("a p c n -> (a p) c n")).then_inc(gates_in, 16)

            @block.scalar
            def _(act):
                act.sem_inc(t_copied, 2)
                act.activation(std[:, :], K["sso"][:, :], ACT.Sqrt, scale=1.0 / P, bias=K["eps"][:, 0:1]).then_inc(rooted, 1)
                act.wait_ge(gsub_ready, 1)
                act.activation(obn[:, :], OB[:, 0, :], ACT.Copy).then_inc(obn_ready, 1)

                def copy_branches(t, first):
                    at = 0 if first else 4 * t - 2
                    if not first:
                        act.wait_ge(y_ready, t)
                    act.wait_ge(t_ready, at + 1)
                    act.activation(oat[:, :, :], tp[0][:, :, :], ACT.Copy, scale=gsub1[:, 0:1]).then_inc(t_copied, 1)
                    act.wait_ge(t_ready, at + 2)
                    act.activation(obt[:, :, :], tp[1][:, :, :], ACT.Copy).then_inc(t_copied, 1)

                def open_gates(t):
                    act.wait_ge(gates_in, 16 * (t + 1))
                    act.activation(gates[:, :, :], gates[:, :, :], ACT.Sigmoid).then_inc(gates_open, 1)

                def copy_merged(t, last_tile=False):
                    at = 4 * t + (2 if last_tile else 4)
                    act.wait_ge(out_ready, t + 1)
                    for x in range(2):
                        act.wait_ge(t_ready, at + x + 1)
                        act.activation(mt[:, 4 * x:4 * x + 4, :], tp[x][:, :, :], ACT.Copy).then_inc(t_copied, 1)

                def squares(t):
                    act.wait_ge(h_added, t + 1 + 1)
                    act.activation(junk[:, :], tile_of(H, t), ACT.Square, accum_out=K["ss"][:, bass.ds(t, 1)])
                    act.drain()

                copy_branches(0, True)
                open_gates(0)
                act.activation(obn[:, :], OB[:, 1, :], ACT.Copy).then_inc(obn_ready, 1)
                with act.Fori(1, NT - 1) as t:
                    copy_branches(t, False)
                    open_gates(t)
                    act.activation(obn[:, :], tile_of(OB, t + 1), ACT.Copy).then_inc(obn_ready, 1)
                    copy_merged(t - 1)
                    squares(t - 1)
                t = NT - 1
                copy_branches(t, False)
                open_gates(t)
                copy_merged(t - 1)
                squares(t - 1)
                copy_merged(t, last_tile=True)
                squares(t)

            @block.vector
            def _(dve):
                dve.sem_inc(h_added, 1)
                dve.wait_ge(gsub_in, 16)
                dve.tensor_scalar(gsub1[:, :], gsub[:, :], 1.0 - LAM0, None, ALU.mult).then_inc(gsub_ready, 1)
                dve.wait_ge(rooted, 1)
                dve.reciprocal(rso[:, :], std[:, :])
                dve.drain()

                def normed(t):
                    dve.tensor_tensor(oan[:, :].rearrange("p (h e) -> p h e", h=NH),
                                      tile_of(OA, t).rearrange("p (h e) -> p h e", h=NH),
                                      along(rso[:, bass.ds(t * NH, NH)], P), ALU.mult).then_inc(oan_ready, 1)

                def merged(t, first):
                    dve.wait_ge(y_ready, t + 1)
                    dve.wait_ge(gates_open, t + 1)
                    dve.tensor_tensor(ma[:, :], ya[:, :], gates[:, 0:2, :].rearrange("p c n -> p (c n)"), ALU.mult)
                    dve.tensor_tensor(mb[:, :], yb[:, :], gates[:, 2:4, :].rearrange("p c n -> p (c n)"), ALU.mult)
                    dve.drain()
                    if not first:
                        dve.wait_ge(t_ready, 4 * t + 2)
                    dve.tensor_tensor(m[:, :], ma[:, :], mb[:, :], ALU.add).then_inc(m_ready, 1)

                def residual(t):
                    dve.wait_ge(out_ready, t + 1 + 1)
                    dve.tensor_tensor(tile_of(H, t), tile_of(H, t), yo[:, :], ALU.add).then_inc(h_added, 1)

                normed(0)
                merged(0, True)
                normed(1)
                with dve.Fori(1, NT - 1) as t:
                    dve.drain()
                    merged(t, False)
                    normed(t + 1)
                    residual(t - 1)
                dve.drain()
                merged(NT - 1, False)
                residual(NT - 2)
                residual(NT - 1)

            @block.tensor
            def _(pe):
                pe.sem_inc(out_ready, 1)
                pe.wait_ge(w_in, 48)

                def branches(t, first):
                    at = 0 if first else 4 * t - 2
                    pe.wait_ge(oan_ready, t + 1)
                    pe.wait_ge(t_copied, at + 1)
                    for j in range(4):
                        last = pe.transpose(tp[0][:, j, :], oan[:, j * P:(j + 1) * P], K["ident"][:, :])
                    last.then_inc(t_ready, 1)
                    pe.wait_ge(obn_ready, t + 1)
                    pe.wait_ge(t_copied, at + 2)
                    for j in range(4):
                        last = pe.transpose(tp[1][:, j, :], obn[:, j * P:(j + 1) * P], K["ident"][:, :])
                    last.then_inc(t_ready, 1)
                    if not first:
                        pe.wait_ge(m_ready, t)
                    pe.wait_ge(t_copied, at + 2 + 2)
                    for w, src, y in ((wa, oat, ya), (wb, obt, yb)):
                        for half in range(2):
                            for j in range(4):
                                last = pe.matmul(y[:, half * CW:(half + 1) * CW], src[:, j, :],
                                                 w[:, j, half * CW:(half + 1) * CW], start=(j == 0), stop=(j == 3))
                    last.then_inc(y_ready, 1)

                def output(t, last_tile=False):
                    at = 4 * t + (2 if last_tile else 4)
                    pe.wait_ge(m_ready, t + 1)
                    for x in range(2):
                        pe.wait_ge(t_copied, at + x + 1)
                        for j in range(4 * x, 4 * x + 4):
                            last = pe.transpose(tp[x][:, j % 4, :], m[:, j * P:(j + 1) * P], K["ident"][:, :])
                        last.then_inc(t_ready, 1)
                    pe.wait_ge(h_added, t + 1)
                    pe.wait_ge(t_copied, at + 2 + 2)
                    for half in range(2):
                        for j in range(KD):
                            last = pe.matmul(yo[:, half * CW:(half + 1) * CW], mt[:, j, :],
                                             wo[:, j, half * CW:(half + 1) * CW], start=(j == 0), stop=(j == KD - 1))
                    last.then_inc(out_ready, 1)

                branches(0, True)
                with pe.Fori(1, NT) as t:
                    branches(t, False)
                    output(t - 1)
                output(NT - 1, last_tile=True)


NM = 256
MSCALE = P ** -0.5


def phase_memory(nc, sem, K, I, S):
    with ExitStack() as ctx:
        sb, ps = open_phase(nc, ctx, "mem")
        wq = sb("wq", [P, KD, CW])
        wkv = sb("wkv", [P, 2, KD, CW])
        wo = sb("wo", [P, 4, D])
        g = sb("g", [P, KD])
        gkv = sb("gkv", [P, KD])
        mem = sb("mem", [P, 2, D])
        mss = sb("mss", [P, 2])
        mstd = sb("mstd", [P, 2])
        mrstd = sb("mrstd", [P, 2])
        std = sb("std", [P, NT])
        mkv = sb("mkv", [P, 2, 2, CW])
        mkt = sb("mkt", [P, 4, NM])
        ckt = sb("ckt", [P, 4, NB * NM])
        cv = wkv[:, :, :, :].rearrange("p c k n -> p (c k) n")
        xn = sb("xn", [P, D])
        xt = sb("xt", [P, KD, P])
        qt = sb("qt", [P, 4, P])
        qpad = sb("qpad", [P, 4, NB * P + P])
        pr = sb("pr", [P, 4, NM])
        pt = sb("pt", [P, KD, P])
        ot = sb("ot", [P, 4, P])
        mx = sb("mx", [P, 4])
        negm = sb("negm", [P, 4])
        den = sb("den", [P, 4])
        rden = sb("rden", [P, 4])
        junk = sb("junk", [P, D])
        tp = ps("t", [P, KD, P])
        qp = ps("q", [P, 4, P])
        op = ps("o", [P, 4, P])
        sp_ = ps("s", [P, 4, NM])
        yo = ps("y", [P, D])

        m_in, w_in, g_in, cache_in = sem("mem_in"), sem("mem_w_in"), sem("mem_g_in"), sem("mem_cache_in")
        squared, rooted, padded = sem("mem_squared"), sem("mem_rooted"), sem("mem_padded")
        x_ready = sem("mem_x_ready")
        x_turned, xt_ready = sem("mem_x_turned"), sem("mem_xt_ready")
        kv_ready, kv_copied = sem("mem_kv_ready"), sem("mem_kv_copied")
        k_turned, k_copied, kv_out = sem("mem_k_turned"), sem("mem_k_copied"), sem("mem_kv_out")
        q_ready, q_copied = sem("mem_q_ready"), sem("mem_q_copied")
        s_ready, m_ready, p_ready, p_normed = sem("mem_s_ready"), sem("mem_m_ready"), sem("mem_p_ready"), sem("mem_p_normed")
        p_turned, pt_ready = sem("mem_p_turned"), sem("mem_pt_ready")
        o_ready, o_copied = sem("mem_o_ready"), sem("mem_o_copied")
        out_ready, h_added = sem("mem_out_ready"), sem("mem_h_added")
        H, ident = K["H"], K["ident"]

        def diag(ap):
            return ap[:, 0:NB * (P + TS)].rearrange("p (b n) -> p b n", b=NB)[:, :, 0:TS]

        with nc.Block() as block:

            @block.sync
            def _(sp):
                sp.dma_start(mem[:, :, :], I["mem_prompt"].rearrange("(t p) d -> p t d", p=P)).then_inc(m_in, 16)
                sp.dma_start(gkv[:, :], I["norm_memkv_g"]).then_inc(g_in, 16)
                sp.dma_start(g[:, :], I["norm_mem_g"]).then_inc(g_in, 16)
                for c, name in enumerate(("w_mem_k", "w_mem_v")):
                    sp.dma_start(wkv[:, c, :, :], I[name].rearrange("(k p) n -> p k n", p=P)).then_inc(w_in, 16)
                sp.dma_start(wq[:, :, :], I["w_mem_q"].rearrange("(k p) n -> p k n", p=P)).then_inc(w_in, 16)
                sp.dma_start(wo[:, :, :], I["w_mem_o"].rearrange("(k p) n -> p k n", p=P)).then_inc(w_in, 16)
                sp.dma_start(ckt[:, :, :], I["cache_mem_kt"].rearrange("h p n -> p h n")).then_inc(cache_in, 16)
                sp.wait_ge(kv_ready, 4)
                sp.dma_start(cv, I["cache_mem_v"].rearrange("(b p) n -> p b n", p=P)).then_inc(cache_in, 16)
                sp.wait_ge(kv_copied, 4)
                for c, out in enumerate(("mk", "mv")):
                    sp.dma_start(S[out].rearrange("(t p) n -> p t n", p=P), mkv[:, :, c, :]).then_inc(kv_out, 16)
                sp.wait_ge(kv_out, 32)

            @block.gpsimd
            def _(pool):
                pool.memset(qpad[:, :, :], 0.0).then_inc(padded, 1)

            @block.scalar
            def _(act):
                act.wait_ge(m_in, 16)
                for t in range(2):
                    act.activation(junk[:, :], mem[:, t, :], ACT.Square, accum_out=mss[:, t:t + 1])
                    act.drain()
                act.activation(mstd[:, :], mss[:, :], ACT.Sqrt, scale=1.0 / D, bias=K["eps"][:, 0:1])
                act.activation(std[:, :], K["ss"][:, :], ACT.Sqrt, scale=1.0 / D, bias=K["eps"][:, 0:1]).then_inc(rooted, 1)
                for n in range(4):
                    t, c = n // 2, n % 2
                    act.wait_ge(kv_ready, n + 1)
                    act.activation(mkv[:, t, c, :], (qp, op)[c][:, :, :].rearrange("p h n -> p (h n)"), ACT.Copy)\
                       .then_inc(kv_copied, 1)
                for t in range(2):
                    act.wait_ge(k_turned, t + 1)
                    act.activation(mkt[:, :, t * P:(t + 1) * P], tp[:, 4 * t:4 * t + 4, :], ACT.Copy).then_inc(k_copied, 1)

                def copy_queries(t):
                    act.wait_ge(q_ready, t + 1)
                    act.activation(qt[:, :, :], qp[:, :, :], ACT.Copy).then_inc(q_copied, 1)

                def exponents(t):
                    act.wait_ge(m_ready, t + 1)
                    for h in range(4):
                        last = act.activation(pr[:, h, :], sp_[:, h, :], ACT.Exp, scale=MSCALE, bias=negm[:, h:h + 1],
                                              accum_out=den[:, h:h + 1])
                    last.then_inc(p_ready, 1)

                def copy_probs(t):
                    act.wait_ge(p_turned, t + 1)
                    act.activation(pt[:, :, :], tp[:, :, :], ACT.Copy).then_inc(pt_ready, 1)

                def copy_outputs(t):
                    act.wait_ge(o_ready, t + 1)
                    act.activation(ot[:, :, :], op[:, :, :], ACT.Copy).then_inc(o_copied, 1)

                def squares(t):
                    act.wait_ge(h_added, t + 1)
                    act.activation(junk[:, :], tile_of(H, t), ACT.Square, accum_out=K["ss"][:, bass.ds(t, 1)])
                    act.drain()

                copy_queries(0)
                exponents(0)
                with act.Fori(1, NT - 1) as t:
                    copy_probs(t - 1)
                    copy_queries(t)
                    copy_outputs(t - 1)
                    exponents(t)
                    squares(t - 1)
                t = NT - 1
                act.wait_ge(padded, 1)
                copy_probs(t - 1)
                act.wait_ge(q_ready, t + 1)
                for h in range(4):
                    last = act.activation(diag(qpad[:, h, :]), qp[:, h, :].rearrange("p (b n) -> p b n", b=NB), ACT.Copy)
                last.then_inc(q_copied, 1)
                copy_outputs(t - 1)
                exponents(t)
                squares(t - 1)
                copy_probs(t)
                copy_outputs(t)
                squares(t)

            @block.vector
            def _(dve):
                dve.wait_ge(g_in, 32)
                dve.wait_ge(rooted, 1)
                dve.reciprocal(mrstd[:, :], mstd[:, :])
                dve.reciprocal(K["rstd"][:, :], std[:, :])
                dve.drain()
                mnt = [xt, pt]
                for t in range(2):
                    if t:
                        dve.wait_ge(x_turned, t)
                    dve.tensor_scalar(xn[:, :], mem[:, t, :], mrstd[:, t:t + 1], None, ALU.mult).then_inc(x_ready, 1)
                    dve.wait_ge(x_turned, t + 1)
                    dve.tensor_tensor(mnt[t][:, :, :], tp[:, :, :], along(gkv[:, :], P), ALU.mult).then_inc(xt_ready, 1)

                def normed(t):
                    dve.tensor_scalar(xn[:, :], tile_of(H, t), K["rstd"][:, bass.ds(t, 1)], None, ALU.mult)\
                       .then_inc(x_ready, 1)

                def scaled(t):
                    dve.wait_ge(x_turned, t + 1 + 2)
                    dve.tensor_tensor(xt[:, :, :], tp[:, :, :], along(g[:, :], P), ALU.mult).then_inc(xt_ready, 1)

                def maxima(t):
                    dve.wait_ge(s_ready, t + 1)
                    dve.tensor_reduce(mx[:, :], sp_[:, :, :], AXX, ALU.max)
                    dve.drain()
                    dve.tensor_scalar(negm[:, :], mx[:, :], -MSCALE, None, ALU.mult).then_inc(m_ready, 1)

                def divided(t):
                    dve.wait_ge(p_ready, t + 1)
                    dve.reciprocal(rden[:, :], den[:, :])
                    dve.drain()
                    dve.tensor_tensor(pr[:, :, :], pr[:, :, :], along(rden[:, :], NM), ALU.mult).then_inc(p_normed, 1)

                def residual(t):
                    dve.wait_ge(out_ready, t + 1)
                    dve.tensor_tensor(tile_of(H, t), tile_of(H, t), yo[:, :], ALU.add).then_inc(h_added, 1)

                normed(0)
                scaled(0)
                normed(1)
                maxima(0)
                with dve.Fori(1, NT - 1) as t:
                    divided(t - 1)
                    scaled(t)
                    dve.drain()
                    normed(t + 1)
                    maxima(t)
                    residual(t - 1)
                t = NT - 1
                divided(t - 1)
                scaled(t)
                maxima(t)
                residual(t - 1)
                divided(t)
                residual(t)

            @block.tensor
            def _(pe):
                mnt = [xt, pt]

                def turn(n):
                    pe.wait_ge(x_ready, n + 1)
                    for k in range(KD):
                        last = pe.transpose(tp[:, k, :], xn[:, k * P:(k + 1) * P], ident[:, :])
                    last.then_inc(x_turned, 1)

                turn(0)
                pe.wait_ge(xt_ready, 1)
                turn(1)
                pe.wait_ge(w_in, 64)
                for t in range(2):
                    pe.wait_ge(xt_ready, t + 1)
                    for c in range(2):
                        if t:
                            pe.wait_ge(kv_copied, c + 1)
                        for k in range(KD):
                            last = pe.matmul((qp, op)[c][:, :, :].rearrange("p h n -> p (h n)"), mnt[t][:, k, :],
                                             wkv[:, c, k, :], start=(k == 0), stop=(k == KD - 1))
                        last.then_inc(kv_ready, 1)
                for t in range(2):
                    pe.wait_ge(kv_copied, 2 * t + 1)
                    for h in range(4):
                        last = pe.transpose(tp[:, 4 * t + h, :], mkv[:, t, 0, h * P:(h + 1) * P], ident[:, :])
                    last.then_inc(k_turned, 1)
                pe.wait_ge(k_copied, 2)
                pe.wait_ge(kv_copied, 4)

                def queries(t):
                    pe.wait_ge(xt_ready, t + 1 + 2)
                    for h in range(4):
                        for k in range(KD):
                            last = pe.matmul(qp[:, h, :], wq[:, k, h * P:(h + 1) * P], xt[:, k, :],
                                             start=(k == 0), stop=(k == KD - 1))
                    last.then_inc(q_ready, 1)

                def scores(t, first=False, samples=False):
                    pe.wait_ge(q_copied, t + 1)
                    if not first:
                        pe.wait_ge(p_ready, t)
                    for h in range(4):
                        if samples:
                            for b in range(NB):
                                last = pe.matmul(sp_[:, h, :], qpad[:, h, b * P:(b + 1) * P],
                                                 ckt[:, h, b * NM:(b + 1) * NM], start=(b == 0), stop=(b == NB - 1))
                        else:
                            last = pe.matmul(sp_[:, h, :], qt[:, h, :], mkt[:, h, :], start=True, stop=True)
                    last.then_inc(s_ready, 1)

                def turn_probs(t):
                    pe.wait_ge(p_normed, t + 1)
                    pe.wait_ge(xt_ready, min(t + 2, NT) + 2 if isinstance(t, int) else t + 2 + 2)
                    for h in range(4):
                        for j in range(2):
                            last = pe.transpose(tp[:, 2 * h + j, :], pr[:, h, j * P:(j + 1) * P], ident[:, :])
                    last.then_inc(p_turned, 1)

                def values(t, samples=False):
                    pe.wait_ge(pt_ready, t + 1)
                    for h in range(4):
                        if samples:
                            for b in range(NB):
                                for j in range(2):
                                    last = pe.matmul(op[:, h, b * TS:(b + 1) * TS], cv[:, 2 * b + j, h * P:(h + 1) * P],
                                                     pt[:, 2 * h + j, b * TS:(b + 1) * TS], start=(j == 0), stop=(j == 1))
                        else:
                            for j in range(2):
                                last = pe.matmul(op[:, h, :], mkv[:, j, 1, h * P:(h + 1) * P], pt[:, 2 * h + j, :],
                                                 start=(j == 0), stop=(j == 1))
                    last.then_inc(o_ready, 1)

                def output(t, first=False):
                    pe.wait_ge(o_copied, t + 1)
                    if not first:
                        pe.wait_ge(h_added, t)
                    for half in range(2):
                        for h in range(4):
                            last = pe.matmul(yo[:, half * CW:(half + 1) * CW], ot[:, h, :],
                                             wo[:, h, half * CW:(half + 1) * CW], start=(h == 0), stop=(h == 3))
                    last.then_inc(out_ready, 1)

                turn(2)
                queries(0)
                scores(0, first=True)
                turn(3)
                turn_probs(0)
                queries(1)
                values(0)
                scores(1)
                output(0, first=True)
                with pe.Fori(2, NT - 1) as t:
                    pe.wait_ge(pt_ready, t - 1)
                    turn(t + 2)
                    turn_probs(t - 1)
                    queries(t)
                    values(t - 1)
                    scores(t)
                    output(t - 1)
                t = NT - 1
                pe.wait_ge(cache_in, 32)
                pe.wait_ge(pt_ready, t - 1)
                turn(t + 2)
                turn_probs(t - 1)
                queries(t)
                values(t - 1)
                scores(t, samples=True)
                output(t - 1)
                turn_probs(t)
                values(t, samples=True)
                output(t)


PH = 8
NKEY = 128
TOP = 16
OH = 8
ON_ACT = 2
LOW = -3.0e38


def phase_retrieve(nc, sem, K, I, S):
    with ExitStack() as ctx:
        sb, ps = open_phase(nc, ctx, "top")
        wq = sb("wq", [P, KD, D])
        keys = sb("keys", [P, PH, NKEY])
        g = sb("g", [P, KD])
        std = sb("std", [P, NT])
        places = [sb(f"place{s}", [P, 2 * PH * NKEY]) for s in range(2)]
        rest = sb("rest", [P, 2 * PH * NKEY])
        xn = sb("xn", [P, D])
        qt = xn[:, :].rearrange("p (h n) -> p h n", h=PH)
        xt = sb("xt", [P, KD, P])
        sc2 = rest[:, :].rearrange("p (a h n) -> p a h n", a=2, h=PH)
        cand2 = rest[:, :].rearrange("p (h n) -> p h n", h=PH)
        hot = sb("hot", [P, TOP, PH * TOP], BF16)
        val = sb("val", [P, 2, PH, TOP])
        ind = sb("ind", [P, 2, PH, TOP], U32)
        indf = sb("indf", [P, 2, PH, TOP], BF16)
        best = sb("best", [P, PH, TOP])
        pos = sb("pos", [P, PH, TOP], U32)
        part = sb("part", [P, 2, PH * TOP], U32)
        partf = sb("partf", [P, 2, PH * TOP], BF16)
        picked = sb("picked", [P, 3, PH * TOP])
        above = sb("above", [P, PH, TOP])
        mass = sb("mass", [P, PH])
        rmass = sb("rmass", [P, PH])
        carrier = sb("carrier", [P, 1])
        place_of = sb("place_of", [P, TOP, PH * TOP], BF16)
        key_of = sb("key_of", [P, NKEY, OH], BF16)
        iota = sb("iota", [P, NKEY])
        key1t, key2t, gt = sb("key1t", [P, P]), sb("key2t", [P, P], BF16), sb("gt", [P, P])
        left = [sb(f"left{r}", [P, OH, NKEY]) for r in range(2)]
        bare = [sb(f"bare{r}", [P, NKEY, OH], BF16) for r in range(2)]
        right = [sb(f"right{r}", [P, OH, NKEY]) for r in range(2)]
        tile_w = sb("tile_w", [P, NKEY, P])
        tp = ps("t", [P, KD, P])
        qp = ps("q", [P, PH, P])
        kp = [ps(f"k{x}", [P, CW]) for x in range(4)]

        w_in, g_in, iotas = sem("top_w_in"), sem("top_g_in"), sem("top_iotas")
        rooted, rstd_ready = sem("top_rooted"), sem("top_rstd_ready")
        x_ready, x_turned, xt_ready = sem("top_x_ready"), sem("top_x_turned"), sem("top_xt_ready")
        q_ready, q_copied = sem("top_q_ready"), sem("top_q_copied")
        s_ready, s_copied = sem("top_s_ready"), sem("top_s_copied")
        above_ready, e_ready = sem("above_ready"), sem("above_e_ready")
        picked_ready, p_turned, turned_ready = sem("picked_ready"), sem("picked_turned"), sem("turned_ready")
        left_ready, bare_ready = sem("left_ready"), sem("bare_ready")
        pool_scaled, act_scaled = sem("pool_scaled"), sem("act_scaled")
        w_made = sem("w_made")
        w_copied = sem("w_copied")
        w_stored = sem("w_stored")
        x_stored = sem("x_stored")
        H, ident = K["H"], K["ident"]
        batches = P // OH

        with nc.Block() as block:

            @block.sync
            def _(sp):
                sp.dma_start(g[:, :], I["norm_ffn_g"]).then_inc(g_in, 16)
                sp.dma_start(wq[:, :, :], I["w_peer_q"].rearrange("(k p) n -> p k n", p=P)).then_inc(w_in, 16)
                sp.dma_start(keys[:, :, :], I["peer_keys"].rearrange("h p n -> p h n")).then_inc(w_in, 16)
                sp.sem_inc(x_stored, 16)

                def store_x(t):
                    sp.wait_ge(xt_ready, t + 1)
                    sp.dma_start(S["xt"][bass.ds(t, 1)].rearrange("a p k n -> (a p) k n"), xt[:, :, :]).then_inc(x_stored, 16)

                def store_w(t):
                    sp.wait_ge(w_copied, 32 * (t + 1) + 4)
                    sp.dma_start(S["w"][:, bass.ds(t, 1), :, :].rearrange("p a j n -> p (a j n)"),
                                 tile_w[:, :, :].rearrange("p j n -> p (j n)")).then_inc(w_stored, 16)

                store_x(0)
                with sp.Fori(0, NT - 1) as t:
                    store_x(t + 1)
                    store_w(t)
                store_w(NT - 1)
                sp.wait_ge(w_stored, 16 * (NT + 1))
                sp.wait_ge(x_stored, 16 * (NT + 1))

            @block.gpsimd
            def _(pool):
                def rows(dst, pattern):
                    pool.iota(dst, pattern=pattern, base=0, channel_multiplier=0,
                              allow_small_or_imprecise_dtypes=True).then_inc(iotas, 1)
                rows(place_of[:, :, :], [[1, TOP], [0, PH * TOP]])
                rows(key_of[:, :, :], [[1, NKEY], [0, OH]])
                rows(iota[:, :], [[1, NKEY]])
                with pool.Fori(0, NT) as t:
                    with pool.Fori(0, batches // 2) as i:
                        for r in range(2):
                            b = i * 2 + r
                            pool.wait_ge(bare_ready, batches * t + b + 1)
                            pool.tensor_tensor(right[r][:, 0:OH - ON_ACT, :],
                                               bare[r][:, :, 0:OH - ON_ACT].rearrange("p j n -> p n j"),
                                               along(gt[:, bass.ds(b * OH, OH - ON_ACT)], NKEY), ALU.mult)\
                                .then_inc(pool_scaled, 1)

            @block.scalar
            def _(act):
                act.sem_inc(w_copied, 4)
                act.sem_inc(w_stored, 16)
                act.activation(std[:, :], K["ss"][:, :], ACT.Sqrt, scale=1.0 / D, bias=K["eps"][:, 0:1]).then_inc(rooted, 1)
                act.wait_ge(g_in, 16)
                act.wait_ge(rstd_ready, 1)

                def scores(t, s):
                    act.activation(xn[:, :], tile_of(H, t), ACT.Copy, scale=K["rstd"][:, bass.ds(t, 1)]).then_inc(x_ready, 1)
                    act.wait_ge(x_turned, t + 1)
                    act.wait_ge(x_stored, 16 * (t + 1))
                    for k in range(KD):
                        last = act.activation(xt[:, k, :], tp[:, k, :], ACT.Copy, scale=g[:, k:k + 1])
                    last.then_inc(xt_ready, 1)
                    act.wait_ge(q_ready, t + 1)
                    act.activation(qt[:, :, :], qp[:, :, :], ACT.Copy).then_inc(q_copied, 1)
                    act.wait_ge(s_ready, t + 1)
                    for x in range(4):
                        last = act.activation(places[s][:, x * CW:(x + 1) * CW], kp[x][:, :], ACT.Copy)
                    last.then_inc(s_copied, 1)

                def scale(t, b, r):
                    act.wait_ge(bare_ready, batches * t + b + 1)
                    for n in range(OH - ON_ACT, OH):
                        last = act.activation(right[r][:, n, :], bare[r][:, :, n], ACT.Copy, scale=gt[:, bass.ds(b * OH + n, 1)])
                    last.then_inc(act_scaled, 1)

                def copy(t, b, r):
                    for x in range(2):
                        act.wait_ge(w_made, 32 * t + 2 * b + x + 1 + 4)
                        act.activation(tile_w[:, :, bass.ds(b * OH + 4 * x, 4)].rearrange("p j n -> p n j"),
                                       kp[2 * r + x][:, :].rearrange("p (n j) -> p n j", n=4), ACT.Copy).then_inc(w_copied, 1)

                def spread(t):
                    act.wait_ge(above_ready, t + 1)
                    act.activation(above[:, :, :], above[:, :, :], ACT.Exp).then_inc(e_ready, 1)
                    act.wait_ge(p_turned, t + 1)
                    act.activation(key1t[:, :], tp[:, 0, :], ACT.Copy)
                    act.activation(key2t[:, :], tp[:, 1, :], ACT.Copy)
                    act.activation(gt[:, :], tp[:, 2, :], ACT.Copy).then_inc(turned_ready, 1)
                    scale(t, 0, 0)
                    act.wait_ge(w_stored, 16 * (t + 1))
                    with act.Fori(0, batches // 2 - 1) as i:
                        for r in range(2):
                            scale(t, i * 2 + r + 1, 1 - r)
                            copy(t, i * 2 + r, r)
                    scale(t, batches - 1, 1)
                    copy(t, batches - 2, 0)
                    copy(t, batches - 1, 1)

                scores(0, 0)
                with act.Fori(0, NT // 2) as i:
                    for s in range(2):
                        scores(i * 2 + s + 1, 1 - s)
                        spread(i * 2 + s)
                spread(NT - 1)

            @block.vector
            def _(dve):
                dve.wait_ge(iotas, 3)
                dve.wait_ge(rooted, 1)
                dve.reciprocal(K["rstd"][:, :], std[:, :]).then_inc(rstd_ready, 1)

                def halves(f):
                    for a in range(2):
                        for h in range(PH):
                            f(a, h)
                    dve.drain()

                def heads(f):
                    for h in range(PH):
                        f(h)
                    dve.drain()

                def choose(t, s):
                    sc = places[s][:, :].rearrange("p (a h n) -> p a h n", a=2, h=PH)
                    cand = places[s][:, :].rearrange("p (h n) -> p h n", h=PH)
                    dve.wait_ge(s_copied, t + 1)
                    dve.memset(carrier[:, :], 0.0)
                    halves(lambda a, h: dve.max(val[:, a, h, 0:8], sc[:, a, h, :]))
                    halves(lambda a, h: dve.max_index(ind[:, a, h, 0:8], val[:, a, h, 0:8], sc[:, a, h, :]))
                    halves(lambda a, h: dve.match_replace(sc2[:, a, h, :], val[:, a, h, 0:8], sc[:, a, h, :], LOW))
                    halves(lambda a, h: dve.max(val[:, a, h, 8:16], sc2[:, a, h, :]))
                    halves(lambda a, h: dve.max_index(ind[:, a, h, 8:16], val[:, a, h, 8:16], sc2[:, a, h, :]))
                    for h in range(PH):
                        dve.tensor_tensor(cand[:, h, :].rearrange("p (a b) -> p a b", a=TOP), along(val[:, 0, h, :], TOP),
                                          over(val[:, 1, h, :], TOP), ALU.add)
                    dve.tensor_copy(indf[:, :, :, :], ind[:, :, :, :])
                    dve.drain()
                    heads(lambda h: dve.max(best[:, h, 0:8], cand[:, h, :]))
                    heads(lambda h: dve.max_index(pos[:, h, 0:8], best[:, h, 0:8], cand[:, h, :]))
                    heads(lambda h: dve.match_replace(cand2[:, h, :], best[:, h, 0:8], cand[:, h, :], LOW))
                    heads(lambda h: dve.max(best[:, h, 8:16], cand2[:, h, :]))
                    dve.tensor_tensor(above[:, :, :], best[:, :, :], best[:, :, 0:1].to_broadcast([P, PH, TOP]), ALU.subtract)\
                       .then_inc(above_ready, 1)
                    heads(lambda h: dve.max_index(pos[:, h, 8:16], best[:, h, 8:16], cand2[:, h, :]))
                    flat = pos[:, :, :].rearrange("p h k -> p (h k)")
                    dve.tensor_scalar(part[:, 0, :], flat, 4, None, ALU.logical_shift_right)
                    dve.tensor_scalar(part[:, 1, :], flat, 15, None, ALU.bitwise_and)
                    dve.drain()
                    dve.tensor_copy(partf[:, :, :], part[:, :, :])
                    for a in range(2):
                        dve.drain()
                        dve.tensor_tensor(hot[:, :, :], over(partf[:, a, :], TOP), place_of[:, :, :], ALU.is_equal)
                        dve.drain()
                        by_head = hot[:, :, :].rearrange("p j (h k) -> p h j k", h=PH)
                        dve.tensor_tensor(by_head, by_head, indf[:, a, :, :].unsqueeze(3).to_broadcast([P, PH, TOP, TOP]), ALU.mult)
                        dve.drain()
                        dve.tensor_reduce(picked[:, a, :], hot[:, :, :].rearrange("p j c -> p c j"), AXX, ALU.add)
                    dve.wait_ge(e_ready, t + 1)
                    dve.tensor_reduce(mass[:, :], above[:, :, :], AXX, ALU.add)
                    dve.drain()
                    dve.reciprocal(rmass[:, :], mass[:, :])
                    dve.drain()
                    dve.tensor_tensor(picked[:, 2, :].rearrange("p (h k) -> p h k", h=PH), above[:, :, :],
                                      along(rmass[:, :], TOP), ALU.mult).then_inc(picked_ready, 1)

                def spread(t):
                    dve.wait_ge(turned_ready, t + 1)
                    dve.memset(carrier[:, :], 0.0)
                    with dve.Fori(0, batches // 2) as i:
                        for r in range(2):
                            b = i * 2 + r
                            dve.wait_ge(w_made, 32 * t + 2 * b + 2)
                            dve.tensor_tensor(bare[r][:, :, :], key_of[:, :, :], over(key2t[:, bass.ds(b * OH, OH)], NKEY),
                                              ALU.is_equal).then_inc(bare_ready, 1)
                            dve.tensor_tensor(left[r][:, :, :], over(iota[:, :], OH), along(key1t[:, bass.ds(b * OH, OH)], NKEY),
                                              ALU.is_equal).then_inc(left_ready, 1)

                with dve.Fori(0, NT // 2) as i:
                    for s in range(2):
                        choose(i * 2 + s, s)
                        spread(i * 2 + s)
                choose(NT - 1, 0)
                spread(NT - 1)

            @block.tensor
            def _(pe):
                pe.sem_inc(w_made, 4)
                pe.wait_ge(w_in, 32)

                def scores(t, again=True):
                    pe.wait_ge(x_ready, t + 1)
                    for k in range(KD):
                        last = pe.transpose(tp[:, k, :], xn[:, k * P:(k + 1) * P], ident[:, :])
                    last.then_inc(x_turned, 1)
                    pe.wait_ge(xt_ready, t + 1)
                    for h in range(PH):
                        for k in range(KD):
                            last = pe.matmul(qp[:, h, :], wq[:, k, h * P:(h + 1) * P], xt[:, k, :],
                                             start=(k == 0), stop=(k == KD - 1))
                    last.then_inc(q_ready, 1)
                    pe.wait_ge(q_copied, t + 1)
                    if again:
                        pe.wait_ge(w_copied, 32 * (t - 1) + 4)
                    for x in range(4):
                        lo = 64 * (x // 2)
                        for h in range(4):
                            hh = 4 * (x % 2) + h
                            last = pe.matmul(kp[x][:, h * P:(h + 1) * P], qt[lo:lo + 64, hh, :], keys[lo:lo + 64, hh, :],
                                             start=True, stop=True)
                    last.then_inc(s_ready, 1)

                def spread(t):
                    pe.wait_ge(picked_ready, t + 1)
                    for x in range(3):
                        last = pe.transpose(tp[:, x, :], picked[:, x, :], ident[:, :])
                    last.then_inc(p_turned, 1)
                    with pe.Fori(0, batches // 2) as i:
                        for r in range(2):
                            b = i * 2 + r
                            pe.wait_ge(left_ready, batches * t + b + 1)
                            pe.wait_ge(pool_scaled, batches * t + b + 1)
                            pe.wait_ge(act_scaled, batches * t + b + 1)
                            for n in range(OH):
                                if n % 4 == 0:
                                    pe.wait_ge(w_copied, 32 * t + 2 * b + n // 4 + 1)
                                last = pe.matmul(kp[2 * r + n // 4][:, (n % 4) * P:(n % 4 + 1) * P], left[r][:, n, :],
                                                 right[r][:, n, :], start=True, stop=True)
                                if n % 4 == 3:
                                    last.then_inc(w_made, 1)

                scores(0, again=False)
                with pe.Fori(0, NT - 1) as t:
                    scores(t + 1)
                    spread(t)
                spread(NT - 1)


NH3 = 3
TC = N // NH3
NY = 2 * NT


def phase_experts(nc, sem, K, I, S):
    with ExitStack() as ctx:
        sb, ps = open_phase(nc, ctx, "exp")
        xh, xl = sb("xh", [P, KD, N], F32R), sb("xl", [P, KD, N], F32R)
        u = [sb(f"u{s}", [P, KD, P]) for s in range(2)]
        v = [sb(f"v{s}", [P, D]) for s in range(2)]
        w = [sb(f"w{s}", [P, NT, P]) for s in range(2)]
        uh = [sb(f"uh{s}", [P, KD, P], F32R) for s in range(2)]
        ul = [sb(f"ul{s}", [P, KD, P], F32R) for s in range(2)]
        vh = [sb(f"vh{s}", [P, D], F32R) for s in range(2)]
        vl = [sb(f"vl{s}", [P, D], F32R) for s in range(2)]
        ah = [sb(f"ah{s}", [P, N], F32R) for s in range(2)]
        al = [sb(f"al{s}", [P, N], F32R) for s in range(2)]
        gel = sb("gel", [P, NH3, TC])
        prod = sb("prod", [P, NH3, TC])
        hp = [ps(f"h{x}", [P, CW]) for x in range(NH3)]
        yp = [ps(f"y{x}", [P, CW]) for x in range(4)]

        x_in = [sem("ex_x_in0"), sem("ex_x_in1")]
        xh_ready, xl_ready = sem("ex_xh_ready"), sem("ex_xl_ready")
        u_in = [sem("ex_u_in0"), sem("ex_u_in1")]
        v_in = [sem("ex_v_in0"), sem("ex_v_in1")]
        w_in = [sem("ex_w_in0"), sem("ex_w_in1")]
        uh_ready, ul_ready = sem("ex_uh_ready"), sem("ex_ul_ready")
        vh_ready, vl_ready = sem("ex_vh_ready"), sem("ex_vl_ready")
        h_ready = sem("ex_h_ready")
        h_taken = sem("ex_h_taken")
        p_ready = sem("ex_p_ready")
        ah_ready = sem("ex_ah_ready")
        al_ready = sem("ex_al_ready")
        y_ready = sem("ex_y_ready")
        y_added = sem("ex_y_added")
        H = K["H"]

        with nc.Block() as block:

            @block.sync
            def _(sp):
                for t in range(NT):
                    if t >= 2:
                        sp.wait_ge(xl_ready, t - 1)
                    sp.dma_start(u[t % 2][:, :, :], S["xt"][t]).then_inc(x_in[t % 2], 16)

                def load(e, s):
                    sp.dma_start(u[s][:, :, :].rearrange("p k n -> p (k n)"),
                                 I["peer_u"][bass.ds(e, 1)].rearrange("a p n -> (a p) n")).then_inc(u_in[s], 16)
                    sp.dma_start(w[s][:, :, :], S["w"][:, :, bass.ds(e, 1), :].rearrange("p t a n -> p t (a n)"))\
                      .then_inc(w_in[s], 16)
                    sp.dma_start(v[s][:, :], I["peer_v"][:, bass.ds(e, 1), :].rearrange("p a n -> p (a n)"))\
                      .then_inc(v_in[s], 16)

                sp.wait_ge(xl_ready, NT)
                load(0, 0)
                load(1, 1)
                with sp.Fori(0, NKEY // 2 - 1) as i:
                    for s in range(2):
                        e = i * 2 + s
                        sp.wait_ge(ul_ready, e + 1)
                        sp.wait_ge(p_ready, NH3 * (e + 1) + NH3)
                        sp.wait_ge(vl_ready, e + 1)
                        load(e + 2, s)

            @block.scalar
            def _(act):
                act.sem_inc(h_taken, NH3)
                act.sem_inc(ah_ready, NH3)
                for t in range(NT):
                    act.wait_ge(x_in[t % 2], 16 * (t // 2 + 1))
                    act.activation(xh[:, :, t * P:(t + 1) * P], u[t % 2][:, :, :], ACT.Copy).then_inc(xh_ready, 1)

                def high_u(e, s, turn):
                    act.wait_ge(u_in[s], 16 * (turn + 1))
                    act.activation(uh[s][:, :, :], u[s][:, :, :], ACT.Copy).then_inc(uh_ready, 1)

                def step(e, s, turn, next_turn):
                    if next_turn is not None:
                        act.wait_ge(h_ready, NH3 * e + NH3)
                        high_u(e + 1, 1 - s, next_turn)
                    act.wait_ge(v_in[s], 16 * (turn + 1))
                    act.wait_ge(y_ready, NY * (e + 1))
                    act.activation(vh[s][:, :], v[s][:, :], ACT.Copy).then_inc(vh_ready, 1)

                    def gelu(c):
                        act.wait_ge(h_ready, NH3 * e + c + 1 + NH3)
                        act.wait_ge(p_ready, NH3 * e + c + 1)
                        act.activation(gel[:, c, :], hp[c][:, 0:TC], ACT.Gelu_apprx_tanh).then_inc(h_taken, 1)

                    def high_a(c):
                        act.wait_ge(p_ready, NH3 * e + c + 1 + NH3)
                        act.activation(ah[s][:, c * TC:(c + 1) * TC], prod[:, c, :], ACT.Copy).then_inc(ah_ready, 1)

                    for c in range(NH3 + 1):
                        if c < NH3:
                            gelu(c)
                        if c > 0:
                            high_a(c - 1)

                act.wait_ge(xl_ready, NT)
                high_u(0, 0, 0)
                step(0, 0, 0, 0)
                with act.Fori(0, NKEY // 2 - 1) as i:
                    step(i * 2 + 1, 1, i, i + 1)
                    step(i * 2 + 2, 0, i + 1, i + 1)
                step(NKEY - 1, 1, NKEY // 2 - 1, None)

            @block.vector
            def _(dve):
                dve.sem_inc(p_ready, NH3)
                dve.sem_inc(y_added, 4)
                for t in range(NT):
                    dve.wait_ge(xh_ready, t + 1)
                    dve.tensor_tensor(xl[:, :, t * P:(t + 1) * P], u[t % 2][:, :, :], xh[:, :, t * P:(t + 1) * P],
                                      ALU.subtract).then_inc(xl_ready, 1)

                def low_u(e, s):
                    dve.wait_ge(uh_ready, e + 1)
                    dve.tensor_tensor(ul[s][:, :, :], u[s][:, :, :], uh[s][:, :, :], ALU.subtract).then_inc(ul_ready, 1)

                def step(e, s, turn, first=False, last=False):
                    dve.drain()
                    if not last:
                        low_u(e + 1, 1 - s)
                    dve.wait_ge(vh_ready, e + 1)
                    dve.tensor_tensor(vl[s][:, :], v[s][:, :], vh[s][:, :], ALU.subtract).then_inc(vl_ready, 1)
                    dve.wait_ge(w_in[s], 16 * (turn + 1))
                    nb = TC // P

                    def weigh(c):
                        dve.wait_ge(h_taken, NH3 * e + c + 1 + NH3)
                        dve.wait_ge(ah_ready, NH3 * e + c + 1)
                        dve.tensor_tensor(prod[:, c, :].rearrange("p (b n) -> p b n", n=P),
                                          gel[:, c, :].rearrange("p (b n) -> p b n", n=P),
                                          w[s][:, c * nb:(c + 1) * nb, :], ALU.mult).then_inc(p_ready, 1)

                    def low_a(c):
                        dve.wait_ge(ah_ready, NH3 * e + c + 1 + NH3)
                        at = slice(c * TC, (c + 1) * TC)
                        dve.tensor_tensor(al[s][:, at], prod[:, c, :], ah[s][:, at], ALU.subtract).then_inc(al_ready, 1)

                    for c in range(NH3 + 1):
                        if c < NH3:
                            weigh(c)
                        if c > 0:
                            low_a(c - 1)
                    if not first:
                        add_up(e - 1, 1 - s)

                def add_up(e, s):
                    dve.drain()
                    for x in range(NY):
                        dst = H[:, x // 2, (x % 2) * CW:(x % 2 + 1) * CW]
                        dve.wait_ge(y_ready, NY * e + x + 1 + 2 * NY)
                        dve.tensor_tensor(dst, dst, yp[(s * NY + x) % 4][:, :], ALU.add).then_inc(y_added, 1)

                low_u(0, 0)
                step(0, 0, 0, first=True)
                with dve.Fori(0, NKEY // 2 - 1) as i:
                    step(i * 2 + 1, 1, i)
                    step(i * 2 + 2, 0, i + 1)
                step(NKEY - 1, 1, NKEY // 2 - 1, last=True)
                add_up(NKEY - 1, 1)

            @block.tensor
            def _(pe):
                pe.sem_inc(h_ready, NH3)
                pe.sem_inc(y_ready, 2 * NY)

                def hidden(e, s):
                    pe.wait_ge(ul_ready, e + 1)
                    for c in range(NH3):
                        pe.wait_ge(h_taken, NH3 * e + c + 1)
                        at = slice(c * TC, (c + 1) * TC)
                        for k in range(KD):
                            pe.matmul(hp[c][:, 0:TC], uh[s][:, k, :], xh[:, k, at], start=(k == 0), stop=False)
                            pe.matmul(hp[c][:, 0:TC], uh[s][:, k, :], xl[:, k, at], start=False, stop=False)
                            last = pe.matmul(hp[c][:, 0:TC], ul[s][:, k, :], xh[:, k, at], start=False, stop=(k == KD - 1))
                        last.then_inc(h_ready, 1)

                def output(e, s):
                    pe.wait_ge(vl_ready, e + 1)
                    pe.wait_ge(al_ready, NH3 * (e + 1))
                    for x in range(NY):
                        rows, cols = slice(x // 2 * P, (x // 2 + 1) * P), slice(x % 2 * CW, (x % 2 + 1) * CW)
                        y = yp[(s * NY + x) % 4][:, :]
                        pe.wait_ge(y_added, NY * e + x + 1)
                        pe.matmul(y, ah[s][:, rows], vh[s][:, cols], start=True, stop=False)
                        pe.matmul(y, ah[s][:, rows], vl[s][:, cols], start=False, stop=False)
                        pe.matmul(y, al[s][:, rows], vh[s][:, cols], start=False, stop=True).then_inc(y_ready, 1)

                pe.wait_ge(xl_ready, NT)
                hidden(0, 0)
                with pe.Fori(0, NKEY // 2 - 1) as i:
                    hidden(i * 2 + 1, 1)
                    output(i * 2, 0)
                    hidden(i * 2 + 2, 0)
                    output(i * 2 + 1, 1)
                hidden(NKEY - 1, 1)
                output(NKEY - 2, 0)
                output(NKEY - 1, 1)


def phase_final(nc, sem, K, I, S):
    with ExitStack() as ctx:
        sb, ps = open_phase(nc, ctx, "fin")
        g = sb("g", [P, D])
        std = sb("std", [P, NT])
        y = sb("y", [P, 3, D])
        junk = sb("junk", [P, D])
        g_in, rooted, y_ready = sem("fin_g_in"), sem("fin_rooted"), sem("fin_y_ready")
        stored = [sem(f"fin_stored{x}") for x in range(3)]
        H = K["H"]

        with nc.Block() as block:

            @block.sync
            def _(sp):
                sp.dma_start(g[:, :], I["final_norm_g"].partition_broadcast(P)).then_inc(g_in, 16)
                for x in range(3):
                    sp.sem_inc(stored[x], 16)
                with sp.Fori(0, 3) as i:
                    for x in range(3):
                        sp.wait_ge(y_ready, i * 3 + x + 1)
                        sp.dma_start(S["y"][bass.ds((i * 3 + x) * P, P), :], y[:, x, :]).then_inc(stored[x], 16)
                for x in range(3):
                    sp.wait_ge(stored[x], 64)

            @block.scalar
            def _(act):
                with act.Fori(0, NT) as t:
                    act.drain()
                    act.activation(junk[:, :], tile_of(H, t), ACT.Square, accum_out=K["ss"][:, bass.ds(t, 1)])
                act.drain()
                act.activation(std[:, :], K["ss"][:, :], ACT.Sqrt, scale=1.0 / D, bias=K["eps"][:, 0:1]).then_inc(rooted, 1)

            @block.vector
            def _(dve):
                dve.wait_ge(g_in, 16)
                dve.wait_ge(rooted, 1)
                dve.reciprocal(K["rstd"][:, :], std[:, :])
                dve.drain()
                with dve.Fori(0, 3) as i:
                    for x in range(3):
                        t = i * 3 + x
                        dve.wait_ge(stored[x], 16 * (i + 1))
                        dve.scalar_tensor_tensor(out=y[:, x, :], in0=tile_of(H, t), scalar=K["rstd"][:, bass.ds(t, 1)],
                                                 in1=g[:, :], op0=ALU.mult, op1=ALU.mult).then_inc(y_ready, 1)


def load_constants(nc, sem, K, I):
    with nc.Block() as block:
        cleared = sem("cleared")

        @block.gpsimd
        def _(pool):
            pool.memset(K["ident"][:, :], 0.0).then_inc(cleared, 1)
            pool.memset(K["eps"][:, :], EPS).then_inc(cleared, 1)
            pool.wait_ge(cleared, 2)
            pool.affine_select(out=K["ident"][:, :], in_=K["ident"][:, :], compare_op=ALU.not_equal, fill=1.0,
                               base=0, pattern=[[-1, P]], channel_multiplier=1)


def build(nc, I, O):
    with ExitStack() as ctx:
        def sem(name):
            return ctx.enter_context(nc.semaphore(name))

        def keep(name, shape, dt=F32):
            return ctx.enter_context(nc.sbuf_tensor(name, shape, dt))

        K = {
            "H": keep("H", [P, NT, D]),
            "ident": keep("ident", [P, P]),
            "eps": keep("eps", [P, 1]),
            "ss": keep("ss", [P, NT]),
            "rstd": keep("rstd", [P, NT]),
        }
        S = {n: nc.dram_tensor(f"s_{n}", shape, F32).ap() for n, shape in SCRATCH.items()}
        S.update(O)
        load_constants(nc, sem, K, I)
        for kept, phases in PHASES:
            with ExitStack() as scope:
                for name, shape in kept.items():
                    K[name] = scope.enter_context(nc.sbuf_tensor(name, shape, F32))
                for phase in phases:
                    phase(nc, sem, K, I, S)


SCRATCH = {
    "xt": (NT, P, KD, P),
    "w": (P, NT, NKEY, P),
    "zt": (ROPED * 4, P, N),
    "skt": (4, P, N),
}
OUTS = {
    "y": (N, D),
    "z": ((ROPED + PLAIN) * N, CW), "skv": (N, 256),
    "mk": (2 * P, CW), "mv": (2 * P, CW),
    "swa_k_sample": (NB, P, P), "swa_v_sample": (NB, P, P),
}


def kernel(**inputs):
    import numpy as _np
    import concourse.bacc as _bacc
    from concourse import mybir as _mybir
    from concourse.bass_utils import run_bass_kernel_spmd as _run

    a = {k: _np.asarray(v) for k, v in inputs.items()}
    arrays = lay_out(a, _np)
    nc = _bacc.Bacc("TRN2", target_bir_lowering=False, num_devices=1)
    ins, feed = {}, {}
    for name, x in arrays.items():
        x = _np.ascontiguousarray(x)
        ins[name] = nc.dram_tensor(f"in_{name}", x.shape, _mybir.dt.from_np(x.dtype), kind="ExternalInput").ap()
        feed[f"in_{name}"] = x
    outs = {n: nc.dram_tensor(f"out_{n}", shape, _mybir.dt.float32, kind="ExternalOutput").ap() for n, shape in OUTS.items()}
    build(nc, ins, outs)
    r = _run(nc, [feed], core_ids=[0]).results[0]
    return give_back({n: r[f"out_{n}"] for n in OUTS})


def rope_tables(np):
    pos = np.concatenate([np.arange(TP), 256 + np.arange(NB * TS) % TS]).astype(np.float32)
    inv = np.float32(10000.0) ** (-np.arange(32, dtype=np.float32) / np.float32(32))
    angle = (pos[:, None] * inv[None, :]).astype(np.float32)
    cos, sin = np.cos(angle), np.sin(angle)
    return np.concatenate([cos, cos], 1).astype(np.float32), np.concatenate([-sin, sin], 1).astype(np.float32)


def lay_out(a, np):
    cols = a["w_in"][0]
    cos, sin = rope_tables(np)
    return {
        "x_prompt": a["x_prompt"][0], "x_sample": a["x_sample"].reshape(N - TP, D),
        "norm_mix_g": a["norm_mix_g"][0].reshape(KD, P).T,
        "w_in": np.concatenate([cols[:, 0:1024], cols[:, 1536:2048], cols[:, 1024:1536], cols[:, 2304:4352],
                                cols[:, 2048:2304]], axis=1),
        "rope_cos": cos, "rope_sin": sin,
        "cache_diff_kt": a["cache_diff_k"][0].reshape(NB, PAST, NH, P).transpose(2, 3, 0, 1).reshape(NH, P, NB * PAST),
        "cache_diff_v": a["cache_diff_v"][0].reshape(NB * PAST, NH * P),
        "lambdas": np.stack([a[f"lambda_{x}"][0] for x in ("q1", "q2", "k1", "k2")]),
        "cache_swa_kt": np.concatenate([a["cache_swa_k"][0].transpose(2, 3, 0, 1).reshape(2, HALF, NB * P)] * 2, axis=1),
        "diff_subln_g": a["diff_subln_g"][0].reshape(P, 1),
        "w_branch_a": a["w_branch_a"][0], "w_branch_b": a["w_branch_b"][0], "w_out": a["w_out"][0],
        "mem_prompt": a["mem_prompt"][0],
        "norm_memkv_g": a["norm_memkv_g"][0].reshape(KD, P).T, "norm_mem_g": a["norm_mem_g"][0].reshape(KD, P).T,
        "w_mem_q": a["w_mem_q"][0], "w_mem_k": a["w_mem_k"][0], "w_mem_v": a["w_mem_v"][0], "w_mem_o": a["w_mem_o"][0],
        "cache_mem_kt": a["cache_mem_k"][0].transpose(2, 3, 0, 1).reshape(4, P, NB * NM),
        "cache_mem_v": a["cache_mem_v"][0].reshape(NB * NM, CW),
        "norm_ffn_g": a["norm_ffn_g"][0].reshape(KD, P).T, "w_peer_q": a["w_peer_q"][0],
        "peer_keys": np.concatenate([a[f"peer_keys{x}"][0].transpose(0, 2, 1) for x in (1, 2)], axis=1),
        "peer_u": a["peer_u"][0].reshape(NKEY, NKEY, KD, P).transpose(1, 3, 2, 0).reshape(NKEY, P, D),
        "peer_v": a["peer_v"][0].reshape(NKEY, NKEY, D),
        "final_norm_g": a["final_norm_g"],
        "swa_sinks": a["swa_sinks"][0],
        "cache_swa_k": a["cache_swa_k"][0].reshape(NB, P, P), "cache_swa_v": a["cache_swa_v"][0].reshape(NB, P, P),
    }



def give_back(o):
    z = o["z"].reshape(ROPED + PLAIN, N, CW)
    dk, dv, skv = z[1], z[3], o["skv"]
    return (
        o["y"][:TP].reshape(1, TP, D), o["y"][TP:].reshape(NB, TS, D),
        dk[:TP].reshape(1, 1, TP, NH, 2, HALF), dv[:TP].reshape(1, 1, TP, NH, P),
        skv[TP - P:TP, 0:P].reshape(1, 1, P, 2, HALF), skv[TP - P:TP, P:2 * P].reshape(1, 1, P, 2, HALF),
        o["mk"].reshape(1, 1, NM, 4, P), o["mv"].reshape(1, 1, NM, 4, P),
        dk[TP:].reshape(1, NB, TS, NH, 2, HALF), dv[TP:].reshape(1, NB, TS, NH, P),
        o["swa_k_sample"].reshape(1, NB, P, 2, HALF), o["swa_v_sample"].reshape(1, NB, P, 2, HALF),
    )


PHASES = [
    ({"OA": [P, NT, CW], "OB": [P, NT, CW], "sso": [P, NH * NT]},
     [phase_project, phase_diff, phase_window, phase_merge]),
    ({}, [phase_memory, phase_retrieve, phase_experts, phase_final]),
]
```

```python
from contextlib import ExitStack

import numpy as np

import concourse.bass as bass
from concourse import mybir

F32 = mybir.dt.float32
F32R = mybir.dt.float32r
BF16 = mybir.dt.bfloat16
U32 = mybir.dt.uint32
ALU = mybir.AluOpType
ACT = mybir.ActivationFunctionType
AXX = mybir.AxisListType.X

P = 128
D = 1024
KD = D // P
TP = 1024
NB, TS = 8, 16
NT = 9
N = NT * P
EPS = 1e-6
CW = 512
ROPED, PLAIN = 3, 5


def along(ap, n):
    return ap.unsqueeze(2).to_broadcast([ap.shape[0], ap.shape[1], n])


def over(ap, n):
    return ap.unsqueeze(1).to_broadcast([ap.shape[0], n, ap.shape[1]])


def open_phase(nc, ctx, name):
    def sb(label, shape, dt=F32):
        return ctx.enter_context(nc.sbuf_tensor(f"{name}_{label}", shape, dt))

    def ps(label, shape, dt=F32):
        return ctx.enter_context(nc.psum_tensor(f"{name}_{label}", shape, dt))
    return sb, ps


def part_of(ap, c, half, width):
    return ap[:, bass.ds(c % 2, 1), 4 * half:4 * half + 4, 0:width].rearrange("p a k n -> p (a k) n")


def phase_project(nc, sem, K, I, S):
    with ExitStack() as ctx:
        sb, ps = open_phase(nc, ctx, "proj")
        xn = sb("xn", [P, D])
        xh, xl = sb("xh", [P, KD, N], F32R), sb("xl", [P, KD, N], F32R)
        g = sb("g", [P, KD])
        w = sb("w", [P, KD // 2, CW])
        wh, wl = sb("wh", [P, 2, KD, CW], F32R), sb("wl", [P, 2, KD, CW], F32R)
        cos = sb("cos", [P, NT, 64])
        sin = sb("sin", [P, NT, 64])
        turned = sb("turned", [P, 2, CW])
        zs = sb("zs", [P, 3, CW])
        zt = sb("zt", [P, 3, CW])
        junk = zt[:, 0:2, :].rearrange("p a n -> p (a n)")
        std = sb("std", [P, NT])
        zp = [ps(f"z{n}", [P, CW]) for n in range(3)]
        tp = [ps(f"t{n}", [P, CW]) for n in range(3)]
        xp = ps("x", [P, D])

        arrive = [0, 1, 2, 2, 3, 3, 4, 4, 4]
        x_in = [sem(f"x_in{t}") for t in range(max(arrive) + 1)]
        g_in, tab_in, rooted, xn_ready = sem("g_in"), sem("tab_in"), sem("rooted"), sem("xn_ready")
        x_turned, xs_ready = sem("x_turned"), sem("xs_ready")
        xh_ready, xl_ready = sem("xh_ready"), sem("xl_ready")
        wh_ready, wl_ready = sem("wh_ready"), sem("wl_ready")
        w_in = sem("w_in")
        z_ready = sem("z_ready")
        roped, plain, small = sem("roped_rows"), sem("plain_rows"), sem("window_rows")
        zs_out = [sem(f"zs_out{n}") for n in range(3)]
        t_ready = sem("t_ready")
        zt_ready = sem("zt_ready")
        zt_out = [sem(f"zt_out{n}") for n in range(3)]
        sk_out, copies = sem("sk_out"), sem("copies")
        H, ident = K["H"], K["ident"]

        with nc.Block() as block:

            @block.sync
            def _(sp):
                w_src = I["w_in"].rearrange("(k p) n -> p k n", p=P)

                def load_half(c, half, width=CW):
                    sp.dma_start(w[:, :, 0:width], w_src[:, 4 * half:4 * half + 4, bass.ds(c * CW, width)]).then_inc(w_in, 16)

                sp.dma_start(H[:, 0, :], I["x_prompt"][0:P, :]).then_inc(x_in[0], 16)
                sp.dma_start(g[:, :], I["norm_mix_g"]).then_inc(g_in, 16)
                load_half(0, 0)
                sp.dma_start(H[:, 1, :], I["x_prompt"][P:2 * P, :]).then_inc(x_in[1], 16)
                sp.dma_start(cos[:, :, :], I["rope_cos"].rearrange("(t p) d -> p t d", p=P)).then_inc(tab_in, 16)
                sp.dma_start(sin[:, :, :], I["rope_sin"].rearrange("(t p) d -> p t d", p=P)).then_inc(tab_in, 16)
                for t in range(2, NT):
                    src = I["x_prompt"][t * P:(t + 1) * P, :] if t < NT - 1 else I["x_sample"]
                    sp.dma_start(H[:, t, :], src).then_inc(x_in[arrive[t]], 16)

                sp.wait_ge(wl_ready, 1)
                load_half(0, 1)

                def store_rows(c, ready, first, width=CW):
                    for t in range(NT):
                        if t in (0, 5):
                            sp.wait_ge(wl_ready, 2 * c + 2 + (t > 0))
                            load_half(c + 1, int(t > 0), width)
                        sp.wait_ge(ready, (c - first) * NT + t + 1 + 3)
                        sp.dma_start(S["z"][bass.ds(c * N + t * P, P), :], zs[:, t % 3, :]).then_inc(zs_out[t % 3], 16)

                with sp.Fori(0, ROPED) as c:
                    store_rows(c, roped, 0)
                with sp.Fori(ROPED, ROPED + PLAIN - 1) as c:
                    store_rows(c, plain, ROPED)
                store_rows(ROPED + PLAIN - 1, plain, ROPED, width=256)
                for t in range(NT):
                    sp.wait_ge(small, t + 1 + 3)
                    sp.dma_start(S["skv"][t * P:t * P + P, :], zs[:, t % 3, 0:256]).then_inc(zs_out[t % 3], 16)
                for n in range(3):
                    sp.wait_ge(zs_out[n], 16 * (3 * (ROPED + PLAIN + 1) + 1))

            @block.gpsimd
            def _(pool):
                pool.dma_start(S["swa_k_sample"][:, 0:P - TS, :], I["cache_swa_k"][:, TS:P, :]).then_inc(copies, 16)
                pool.dma_start(S["swa_v_sample"][:, 0:P - TS, :], I["cache_swa_v"][:, TS:P, :]).then_inc(copies, 16)
                pool.wait_ge(copies, 32)

            @block.scalar
            def _(act):
                act.sem_inc(zt_ready, 3)
                act.sem_inc(plain, 3)
                for n in range(3):
                    act.sem_inc(zt_out[n], 16)

                def squares(t):
                    act.wait_ge(x_in[arrive[t]], 16 * arrive.count(arrive[t]))
                    act.activation(junk, H[:, t, :], ACT.Square, accum_out=K["ss"][:, t:t + 1])
                    act.drain()
                    act.activation(std[:, t:t + 1], K["ss"][:, t:t + 1], ACT.Sqrt, scale=1.0 / D, bias=K["eps"][:, 0:1])\
                       .then_inc(rooted, 1)

                def high_w(c, half, width=CW, reused=True):
                    act.wait_ge(w_in, 16 * (2 * c + half + 1))
                    if reused:
                        act.wait_ge(z_ready, (c - 1) * NT)
                    act.activation(part_of(wh, c, half, width), w[:, :, 0:width], ACT.Copy).then_inc(wh_ready, 1)

                def high_x(t):
                    act.wait_ge(xs_ready, t + 1 + 1)
                    act.activation(xh[:, :, t * P:(t + 1) * P], xn[:, :].rearrange("p (k n) -> p k n", k=KD), ACT.Copy)\
                       .then_inc(xh_ready, 1)

                def store_turned(c, t):
                    act.wait_ge(t_ready, c * NT + t + 1)
                    act.wait_ge(zt_out[t % 3], 16 * (c * 3 + t // 3 + 1))
                    act.activation(zt[:, t % 3, :], tp[t % 3][:, :], ACT.Copy).then_inc(zt_ready, 1)
                    act.wait_ge(zt_ready, c * NT + t + 1 + 3)
                    act.dma_start(S["zt"][bass.ds(c * 4, 4), :, t * P:t * P + P].rearrange("j p n -> p j n"),
                                  zt[:, t % 3, :].rearrange("p (j n) -> p j n", j=4)).then_inc(zt_out[t % 3], 16)

                squares(0)
                high_w(0, 0, reused=False)
                squares(1)
                high_w(0, 1, reused=False)
                for t in range(NT + 4):
                    if t < NT:
                        high_x(t)
                    for later in (2 * t + 2, 2 * t + 3):
                        if later < NT:
                            squares(later)
                    if t >= 4:
                        store_turned(0, t - 4)
                        if t - 4 in (2, 6):
                            high_w(1, (t - 4) // 6, reused=False)
                with act.Fori(1, ROPED) as c:
                    for t in range(NT):
                        store_turned(c, t)
                        if t in (2, 6):
                            high_w(c + 1, t // 6)

                def plain_rows(c, width=CW):
                    for t in range(NT):
                        act.wait_ge(z_ready, c * NT + t + 1)
                        act.wait_ge(zs_out[t % 3], 16 * (c * 3 + t // 3 + 1))
                        act.activation(zs[:, t % 3, :], zp[t % 3][:, :], ACT.Copy).then_inc(plain, 1)
                        if t in (2, 6):
                            high_w(c + 1, t // 6, width)

                with act.Fori(ROPED, ROPED + PLAIN - 1) as c:
                    plain_rows(c)
                plain_rows(ROPED + PLAIN - 1, width=256)
                for t in range(NT):
                    c = ROPED
                    act.wait_ge(t_ready, c * NT + t + 1)
                    act.wait_ge(zt_out[t % 3], 16 * (c * 3 + 1) + 64 * (t // 3))
                    act.activation(zt[:, t % 3, 0:P], tp[t % 3][:, 0:P], ACT.Copy).then_inc(zt_ready, 1)
                    act.wait_ge(zt_ready, c * NT + t + 1 + 3)
                    for kv in range(2):
                        for half in range(2):
                            act.dma_start(S["skt"][2 * kv:2 * kv + 2, 64 * half:64 * half + 64, t * P:t * P + P]
                                          .rearrange("j p n -> p j n"),
                                          zt[64 * kv:64 * kv + 64, t % 3, 0:P].unsqueeze(1).to_broadcast([64, 2, P]))\
                               .then_inc(zt_out[t % 3], 16)
                for n in range(3):
                    act.wait_ge(zt_out[n], 16 * (ROPED * 3 + 1) + 64 * 3)

            @block.vector
            def _(dve):
                dve.sem_inc(roped, 3)
                dve.sem_inc(small, 3)
                dve.sem_inc(xs_ready, 1)
                for n in range(3):
                    dve.sem_inc(zs_out[n], 16)
                dve.wait_ge(g_in, 16)

                def normed(t):
                    dve.wait_ge(rooted, t + 1)
                    dve.reciprocal(K["rstd"][:, t:t + 1], std[:, t:t + 1])
                    dve.drain()
                    dve.wait_ge(x_turned, t + 1)
                    dve.tensor_scalar(xn[:, :], H[:, t, :], K["rstd"][:, t:t + 1], None, ALU.mult).then_inc(xn_ready, 1)
                    dve.wait_ge(x_turned, t + 2)
                    dve.tensor_tensor(xn[:, :].rearrange("p (k n) -> p k n", k=KD), xp[:, :].rearrange("p (k n) -> p k n", k=KD),
                                      along(g[:, :], P), ALU.mult).then_inc(xs_ready, 1)

                def low_x(t):
                    dve.wait_ge(xh_ready, t + 1)
                    at = slice(t * P, (t + 1) * P)
                    dve.tensor_tensor(xl[:, :, at], xn[:, :].rearrange("p (k n) -> p k n", k=KD), xh[:, :, at], ALU.subtract)\
                       .then_inc(xl_ready, 1)

                def low_w(c, half, width=CW):
                    dve.wait_ge(wh_ready, 2 * c + half + 1)
                    dve.tensor_tensor(part_of(wl, c, half, width), w[:, :, 0:width], part_of(wh, c, half, width), ALU.subtract)\
                       .then_inc(wl_ready, 1)

                def rope(c, t, heads, ready):
                    n, width = t % 3, heads * 64
                    z3 = zp[n][:, 0:width].rearrange("p (h d) -> p h d", d=64)
                    r3 = turned[:, t % 2, 0:width].rearrange("p (h d) -> p h d", d=64)
                    s3 = zs[:, n, 0:width].rearrange("p (h d) -> p h d", d=64)
                    dve.wait_ge(z_ready, c * NT + t + 1)
                    dve.wait_ge(zs_out[n], 16 * (c * 3 + t // 3 + 1))
                    dve.tensor_tensor(s3, z3, over(cos[:, t, :], heads), ALU.mult)
                    dve.tensor_tensor(r3[:, :, 0:32], z3[:, :, 32:64], over(sin[:, t, 0:32], heads), ALU.mult)
                    dve.tensor_tensor(r3[:, :, 32:64], z3[:, :, 0:32], over(sin[:, t, 32:64], heads), ALU.mult)
                    dve.drain()
                    if width < CW:
                        dve.tensor_copy(zs[:, n, width:2 * width], zp[n][:, width:2 * width])
                        dve.drain()
                    dve.tensor_tensor(zs[:, n, 0:width], zs[:, n, 0:width], turned[:, t % 2, 0:width], ALU.add)\
                       .then_inc(ready, 1)

                low_w(0, 0)
                normed(0)
                low_w(0, 1)
                low_x(0)
                dve.wait_ge(tab_in, 32)
                for t in range(1, NT + 2):
                    if t < NT:
                        normed(t)
                    if t >= 2:
                        rope(0, t - 2, 8, roped)
                    if t < NT:
                        low_x(t)
                    if t == 7:
                        low_w(1, 0)
                low_w(1, 1)
                with dve.Fori(1, ROPED) as c:
                    dve.drain()
                    for t in range(NT):
                        rope(c, t, 8, roped)
                        if t in (3, 7):
                            low_w(c + 1, t // 7)
                with dve.Fori(ROPED, ROPED + PLAIN - 1) as c:
                    for half in range(2):
                        low_w(c + 1, half)
                for half in range(2):
                    low_w(ROPED + PLAIN, half, width=256)
                dve.drain()
                for t in range(NT):
                    rope(ROPED + PLAIN, t, 2, small)

            @block.tensor
            def _(pe):
                pe.sem_inc(x_turned, 1)

                def turn_x(t):
                    pe.wait_ge(xn_ready, t + 1)
                    pe.wait_ge(xs_ready, t + 1)
                    for k in range(KD):
                        last = pe.transpose(xp[:, k * P:(k + 1) * P], xn[:, k * P:(k + 1) * P], ident[:, :])
                    last.then_inc(x_turned, 1)

                def turn(c, t, blocks):
                    if blocks == 1:
                        pe.wait_ge(small, t + 1 + 3)
                    else:
                        pe.wait_ge(roped, c * NT + t + 1 + 3)
                    pe.wait_ge(zt_ready, c * NT + t + 1)
                    for j in range(blocks):
                        last = pe.transpose(tp[t % 3][:, j * P:(j + 1) * P], zs[:, t % 3, j * P:(j + 1) * P], ident[:, :])
                    last.then_inc(t_ready, 1)

                def project(c, t, width, slot, ready):
                    pe.wait_ge(ready, c * NT + t + 1)
                    at = slice(t * P, (t + 1) * P)
                    for k in range(KD):
                        high = wh[:, bass.ds(slot, 1), k, 0:width].rearrange("p a n -> p (a n)")
                        low = wl[:, bass.ds(slot, 1), k, 0:width].rearrange("p a n -> p (a n)")
                        pe.matmul(zp[t % 3][:, 0:width], xh[:, k, at], high, start=(k == 0), stop=False)
                        pe.matmul(zp[t % 3][:, 0:width], xh[:, k, at], low, start=False, stop=False)
                        last = pe.matmul(zp[t % 3][:, 0:width], xl[:, k, at], high, start=False, stop=(k == KD - 1))
                    last.then_inc(z_ready, 1)

                turn_x(0)
                pe.wait_ge(wl_ready, 2)
                for t in range(NT):
                    if t < NT - 1:
                        turn_x(t + 1)
                    pe.wait_ge(xl_ready, t + 1)
                    project(0, t, CW, 0, roped)
                    if t >= 2:
                        turn(0, t - 2, 4)
                turn(0, NT - 2, 4)
                turn(0, NT - 1, 4)
                with pe.Fori(1, ROPED) as c:
                    pe.wait_ge(wl_ready, 2 * c + 2)
                    for t in range(NT):
                        project(c, t, CW, c % 2, roped)
                        if t > 0:
                            turn(c, t - 1, 4)
                    turn(c, NT - 1, 4)
                with pe.Fori(ROPED, ROPED + PLAIN) as c:
                    pe.wait_ge(wl_ready, 2 * c + 2)
                    for t in range(NT):
                        project(c - ROPED, t, CW, c % 2, plain)
                pe.wait_ge(wl_ready, 2 * (ROPED + PLAIN) + 2)
                pe.wait_ge(plain, PLAIN * NT + 3)
                for t in range(NT):
                    project(0, t, 256, 0, small)
                    if t > 0:
                        turn(ROPED, t - 1, 1)
                turn(ROPED, NT - 1, 1)


NH = 4
PAST = 256
NKS = PAST + TS
HALF = 64
SCALE = HALF ** -0.5
FAR = -1e30
LAM0 = 0.8 - 0.6


def at(pair, x):
    return pair * 2 + x // NT, x // NT, x % NT


def phase_diff(nc, sem, K, I, S):
    with ExitStack() as ctx:
        sb, ps = open_phase(nc, ctx, "diff")
        q = [sb(f"q{s}", [P, N]) for s in range(2)]
        k = [sb(f"k{s}", [P, N]) for s in range(2)]
        v = [sb(f"v{s}", [P, NT, P]) for s in range(2)]
        ck = [sb(f"ck{s}", [P, NB, NKS]) for s in range(2)]
        cv = [sb(f"cv{s}", [P, 2 * NB, P]) for s in range(2)]
        nv = [sb(f"nv{s}", [TS, NB, P]) for s in range(2)]
        qpad = sb("qpad", [P, NB * P + P])
        wpad = sb("wpad", [P, 3, NB * P + P])
        lam = sb("lam", [P, 4, HALF])
        lprod = sb("lprod", [P, 2, HALF])
        lsum = sb("lsum", [P, 2])
        lexp = sb("lexp", [P, 2])
        neglam = sb("neglam", [P, 1])
        far = sb("far", [1, HALF])
        early = sb("early", [1, P])
        pr = [[sb(f"p{a}{m}", [P, TP]) for m in range(2)] for a in range(2)]
        wt = [sb(f"wt{a}", [P, TP]) for a in range(2)]
        mx = sb("mx", [P, 2, 2])
        negm = sb("negm", [P, 2, 2])
        den = sb("den", [P, 2, 2])
        rden = sb("rden", [P, 3, 2])
        ratio = sb("ratio", [P, 2])
        junk = sb("junk", [P, P])
        sp_ = [ps(f"s{m}", [P, TP]) for m in range(2)]
        tp = [ps(f"t{a}", [P, 4, P]) for a in range(2)]
        op = [ps(f"o{a}", [P, P]) for a in range(2)]

        loaded = [sem("diff_loaded0"), sem("diff_loaded1")]
        lam_in, lam_sum, lam_exp = sem("lam_in"), sem("lam_sum"), sem("lam_exp")
        constants, samples_in = sem("diff_constants"), sem("diff_samples_in")
        s_ready, m_ready = sem("diff_s_ready"), sem("diff_m_ready")
        p_ready = sem("diff_p_ready")
        w_ready, t_ready = sem("diff_w_ready"), sem("diff_t_ready")
        t_copied = sem("diff_t_copied")
        o_ready = sem("diff_o_ready")
        o_done = sem("diff_o_done")
        OA = K["OA"]
        groups = [1, 1, 1, 1, 2, 2, 2, 2, 1]
        NG = sum(groups)

        def diag(ap):
            return ap[:, 0:NB * (P + TS)].rearrange("p (b n) -> p b n", b=NB)[:, :, 0:TS]

        with nc.Block() as block:

            @block.sync
            def _(sp):
                def load(h, s):
                    col = h * P
                    for dst, src in (
                        (q[s][:, :], S["zt"][h, :, :]),
                        (k[s][:, :], S["zt"][4 + h, :, :]),
                        (ck[s][:, :, 0:PAST], I["cache_diff_kt"][h].rearrange("p (b n) -> p b n", b=NB)),
                        (v[s][:, :, :], S["z"][3 * N:4 * N, col:col + P].rearrange("(t p) e -> p t e", p=P)),
                        (cv[s][:, :, :], I["cache_diff_v"][:, col:col + P].rearrange("(b p) e -> p b e", p=P)),
                        (nv[s][:, :, :], S["z"][3 * N + TP:4 * N, col:col + P].rearrange("(b p) e -> p b e", p=TS)),
                    ):
                        sp.dma_start(dst, src).then_inc(loaded[s], 16)

                sp.dma_start(lam[:, :, :], I["lambdas"].partition_broadcast(P)).then_inc(lam_in, 16)
                load(0, 0)
                load(1, 1)
                for s in range(2):
                    sp.wait_ge(o_ready, NT * (s + 1) + 2)
                    load(2 + s, s)

            @block.gpsimd
            def _(pool):
                pool.memset(qpad[:, :], 0.0).then_inc(constants, 1)
                pool.memset(wpad[:, :, :], 0.0).then_inc(constants, 1)
                pool.memset(far[:, :], FAR).then_inc(constants, 1)
                pool.memset(early[:, 0:HALF], 1.0).then_inc(constants, 1)
                pool.memset(early[:, HALF:P], 0.0).then_inc(constants, 1)

            @block.scalar
            def _(act):
                act.sem_inc(p_ready, 2)
                act.sem_inc(t_copied, 2)
                act.wait_ge(constants, 5)
                act.wait_ge(lam_sum, 1)
                act.activation(lexp[:, :], lsum[:, :], ACT.Exp).then_inc(lam_exp, 1)

                def exponents(h, s, i):
                    n, a = h * NT + i, (s * NT + i) % 2
                    width = (i + 1) * P if i < 8 else NKS
                    for m in range(2):
                        act.wait_ge(m_ready, 2 * n + m + 1)
                        act.activation(pr[a][m][:, 0:width], sp_[m][:, 0:width], ACT.Exp, scale=SCALE,
                                       bias=negm[:, a, m:m + 1], accum_out=den[:, a, m:m + 1]).then_inc(p_ready, 1)

                def copy_turned(h, s, i):
                    n, a = h * NT + i, (s * NT + i) % 2
                    first = sum(groups[:i])
                    act.wait_ge(o_ready, n + 1)
                    for c in range(groups[i]):
                        g = first + c
                        bank = tp[(s * NG + g) % 2]
                        act.wait_ge(t_ready, h * NG + g + 1)
                        if i < 8:
                            w = min(4, i + 1 - 4 * c) * P
                            act.activation(wt[a][:, c * 4 * P:c * 4 * P + w],
                                           bank[:, :, :].rearrange("p j n -> p (j n)")[:, 0:w], ACT.Copy)\
                               .then_inc(t_copied, 1)
                        else:
                            for j in range(3):
                                rows = P if j < 2 else TS
                                last = act.activation(diag(wpad[0:rows, j, :]),
                                                      bank[0:rows, j, :].rearrange("p (b n) -> p b n", b=NB), ACT.Copy)
                            last.then_inc(t_copied, 1)

                def squares(h, s, i):
                    act.wait_ge(o_done, h * NT + i + 1 + 2)
                    act.activation(junk[:, :], OA[:, i, bass.ds(h * P, P)], ACT.Square,
                                   accum_out=K["sso"][:, bass.ds(h + NH * i, 1)])
                    act.drain()

                with act.Fori(0, 2) as pair:
                    for x in range(2 * NT + 3):
                        if x < 2 * NT:
                            exponents(*at(pair, x))
                        if 1 <= x <= 2 * NT:
                            copy_turned(*at(pair, x - 1))
                        if x >= 3:
                            squares(*at(pair, x - 3))

            @block.vector
            def _(dve):
                dve.sem_inc(o_done, 2)
                dve.wait_ge(lam_in, 16)
                dve.tensor_tensor(lprod[:, :, :], lam[:, 0:2, :], lam[:, 2:4, :], ALU.mult)
                dve.drain()
                dve.tensor_reduce(lsum[:, :], lprod[:, :, :], AXX, ALU.add).then_inc(lam_sum, 1)
                dve.wait_ge(lam_exp, 1)
                dve.scalar_tensor_tensor(out=neglam[:, :], in0=lexp[:, 1:2], scalar=-LAM0, in1=lexp[:, 0:1],
                                         op0=ALU.add, op1=ALU.subtract)
                dve.wait_ge(constants, 5)

                def maxima(h, s, i):
                    n, a = h * NT + i, (s * NT + i) % 2
                    width = (i + 1) * P if i < 8 else NKS
                    for m in range(2):
                        dve.wait_ge(s_ready, 2 * n + m + 1)
                        dve.tensor_reduce(mx[:, a, m:m + 1], sp_[m][:, 0:width], AXX, ALU.max)
                        dve.drain()
                        dve.tensor_scalar(negm[:, a, m:m + 1], mx[:, a, m:m + 1], -SCALE, None, ALU.mult)\
                           .then_inc(m_ready, 1)

                def samples(pair, s):
                    dve.drain()
                    dve.wait_ge(loaded[s], (pair + 1) * 96)
                    dve.tensor_copy(diag(qpad[:, :]), q[s][:, TP:N].rearrange("p (b n) -> p b n", b=NB))
                    dve.tensor_copy(ck[s][:, :, PAST:NKS], k[s][:, TP:N].rearrange("p (b n) -> p b n", b=NB))\
                       .then_inc(samples_in, 1)

                def combine(h, s, i):
                    n, a, r = h * NT + i, (s * NT + i) % 2, (s * NT + i) % 3
                    width = (i + 1) * P if i < 8 else NKS
                    dve.wait_ge(p_ready, 2 * n + 2 + 2)
                    dve.reciprocal(rden[:, r, :], den[:, a, :])
                    dve.drain()
                    dve.tensor_scalar(ratio[:, a:a + 1], den[:, a, 0:1], rden[:, r, 1:2], neglam[:, :], ALU.mult, ALU.mult)
                    dve.drain()
                    dve.scalar_tensor_tensor(out=pr[a][0][:, 0:width], in0=pr[a][1][:, 0:width], scalar=ratio[:, a:a + 1],
                                             in1=pr[a][0][:, 0:width], op0=ALU.mult, op1=ALU.add).then_inc(w_ready, 1)

                def finish(h, s, i):
                    n, a, r = h * NT + i, (s * NT + i) % 2, (s * NT + i) % 3
                    dve.wait_ge(o_ready, n + 1 + 2)
                    dve.tensor_scalar(OA[:, i, bass.ds(h * P, P)], op[a][:, :], rden[:, r, 0:1], None, ALU.mult)\
                       .then_inc(o_done, 1)

                with dve.Fori(0, 2) as pair:
                    for x in range(2 * NT + 2):
                        if 1 <= x <= 2 * NT:
                            combine(*at(pair, x - 1))
                        if x % NT == 0 and x < 2 * NT:
                            samples(pair, x // NT)
                        if x < 2 * NT:
                            maxima(*at(pair, x))
                        if x >= 2:
                            finish(*at(pair, x - 2))

            @block.tensor
            def _(pe):
                pe.sem_inc(o_ready, 2)

                def scores(h, s, i):
                    n = h * NT + i
                    for m in range(2):
                        lo = HALF * m
                        pe.wait_ge(p_ready, 2 * n + m + 1)
                        if i == NT - 1:
                            if m == 0:
                                pe.wait_ge(samples_in, h + 1)
                            for b in range(NB):
                                last = pe.matmul(sp_[m][:, 0:NKS], qpad[lo:lo + HALF, b * P:(b + 1) * P],
                                                 ck[s][lo:lo + HALF, b, :], start=(b == 0), stop=(b == NB - 1))
                            last.then_inc(s_ready, 1)
                            continue
                        width = (i + 1) * P
                        for c in range(0, width, 512):
                            w = min(512, width - c)
                            pe.matmul(sp_[m][:, c:c + w], q[s][lo:lo + HALF, i * P:(i + 1) * P],
                                      k[s][lo:lo + HALF, c:c + w], start=True, stop=(c + w < width))
                        pe.matmul(sp_[m][:, width - HALF:width], early[:, :], far[:, :], start=False, stop=True)\
                          .then_inc(s_ready, 1)

                def turn(h, s, i):
                    n, a = h * NT + i, (s * NT + i) % 2
                    first = sum(groups[:i])
                    pe.wait_ge(w_ready, n + 1)
                    for c in range(groups[i]):
                        g = first + c
                        pe.wait_ge(t_copied, h * NG + g + 1)
                        bank = tp[(s * NG + g) % 2]
                        blocks = 3 if i == NT - 1 else min(4, i + 1 - 4 * c)
                        for j in range(blocks):
                            at = (4 * c + j) * P
                            w = TS if i == NT - 1 and j == 2 else P
                            last = pe.transpose(bank[0:w, j, :], pr[a][0][:, at:at + w], K["ident"][:, :])
                        last.then_inc(t_ready, 1)

                def values(h, s, i):
                    n, a = h * NT + i, (s * NT + i) % 2
                    pe.wait_ge(o_done, n + 1)
                    pe.wait_ge(t_copied, h * NG + sum(groups[:i + 1]) + 2)
                    if i < NT - 1:
                        for j in range(i + 1):
                            last = pe.matmul(op[a][:, :], wt[a][:, j * P:(j + 1) * P], v[s][:, j, :],
                                             start=(j == 0), stop=(j == i))
                    else:
                        for b in range(NB):
                            for j in range(3):
                                rows = P if j < 2 else TS
                                rhs = cv[s][:, 2 * b + j, :] if j < 2 else nv[s][:, b, :]
                                last = pe.matmul(op[a][:, :], wpad[0:rows, j, b * P:(b + 1) * P], rhs,
                                                 start=(b == 0 and j == 0), stop=(b == NB - 1 and j == 2))
                    last.then_inc(o_ready, 1)

                pe.wait_ge(constants, 5)
                with pe.Fori(0, 2) as pair:
                    for x in range(2 * NT + 2):
                        if x % NT == 0 and x < 2 * NT:
                            pe.wait_ge(loaded[x // NT], (pair + 1) * 96)
                        if x < 2 * NT:
                            scores(*at(pair, x))
                        if 1 <= x <= 2 * NT:
                            turn(*at(pair, x - 1))
                        if x >= 2:
                            values(*at(pair, x - 2))


NPAIR = 4
NKW = P + TS


def phase_window(nc, sem, K, I, S):
    with ExitStack() as ctx:
        sb, ps = open_phase(nc, ctx, "win")
        q = [sb(f"q{s}", [P, N]) for s in range(2)]
        k = [sb(f"k{s}", [P, N]) for s in range(2)]
        v = [sb(f"v{s}", [P, NT, HALF]) for s in range(2)]
        ck = [sb(f"ck{s}", [P, NB, NKW]) for s in range(2)]
        cv = [sb(f"cv{s}", [P, NB, HALF]) for s in range(2)]
        nv = [sb(f"nv{s}", [TS, NB, HALF]) for s in range(2)]
        qpad = sb("qpad", [P, NB * P + P])
        wpad = sb("wpad", [P, 4, NB * P + P])
        sink = sb("sink", [P, 8])
        nsink = sb("nsink", [P, 8])
        far = sb("far", [1, HALF])
        seen = sb("seen", [1, 2, P])
        pr = [sb(f"p{a}", [P, 2, 2 * P]) for a in range(2)]
        wt = [sb(f"wt{a}", [P, 4, P]) for a in range(2)]
        mx = sb("mx", [P, 2, 2])
        negm = sb("negm", [P, 2, 2])
        gap = sb("gap", [P, 2, 2])
        den = sb("den", [P, 3, 3, 2])
        rden = sb("rden", [P, 2, 2])
        sp_ = [ps(f"s{a}", [P, 2, 4 * P]) for a in range(2)]
        tp = [ps(f"t{a}", [P, 4, P]) for a in range(2)]
        op = [ps(f"o{a}", [P, 2, HALF]) for a in range(2)]

        loaded = [sem("win_loaded0"), sem("win_loaded1")]
        sink_in, constants, samples_in = sem("win_sink_in"), sem("win_constants"), sem("win_samples_in")
        s_ready, m_ready = sem("win_s_ready"), sem("win_m_ready")
        p_ready = sem("win_p_ready")
        t_ready = sem("win_t_ready")
        t_copied = sem("win_t_copied")
        o_ready = sem("win_o_ready")
        o_done = sem("win_o_done")
        new_rows = sem("win_new_rows")
        OB = K["OB"]

        def diag(ap):
            return ap[:, 0:NB * (P + TS)].rearrange("p (b n) -> p b n", b=NB)[:, :, 0:TS]

        with nc.Block() as block:

            @block.sync
            def _(sp):
                def load(j, kv, s):
                    for dst, src in (
                        (q[s][:, :], S["zt"][8 + j, :, :]),
                        (k[s][:, :], S["skt"][j, :, :]),
                        (ck[s][:, :, 0:P], I["cache_swa_kt"][kv].rearrange("p (b n) -> p b n", b=NB)),
                        (v[s][:, :, :], S["skv"][:, P + kv * HALF:P + (kv + 1) * HALF].rearrange("(t p) e -> p t e", p=P)),
                        (cv[s][:, :, :], I["cache_swa_v"][:, :, kv * HALF:(kv + 1) * HALF].rearrange("b p e -> p b e")),
                        (nv[s][:, :, :], S["skv"][TP:N, P + kv * HALF:P + (kv + 1) * HALF].rearrange("(b p) e -> p b e", p=TS)),
                    ):
                        sp.dma_start(dst, src).then_inc(loaded[s], 16)

                sp.dma_start(sink[:, :], I["swa_sinks"].partition_broadcast(P)).then_inc(sink_in, 16)
                load(0, 0, 0)
                load(1, 0, 1)
                for out, col in (("swa_k_sample", 0), ("swa_v_sample", P)):
                    sp.dma_start(S[out][:, P - TS:P, :], S["skv"][TP:N, col:col + P].rearrange("(b n) e -> b n e", n=TS))\
                      .then_inc(new_rows, 16)
                for s in range(2):
                    sp.wait_ge(o_ready, NT * (s + 1) + 2)
                    load(2 + s, 1, s)
                sp.wait_ge(new_rows, 32)

            @block.gpsimd
            def _(pool):
                pool.memset(qpad[:, :], 0.0).then_inc(constants, 1)
                pool.memset(wpad[:, :, :], 0.0).then_inc(constants, 1)
                pool.memset(far[:, :], FAR).then_inc(constants, 1)
                for a in range(2):
                    pool.memset(seen[:, a, 0:HALF], 1.0 - a).then_inc(constants, 1)
                    pool.memset(seen[:, a, HALF:P], float(a)).then_inc(constants, 1)

            @block.scalar
            def _(act):
                act.sem_inc(p_ready, 2)
                act.sem_inc(t_copied, 2)
                act.wait_ge(constants, 7)

                def exponents(j, s, i):
                    n, a, d = j * NT + i, (s * NT + i) % 2, (s * NT + i) % 3
                    width = P if i == 0 else 2 * P if i < 8 else NKW
                    act.wait_ge(m_ready, n + 1)
                    for r in range(2):
                        act.activation(pr[a][:, r, 0:width], sp_[a][:, r, 0:width], ACT.Exp, scale=SCALE,
                                       bias=negm[:, a, r:r + 1], accum_out=den[:, d, 0, r:r + 1])
                    act.activation(den[:, d, 1, :], gap[:, a, :], ACT.Exp).then_inc(p_ready, 1)

                def copy_turned(j, s, i):
                    n, a = j * NT + i, (s * NT + i) % 2
                    act.wait_ge(o_ready, n + 1)
                    act.wait_ge(t_ready, n + 1)
                    if i < NT - 1:
                        w = 2 if i == 0 else 4
                        act.activation(wt[a][:, 0:w, :], tp[a][:, 0:w, :], ACT.Copy).then_inc(t_copied, 1)
                    else:
                        for x in range(4):
                            rows = P if x % 2 == 0 else TS
                            last = act.activation(diag(wpad[0:rows, x, :]),
                                                  tp[a][0:rows, x, :].rearrange("p (b n) -> p b n", b=NB), ACT.Copy)
                        last.then_inc(t_copied, 1)

                with act.Fori(0, 2) as kv:
                    for x in range(2 * NT + 1):
                        if x < 2 * NT:
                            exponents(*at(kv, x))
                        if x >= 1:
                            copy_turned(*at(kv, x - 1))

            @block.vector
            def _(dve):
                dve.sem_inc(o_done, 2)
                dve.wait_ge(sink_in, 16)
                dve.tensor_scalar(nsink[:, :], sink[:, :], -1.0, None, ALU.mult)
                dve.wait_ge(constants, 7)

                def maxima(j, s, i):
                    n, a = j * NT + i, (s * NT + i) % 2
                    width = P if i == 0 else 2 * P if i < 8 else NKW
                    dve.wait_ge(s_ready, n + 1)
                    dve.tensor_reduce(mx[:, a, :], sp_[a][:, :, 0:width], AXX, ALU.max)
                    dve.drain()
                    dve.scalar_tensor_tensor(out=negm[:, a, :], in0=mx[:, a, :], scalar=-SCALE,
                                             in1=nsink[:, bass.ds(j * 2, 2)], op0=ALU.mult, op1=ALU.min)
                    dve.drain()
                    dve.tensor_tensor(gap[:, a, :], negm[:, a, :], nsink[:, bass.ds(j * 2, 2)], ALU.subtract)\
                       .then_inc(m_ready, 1)

                def samples(kv, s):
                    dve.drain()
                    dve.wait_ge(loaded[s], (kv + 1) * 96)
                    dve.tensor_copy(diag(qpad[:, :]), q[s][:, TP:N].rearrange("p (b n) -> p b n", b=NB))
                    dve.tensor_copy(ck[s][:, :, P:NKW], k[s][:, TP:N].rearrange("p (b n) -> p b n", b=NB))\
                       .then_inc(samples_in, 1)

                def finish(j, s, i):
                    n, a, d = j * NT + i, (s * NT + i) % 2, (s * NT + i) % 3
                    dve.wait_ge(p_ready, n + 1 + 2)
                    dve.tensor_tensor(den[:, d, 2, :], den[:, d, 0, :], den[:, d, 1, :], ALU.add)
                    dve.drain()
                    dve.reciprocal(rden[:, a, :], den[:, d, 2, :])
                    dve.drain()
                    dve.wait_ge(o_ready, n + 1 + 2)
                    dve.tensor_tensor(OB[:, i, bass.ds(j * P, P)].rearrange("p (r e) -> p r e", r=2), op[a][:, :, :],
                                      along(rden[:, a, :], HALF), ALU.mult).then_inc(o_done, 1)

                with dve.Fori(0, 2) as kv:
                    for x in range(2 * NT + 2):
                        if x % NT == 0 and x < 2 * NT:
                            samples(kv, x // NT)
                        if x < 2 * NT:
                            maxima(*at(kv, x))
                        if x >= 2:
                            finish(*at(kv, x - 2))

            @block.tensor
            def _(pe):
                pe.sem_inc(o_ready, 2)

                def scores(j, s, i):
                    n, a = j * NT + i, (s * NT + i) % 2
                    pe.wait_ge(p_ready, n + 1)
                    if i == NT - 1:
                        pe.wait_ge(samples_in, j + 1)
                    for r in range(2):
                        lo = HALF * r
                        if i == NT - 1:
                            for b in range(NB):
                                last = pe.matmul(sp_[a][:, r, 0:NKW], qpad[lo:lo + HALF, b * P:(b + 1) * P],
                                                 ck[s][lo:lo + HALF, b, :], start=(b == 0), stop=(b == NB - 1))
                            continue
                        first = max(i - 1, 0) * P
                        width = (i + 1) * P - first
                        pe.matmul(sp_[a][:, r, 0:width], q[s][lo:lo + HALF, i * P:(i + 1) * P],
                                  k[s][lo:lo + HALF, first:first + width], start=True, stop=False)
                        if i > 0:
                            pe.matmul(sp_[a][:, r, 0:HALF], seen[:, 1, :], far[:, :], start=False, stop=False)
                        last = pe.matmul(sp_[a][:, r, width - HALF:width], seen[:, 0, :], far[:, :], start=False, stop=True)
                    last.then_inc(s_ready, 1)

                def turn(j, s, i):
                    n, a = j * NT + i, (s * NT + i) % 2
                    pe.wait_ge(p_ready, n + 1 + 2)
                    pe.wait_ge(t_copied, n + 1)
                    x = 0
                    for r in range(2):
                        for c in range(1 if i == 0 else 2):
                            w = TS if i == NT - 1 and c == 1 else P
                            last = pe.transpose(tp[a][0:w, x, :], pr[a][:, r, c * P:c * P + w], K["ident"][:, :])
                            x += 1
                    last.then_inc(t_ready, 1)

                def values(j, s, i):
                    n, a = j * NT + i, (s * NT + i) % 2
                    pe.wait_ge(o_done, n + 1)
                    pe.wait_ge(t_copied, n + 1 + 2)
                    for r in range(2):
                        if i < NT - 1:
                            tiles = range(max(i - 1, 0), i + 1)
                            for c, t in enumerate(tiles):
                                last = pe.matmul(op[a][:, r, :], wt[a][:, r * len(tiles) + c, :], v[s][:, t, :],
                                                 start=(c == 0), stop=(t == i))
                            continue
                        for b in range(NB):
                            pe.matmul(op[a][:, r, :], wpad[:, 2 * r, b * P:(b + 1) * P], cv[s][:, b, :],
                                      start=(b == 0), stop=False)
                            last = pe.matmul(op[a][:, r, :], wpad[0:TS, 2 * r + 1, b * P:(b + 1) * P], nv[s][:, b, :],
                                             start=False, stop=(b == NB - 1))
                    last.then_inc(o_ready, 1)

                pe.wait_ge(constants, 7)
                with pe.Fori(0, 2) as kv:
                    for x in range(2 * NT + 2):
                        if x % NT == 0 and x < 2 * NT:
                            pe.wait_ge(loaded[x // NT], (kv + 1) * 96)
                        if x < 2 * NT:
                            scores(*at(kv, x))
                        if 1 <= x <= 2 * NT:
                            turn(*at(kv, x - 1))
                        if x >= 2:
                            values(*at(kv, x - 2))




def tile_of(ap, t):
    return ap[:, bass.ds(t, 1), :].rearrange("p a d -> p (a d)")


def phase_merge(nc, sem, K, I, S):
    with ExitStack() as ctx:
        sb, ps = open_phase(nc, ctx, "merge")
        wa = sb("wa", [P, 4, D])
        wb = sb("wb", [P, 4, D])
        wo = sb("wo", [P, KD, D])
        gates = sb("gates", [P, 4, CW])
        gsub = sb("gsub", [P, 1])
        gsub1 = sb("gsub1", [P, 1])
        std = sb("std", [P, NH * NT])
        rso = sb("rso", [P, NH * NT])
        oan = sb("oan", [P, CW])
        obn = sb("obn", [P, CW])
        oat = sb("oat", [P, 4, P])
        obt = sb("obt", [P, 4, P])
        ma = sb("ma", [P, D])
        mb = sb("mb", [P, D])
        m = sb("m", [P, D])
        mt = sb("mt", [P, KD, P])
        junk = sb("junk", [P, D])
        tp = [ps(f"t{a}", [P, 4, P]) for a in range(2)]
        ya, yb, yo = ps("ya", [P, D]), ps("yb", [P, D]), ps("yo", [P, D])

        w_in, wo_in, gsub_in, gates_in = sem("merge_w_in"), sem("merge_wo_in"), sem("gsub_in"), sem("gates_in")
        rooted, gates_open = sem("merge_rooted"), sem("gates_open")
        gsub_ready = sem("gsub_ready")
        oan_ready, obn_ready = sem("oan_ready"), sem("obn_ready")
        t_ready = sem("merge_t_ready")
        t_copied = sem("merge_t_copied")
        y_ready, m_ready = sem("merge_y_ready"), sem("merge_m_ready")
        out_ready = sem("merge_out_ready")
        h_added = sem("merge_h_added")
        H, OA, OB = K["H"], K["OA"], K["OB"]

        with nc.Block() as block:

            @block.sync
            def _(sp):
                sp.dma_start(gsub[:, :], I["diff_subln_g"]).then_inc(gsub_in, 16)
                sp.dma_start(wa[:, :, :], I["w_branch_a"].rearrange("(k p) n -> p k n", p=P)).then_inc(w_in, 16)
                sp.dma_start(wb[:, :, :], I["w_branch_b"].rearrange("(k p) n -> p k n", p=P)).then_inc(w_in, 16)
                zg = S["z"][4 * N:8 * N, :].rearrange("(c t p) n -> t p c n", c=4, p=P)
                sp.dma_start(gates[:, :, :], zg[0]).then_inc(gates_in, 16)
                sp.dma_start(wo[:, :, :], I["w_out"].rearrange("(k p) n -> p k n", p=P)).then_inc(wo_in, 16)
                with sp.Fori(1, NT) as t:
                    sp.wait_ge(m_ready, t)
                    sp.dma_start(gates[:, :, :], zg[bass.ds(t, 1)].rearrange("a p c n -> (a p) c n")).then_inc(gates_in, 16)

            @block.scalar
            def _(act):
                act.sem_inc(t_copied, 2)
                act.activation(std[:, :], K["sso"][:, :], ACT.Sqrt, scale=1.0 / P, bias=K["eps"][:, 0:1]).then_inc(rooted, 1)
                act.wait_ge(gsub_ready, 1)
                act.activation(obn[:, :], OB[:, 0, :], ACT.Copy).then_inc(obn_ready, 1)

                def copy_branches(t, first):
                    at = 0 if first else 4 * t - 2
                    if not first:
                        act.wait_ge(y_ready, t)
                    act.wait_ge(t_ready, at + 1)
                    act.activation(oat[:, :, :], tp[0][:, :, :], ACT.Copy, scale=gsub1[:, 0:1]).then_inc(t_copied, 1)
                    act.wait_ge(t_ready, at + 2)
                    act.activation(obt[:, :, :], tp[1][:, :, :], ACT.Copy).then_inc(t_copied, 1)

                def open_gates(t):
                    act.wait_ge(gates_in, 16 * (t + 1))
                    act.activation(gates[:, :, :], gates[:, :, :], ACT.Sigmoid).then_inc(gates_open, 1)

                def copy_merged(t, last_tile=False):
                    at = 4 * t + (2 if last_tile else 4)
                    act.wait_ge(out_ready, t + 1)
                    for x in range(2):
                        act.wait_ge(t_ready, at + x + 1)
                        act.activation(mt[:, 4 * x:4 * x + 4, :], tp[x][:, :, :], ACT.Copy).then_inc(t_copied, 1)

                def squares(t):
                    act.wait_ge(h_added, t + 1 + 1)
                    act.activation(junk[:, :], tile_of(H, t), ACT.Square, accum_out=K["ss"][:, bass.ds(t, 1)])
                    act.drain()

                copy_branches(0, True)
                open_gates(0)
                act.activation(obn[:, :], OB[:, 1, :], ACT.Copy).then_inc(obn_ready, 1)
                with act.Fori(1, NT - 1) as t:
                    copy_branches(t, False)
                    open_gates(t)
                    act.activation(obn[:, :], tile_of(OB, t + 1), ACT.Copy).then_inc(obn_ready, 1)
                    copy_merged(t - 1)
                    squares(t - 1)
                t = NT - 1
                copy_branches(t, False)
                open_gates(t)
                copy_merged(t - 1)
                squares(t - 1)
                copy_merged(t, last_tile=True)
                squares(t)

            @block.vector
            def _(dve):
                dve.sem_inc(h_added, 1)
                dve.wait_ge(gsub_in, 16)
                dve.tensor_scalar(gsub1[:, :], gsub[:, :], 1.0 - LAM0, None, ALU.mult).then_inc(gsub_ready, 1)
                dve.wait_ge(rooted, 1)
                dve.reciprocal(rso[:, :], std[:, :])
                dve.drain()

                def normed(t):
                    dve.tensor_tensor(oan[:, :].rearrange("p (h e) -> p h e", h=NH),
                                      tile_of(OA, t).rearrange("p (h e) -> p h e", h=NH),
                                      along(rso[:, bass.ds(t * NH, NH)], P), ALU.mult).then_inc(oan_ready, 1)

                def merged(t, first):
                    dve.wait_ge(y_ready, t + 1)
                    dve.wait_ge(gates_open, t + 1)
                    dve.tensor_tensor(ma[:, :], ya[:, :], gates[:, 0:2, :].rearrange("p c n -> p (c n)"), ALU.mult)
                    dve.tensor_tensor(mb[:, :], yb[:, :], gates[:, 2:4, :].rearrange("p c n -> p (c n)"), ALU.mult)
                    dve.drain()
                    if not first:
                        dve.wait_ge(t_ready, 4 * t + 2)
                    dve.tensor_tensor(m[:, :], ma[:, :], mb[:, :], ALU.add).then_inc(m_ready, 1)

                def residual(t):
                    dve.wait_ge(out_ready, t + 1 + 1)
                    dve.tensor_tensor(tile_of(H, t), tile_of(H, t), yo[:, :], ALU.add).then_inc(h_added, 1)

                normed(0)
                merged(0, True)
                normed(1)
                with dve.Fori(1, NT - 1) as t:
                    dve.drain()
                    merged(t, False)
                    normed(t + 1)
                    residual(t - 1)
                dve.drain()
                merged(NT - 1, False)
                residual(NT - 2)
                residual(NT - 1)

            @block.tensor
            def _(pe):
                pe.sem_inc(out_ready, 1)

                def branches(t, first):
                    at = 0 if first else 4 * t - 2
                    pe.wait_ge(oan_ready, t + 1)
                    pe.wait_ge(t_copied, at + 1)
                    for j in range(4):
                        last = pe.transpose(tp[0][:, j, :], oan[:, j * P:(j + 1) * P], K["ident"][:, :])
                    last.then_inc(t_ready, 1)
                    pe.wait_ge(obn_ready, t + 1)
                    pe.wait_ge(t_copied, at + 2)
                    for j in range(4):
                        last = pe.transpose(tp[1][:, j, :], obn[:, j * P:(j + 1) * P], K["ident"][:, :])
                    last.then_inc(t_ready, 1)
                    if not first:
                        pe.wait_ge(m_ready, t)
                    pe.wait_ge(t_copied, at + 2 + 2)
                    if first:
                        pe.wait_ge(w_in, 32)
                    for w, src, y in ((wa, oat, ya), (wb, obt, yb)):
                        for half in range(2):
                            for j in range(4):
                                last = pe.matmul(y[:, half * CW:(half + 1) * CW], src[:, j, :],
                                                 w[:, j, half * CW:(half + 1) * CW], start=(j == 0), stop=(j == 3))
                    last.then_inc(y_ready, 1)

                def output(t, last_tile=False):
                    at = 4 * t + (2 if last_tile else 4)
                    pe.wait_ge(m_ready, t + 1)
                    for x in range(2):
                        pe.wait_ge(t_copied, at + x + 1)
                        for j in range(4 * x, 4 * x + 4):
                            last = pe.transpose(tp[x][:, j % 4, :], m[:, j * P:(j + 1) * P], K["ident"][:, :])
                        last.then_inc(t_ready, 1)
                    pe.wait_ge(h_added, t + 1)
                    pe.wait_ge(t_copied, at + 2 + 2)
                    for half in range(2):
                        for j in range(KD):
                            last = pe.matmul(yo[:, half * CW:(half + 1) * CW], mt[:, j, :],
                                             wo[:, j, half * CW:(half + 1) * CW], start=(j == 0), stop=(j == KD - 1))
                    last.then_inc(out_ready, 1)

                branches(0, True)
                pe.wait_ge(wo_in, 16)
                with pe.Fori(1, NT) as t:
                    branches(t, False)
                    output(t - 1)
                output(NT - 1, last_tile=True)


NM = 256
MSCALE = P ** -0.5


def phase_memory(nc, sem, K, I, S):
    with ExitStack() as ctx:
        sb, ps = open_phase(nc, ctx, "mem")
        wq = sb("wq", [P, KD, CW])
        wkv = sb("wkv", [P, 2, KD, CW])
        wo = sb("wo", [P, 4, D])
        g = sb("g", [P, KD])
        gkv = sb("gkv", [P, KD])
        mem = sb("mem", [P, 2, D])
        mss = sb("mss", [P, 2])
        mstd = sb("mstd", [P, 2])
        mrstd = sb("mrstd", [P, 2])
        std = sb("std", [P, NT])
        mkv = sb("mkv", [P, 2, 2, CW])
        mkt = sb("mkt", [P, 4, NM])
        ckt = sb("ckt", [P, 4, NB * NM])
        cv = wkv[:, :, :, :].rearrange("p c k n -> p (c k) n")
        xn = sb("xn", [P, D])
        xt = sb("xt", [P, KD, P])
        qt = sb("qt", [P, 4, P])
        qpad = sb("qpad", [P, 4, NB * P + P])
        pr = sb("pr", [P, 4, NM])
        pt = sb("pt", [P, KD, P])
        ot = sb("ot", [P, 4, P])
        mx = sb("mx", [P, 4])
        negm = sb("negm", [P, 4])
        den = sb("den", [P, 4])
        rden = sb("rden", [P, 4])
        junk = sb("junk", [P, D])
        tp = ps("t", [P, KD, P])
        qp = ps("q", [P, 4, P])
        op = ps("o", [P, 4, P])
        sp_ = ps("s", [P, 4, NM])
        yo = ps("y", [P, D])

        m_in, w_in, g_in, cache_in = sem("mem_in"), sem("mem_w_in"), sem("mem_g_in"), sem("mem_cache_in")
        wk_in, wv_in = sem("mem_wk_in"), sem("mem_wv_in")
        rooted, padded = sem("mem_rooted"), sem("mem_padded")
        x_ready = sem("mem_x_ready")
        x_turned, xt_ready = sem("mem_x_turned"), sem("mem_xt_ready")
        kv_ready, kv_copied = sem("mem_kv_ready"), sem("mem_kv_copied")
        k_turned, k_copied, kv_out = sem("mem_k_turned"), sem("mem_k_copied"), sem("mem_kv_out")
        q_ready, q_copied = sem("mem_q_ready"), sem("mem_q_copied")
        s_ready, m_ready, p_ready, p_normed = sem("mem_s_ready"), sem("mem_m_ready"), sem("mem_p_ready"), sem("mem_p_normed")
        p_turned, pt_ready = sem("mem_p_turned"), sem("mem_pt_ready")
        o_ready, o_copied = sem("mem_o_ready"), sem("mem_o_copied")
        out_ready, h_added = sem("mem_out_ready"), sem("mem_h_added")
        H, ident = K["H"], K["ident"]

        def diag(ap):
            return ap[:, 0:NB * (P + TS)].rearrange("p (b n) -> p b n", b=NB)[:, :, 0:TS]

        with nc.Block() as block:

            @block.sync
            def _(sp):
                sp.dma_start(mem[:, :, :], I["mem_prompt"].rearrange("(t p) d -> p t d", p=P)).then_inc(m_in, 16)
                sp.dma_start(gkv[:, :], I["norm_memkv_g"]).then_inc(g_in, 16)
                sp.dma_start(g[:, :], I["norm_mem_g"]).then_inc(g_in, 16)
                for c, name in enumerate(("w_mem_k", "w_mem_v")):
                    sp.dma_start(wkv[:, c, :, :], I[name].rearrange("(k p) n -> p k n", p=P)).then_inc((wk_in, wv_in)[c], 16)
                sp.dma_start(wq[:, :, :], I["w_mem_q"].rearrange("(k p) n -> p k n", p=P)).then_inc(w_in, 16)
                sp.dma_start(wo[:, :, :], I["w_mem_o"].rearrange("(k p) n -> p k n", p=P)).then_inc(w_in, 16)
                sp.dma_start(ckt[:, :, :], I["cache_mem_kt"].rearrange("h p n -> p h n")).then_inc(cache_in, 16)
                sp.wait_ge(kv_ready, 4)
                sp.dma_start(cv, I["cache_mem_v"].rearrange("(b p) n -> p b n", p=P)).then_inc(cache_in, 16)
                sp.wait_ge(kv_copied, 4)
                for c, out in enumerate(("mk", "mv")):
                    sp.dma_start(S[out].rearrange("(t p) n -> p t n", p=P), mkv[:, :, c, :]).then_inc(kv_out, 16)
                sp.wait_ge(kv_out, 32)

            @block.gpsimd
            def _(pool):
                pool.memset(qpad[:, :, :], 0.0).then_inc(padded, 1)

            @block.scalar
            def _(act):
                act.wait_ge(m_in, 16)
                for t in range(2):
                    act.activation(junk[:, :], mem[:, t, :], ACT.Square, accum_out=mss[:, t:t + 1])
                    act.drain()
                act.activation(mstd[:, :], mss[:, :], ACT.Sqrt, scale=1.0 / D, bias=K["eps"][:, 0:1])
                act.activation(std[:, :], K["ss"][:, :], ACT.Sqrt, scale=1.0 / D, bias=K["eps"][:, 0:1]).then_inc(rooted, 1)
                for n in range(4):
                    t, c = n // 2, n % 2
                    act.wait_ge(kv_ready, n + 1)
                    act.activation(mkv[:, t, c, :], (qp, op)[c][:, :, :].rearrange("p h n -> p (h n)"), ACT.Copy)\
                       .then_inc(kv_copied, 1)
                for t in range(2):
                    act.wait_ge(k_turned, t + 1)
                    act.activation(mkt[:, :, t * P:(t + 1) * P], tp[:, 4 * t:4 * t + 4, :], ACT.Copy).then_inc(k_copied, 1)

                def copy_queries(t):
                    act.wait_ge(q_ready, t + 1)
                    act.activation(qt[:, :, :], qp[:, :, :], ACT.Copy).then_inc(q_copied, 1)

                def exponents(t):
                    act.wait_ge(m_ready, t + 1)
                    for h in range(4):
                        last = act.activation(pr[:, h, :], sp_[:, h, :], ACT.Exp, scale=MSCALE, bias=negm[:, h:h + 1],
                                              accum_out=den[:, h:h + 1])
                    last.then_inc(p_ready, 1)

                def copy_probs(t):
                    act.wait_ge(p_turned, t + 1)
                    act.activation(pt[:, :, :], tp[:, :, :], ACT.Copy).then_inc(pt_ready, 1)

                def copy_outputs(t):
                    act.wait_ge(o_ready, t + 1)
                    act.activation(ot[:, :, :], op[:, :, :], ACT.Copy).then_inc(o_copied, 1)

                def squares(t):
                    act.wait_ge(h_added, t + 1)
                    act.activation(junk[:, :], tile_of(H, t), ACT.Square, accum_out=K["ss"][:, bass.ds(t, 1)])
                    act.drain()

                copy_queries(0)
                exponents(0)
                with act.Fori(1, NT - 1) as t:
                    copy_probs(t - 1)
                    copy_queries(t)
                    copy_outputs(t - 1)
                    exponents(t)
                    squares(t - 1)
                t = NT - 1
                act.wait_ge(padded, 1)
                copy_probs(t - 1)
                act.wait_ge(q_ready, t + 1)
                for h in range(4):
                    last = act.activation(diag(qpad[:, h, :]), qp[:, h, :].rearrange("p (b n) -> p b n", b=NB), ACT.Copy)
                last.then_inc(q_copied, 1)
                copy_outputs(t - 1)
                exponents(t)
                squares(t - 1)
                copy_probs(t)
                copy_outputs(t)
                squares(t)

            @block.vector
            def _(dve):
                dve.wait_ge(g_in, 32)
                dve.wait_ge(rooted, 1)
                dve.reciprocal(mrstd[:, :], mstd[:, :])
                dve.reciprocal(K["rstd"][:, :], std[:, :])
                dve.drain()
                mnt = [xt, pt]
                for t in range(2):
                    if t:
                        dve.wait_ge(x_turned, t)
                    dve.tensor_scalar(xn[:, :], mem[:, t, :], mrstd[:, t:t + 1], None, ALU.mult).then_inc(x_ready, 1)
                    dve.wait_ge(x_turned, t + 1)
                    dve.tensor_tensor(mnt[t][:, :, :], tp[:, :, :], along(gkv[:, :], P), ALU.mult).then_inc(xt_ready, 1)

                def normed(t):
                    dve.tensor_scalar(xn[:, :], tile_of(H, t), K["rstd"][:, bass.ds(t, 1)], None, ALU.mult)\
                       .then_inc(x_ready, 1)

                def scaled(t):
                    dve.wait_ge(x_turned, t + 1 + 2)
                    dve.tensor_tensor(xt[:, :, :], tp[:, :, :], along(g[:, :], P), ALU.mult).then_inc(xt_ready, 1)

                def maxima(t):
                    dve.wait_ge(s_ready, t + 1)
                    dve.tensor_reduce(mx[:, :], sp_[:, :, :], AXX, ALU.max)
                    dve.drain()
                    dve.tensor_scalar(negm[:, :], mx[:, :], -MSCALE, None, ALU.mult).then_inc(m_ready, 1)

                def divided(t):
                    dve.wait_ge(p_ready, t + 1)
                    dve.reciprocal(rden[:, :], den[:, :])
                    dve.drain()
                    dve.tensor_tensor(pr[:, :, :], pr[:, :, :], along(rden[:, :], NM), ALU.mult).then_inc(p_normed, 1)

                def residual(t):
                    dve.wait_ge(out_ready, t + 1)
                    dve.tensor_tensor(tile_of(H, t), tile_of(H, t), yo[:, :], ALU.add).then_inc(h_added, 1)

                normed(0)
                scaled(0)
                normed(1)
                maxima(0)
                with dve.Fori(1, NT - 1) as t:
                    scaled(t)
                    divided(t - 1)
                    dve.drain()
                    normed(t + 1)
                    maxima(t)
                    residual(t - 1)
                t = NT - 1
                scaled(t)
                divided(t - 1)
                maxima(t)
                residual(t - 1)
                divided(t)
                residual(t)

            @block.tensor
            def _(pe):
                mnt = [xt, pt]

                def turn(n):
                    pe.wait_ge(x_ready, n + 1)
                    for k in range(KD):
                        last = pe.transpose(tp[:, k, :], xn[:, k * P:(k + 1) * P], ident[:, :])
                    last.then_inc(x_turned, 1)

                turn(0)
                pe.wait_ge(xt_ready, 1)
                turn(1)
                for t in range(2):
                    pe.wait_ge(xt_ready, t + 1)
                    for c in range(2):
                        if t:
                            pe.wait_ge(kv_copied, c + 1)
                        else:
                            pe.wait_ge((wk_in, wv_in)[c], 16)
                        for k in range(KD):
                            last = pe.matmul((qp, op)[c][:, :, :].rearrange("p h n -> p (h n)"), mnt[t][:, k, :],
                                             wkv[:, c, k, :], start=(k == 0), stop=(k == KD - 1))
                        last.then_inc(kv_ready, 1)
                for t in range(2):
                    pe.wait_ge(kv_copied, 2 * t + 1)
                    for h in range(4):
                        last = pe.transpose(tp[:, 4 * t + h, :], mkv[:, t, 0, h * P:(h + 1) * P], ident[:, :])
                    last.then_inc(k_turned, 1)
                pe.wait_ge(k_copied, 2)
                pe.wait_ge(kv_copied, 4)

                def queries(t):
                    pe.wait_ge(xt_ready, t + 1 + 2)
                    for h in range(4):
                        for k in range(KD):
                            last = pe.matmul(qp[:, h, :], wq[:, k, h * P:(h + 1) * P], xt[:, k, :],
                                             start=(k == 0), stop=(k == KD - 1))
                    last.then_inc(q_ready, 1)

                def scores(t, first=False, samples=False):
                    pe.wait_ge(q_copied, t + 1)
                    if not first:
                        pe.wait_ge(p_ready, t)
                    for h in range(4):
                        if samples:
                            for b in range(NB):
                                last = pe.matmul(sp_[:, h, :], qpad[:, h, b * P:(b + 1) * P],
                                                 ckt[:, h, b * NM:(b + 1) * NM], start=(b == 0), stop=(b == NB - 1))
                        else:
                            last = pe.matmul(sp_[:, h, :], qt[:, h, :], mkt[:, h, :], start=True, stop=True)
                    last.then_inc(s_ready, 1)

                def turn_probs(t):
                    pe.wait_ge(p_normed, t + 1)
                    pe.wait_ge(xt_ready, min(t + 2, NT) + 2 if isinstance(t, int) else t + 2 + 2)
                    for h in range(4):
                        for j in range(2):
                            last = pe.transpose(tp[:, 2 * h + j, :], pr[:, h, j * P:(j + 1) * P], ident[:, :])
                    last.then_inc(p_turned, 1)

                def values(t, samples=False):
                    pe.wait_ge(pt_ready, t + 1)
                    for h in range(4):
                        if samples:
                            for b in range(NB):
                                for j in range(2):
                                    last = pe.matmul(op[:, h, b * TS:(b + 1) * TS], cv[:, 2 * b + j, h * P:(h + 1) * P],
                                                     pt[:, 2 * h + j, b * TS:(b + 1) * TS], start=(j == 0), stop=(j == 1))
                        else:
                            for j in range(2):
                                last = pe.matmul(op[:, h, :], mkv[:, j, 1, h * P:(h + 1) * P], pt[:, 2 * h + j, :],
                                                 start=(j == 0), stop=(j == 1))
                    last.then_inc(o_ready, 1)

                def output(t, first=False):
                    pe.wait_ge(o_copied, t + 1)
                    if not first:
                        pe.wait_ge(h_added, t)
                    for half in range(2):
                        for h in range(4):
                            last = pe.matmul(yo[:, half * CW:(half + 1) * CW], ot[:, h, :],
                                             wo[:, h, half * CW:(half + 1) * CW], start=(h == 0), stop=(h == 3))
                    last.then_inc(out_ready, 1)

                turn(2)
                pe.wait_ge(w_in, 32)
                queries(0)
                scores(0, first=True)
                turn(3)
                queries(1)
                turn_probs(0)
                values(0)
                scores(1)
                output(0, first=True)
                with pe.Fori(2, NT - 1) as t:
                    pe.wait_ge(pt_ready, t - 1)
                    turn(t + 2)
                    queries(t)
                    turn_probs(t - 1)
                    values(t - 1)
                    scores(t)
                    output(t - 1)
                t = NT - 1
                pe.wait_ge(cache_in, 32)
                pe.wait_ge(pt_ready, t - 1)
                turn(t + 2)
                queries(t)
                turn_probs(t - 1)
                values(t - 1)
                scores(t, samples=True)
                output(t - 1)
                turn_probs(t)
                values(t, samples=True)
                output(t)


PH = 8
NKEY = 128
TOP = 16
OH = 8
ON_ACT = 2
LOW = -3.0e38


def phase_retrieve(nc, sem, K, I, S):
    with ExitStack() as ctx:
        sb, ps = open_phase(nc, ctx, "top")
        wq = sb("wq", [P, KD, D])
        keys = sb("keys", [P, PH, NKEY])
        g = sb("g", [P, KD])
        std = sb("std", [P, NT])
        places = [sb(f"place{s}", [P, 2 * PH * NKEY]) for s in range(2)]
        rest = sb("rest", [P, 2 * PH * NKEY])
        xn = sb("xn", [P, D])
        qt = xn[:, :].rearrange("p (h n) -> p h n", h=PH)
        xt = sb("xt", [P, KD, P])
        sc2 = rest[:, :].rearrange("p (a h n) -> p a h n", a=2, h=PH)
        cand2 = rest[:, :].rearrange("p (h n) -> p h n", h=PH)
        hot = sb("hot", [P, TOP, PH * TOP], BF16)
        val = sb("val", [P, 2, PH, TOP])
        ind = sb("ind", [P, 2, PH, TOP], U32)
        indf = sb("indf", [P, 2, TOP, PH], BF16)
        best = sb("best", [P, PH, TOP])
        pos = sb("pos", [P, PH, TOP], U32)
        part = sb("part", [P, 2, PH * TOP], U32)
        partf = sb("partf", [P, 2, PH * TOP], BF16)
        picked = sb("picked", [P, 3, TOP * PH])
        above = sb("above", [P, PH, TOP])
        mass = sb("mass", [P, PH])
        rmass = sb("rmass", [P, PH])
        carrier = sb("carrier", [P, 1])
        place_of = sb("place_of", [P, TOP, PH * TOP], BF16)
        key_of = sb("key_of", [P, NKEY, OH], BF16)
        iota = sb("iota", [P, NKEY])
        key1t, key2t, gt = sb("key1t", [P, P]), sb("key2t", [P, P], BF16), sb("gt", [P, P])
        left = [sb(f"left{r}", [P, OH, NKEY]) for r in range(2)]
        bare = [sb(f"bare{r}", [P, NKEY, OH], BF16) for r in range(2)]
        right = [sb(f"right{r}", [P, OH, NKEY]) for r in range(2)]
        tile_w = sb("tile_w", [P, NKEY, P])
        tp = ps("t", [P, KD, P])
        qp = ps("q", [P, PH, P])
        kp = [ps(f"k{x}", [P, CW]) for x in range(4)]

        w_in, g_in, iotas = sem("top_w_in"), sem("top_g_in"), sem("top_iotas")
        rooted, rstd_ready = sem("top_rooted"), sem("top_rstd_ready")
        x_ready, x_turned, xt_ready = sem("top_x_ready"), sem("top_x_turned"), sem("top_xt_ready")
        q_ready, q_copied = sem("top_q_ready"), sem("top_q_copied")
        s_ready, s_copied = sem("top_s_ready"), sem("top_s_copied")
        above_ready, e_ready = sem("above_ready"), sem("above_e_ready")
        picked_ready, p_turned, turned_ready = sem("picked_ready"), sem("picked_turned"), sem("turned_ready")
        left_ready, bare_ready = sem("left_ready"), sem("bare_ready")
        pool_scaled, act_scaled = sem("pool_scaled"), sem("act_scaled")
        w_made = sem("w_made")
        w_copied = sem("w_copied")
        w_stored = sem("w_stored")
        x_stored = sem("x_stored")
        H, ident = K["H"], K["ident"]
        batches = P // OH

        with nc.Block() as block:

            @block.sync
            def _(sp):
                sp.dma_start(g[:, :], I["norm_ffn_g"]).then_inc(g_in, 16)
                sp.dma_start(wq[:, :, :], I["w_peer_q"].rearrange("(k p) n -> p k n", p=P)).then_inc(w_in, 16)
                sp.dma_start(keys[:, :, :], I["peer_keys"].rearrange("h p n -> p h n")).then_inc(w_in, 16)
                sp.sem_inc(x_stored, 16)

                def store_x(t):
                    sp.wait_ge(xt_ready, t + 1)
                    sp.dma_start(S["xt"][bass.ds(t, 1)].rearrange("a p k n -> (a p) k n"), xt[:, :, :]).then_inc(x_stored, 16)

                def store_w(t):
                    sp.wait_ge(w_copied, 32 * (t + 1) + 4)
                    sp.dma_start(S["w"][:, bass.ds(t, 1), :, :].rearrange("p a j n -> p (a j n)"),
                                 tile_w[:, :, :].rearrange("p j n -> p (j n)")).then_inc(w_stored, 16)

                store_x(0)
                with sp.Fori(0, NT - 1) as t:
                    store_x(t + 1)
                    store_w(t)
                store_w(NT - 1)
                sp.wait_ge(w_stored, 16 * (NT + 1))
                sp.wait_ge(x_stored, 16 * (NT + 1))

            @block.gpsimd
            def _(pool):
                pool.sem_inc(pool_scaled, 2)

                def rows(dst, pattern):
                    pool.iota(dst, pattern=pattern, base=0, channel_multiplier=0,
                              allow_small_or_imprecise_dtypes=True).then_inc(iotas, 1)
                rows(place_of[:, :, :], [[1, TOP], [0, PH * TOP]])
                rows(key_of[:, :, :], [[1, NKEY], [0, OH]])
                rows(iota[:, :], [[1, NKEY]])
                with pool.Fori(0, NT) as t:
                    with pool.Fori(0, batches // 2) as i:
                        for r in range(2):
                            b = i * 2 + r
                            pool.wait_ge(bare_ready, batches * t + b + 1)
                            pool.wait_ge(w_made, 32 * t + 2 * b + 2)
                            pool.tensor_tensor(right[r][:, 0:OH - ON_ACT, :],
                                               bare[r][:, :, 0:OH - ON_ACT].rearrange("p j n -> p n j"),
                                               along(gt[:, bass.ds(b * OH, OH - ON_ACT)], NKEY), ALU.mult)\
                                .then_inc(pool_scaled, 1)

            @block.scalar
            def _(act):
                act.sem_inc(w_copied, 4)
                act.sem_inc(act_scaled, 2)
                act.sem_inc(w_stored, 16)
                act.activation(std[:, :], K["ss"][:, :], ACT.Sqrt, scale=1.0 / D, bias=K["eps"][:, 0:1]).then_inc(rooted, 1)
                act.wait_ge(g_in, 16)
                act.wait_ge(rstd_ready, 1)

                def scores(t, s):
                    act.activation(xn[:, :], tile_of(H, t), ACT.Copy, scale=K["rstd"][:, bass.ds(t, 1)]).then_inc(x_ready, 1)
                    act.wait_ge(x_turned, t + 1)
                    act.wait_ge(x_stored, 16 * (t + 1))
                    for k in range(KD):
                        last = act.activation(xt[:, k, :], tp[:, k, :], ACT.Copy, scale=g[:, k:k + 1])
                    last.then_inc(xt_ready, 1)
                    act.wait_ge(q_ready, t + 1)
                    act.activation(qt[:, :, :], qp[:, :, :], ACT.Copy).then_inc(q_copied, 1)
                    act.wait_ge(s_ready, t + 1)
                    for x in range(4):
                        last = act.activation(places[s][:, x * CW:(x + 1) * CW], kp[x][:, :], ACT.Copy)
                    last.then_inc(s_copied, 1)

                def scale(t, b, r):
                    act.wait_ge(bare_ready, batches * t + b + 1)
                    act.wait_ge(w_made, 32 * t + 2 * b + 2)
                    for n in range(OH - ON_ACT, OH):
                        last = act.activation(right[r][:, n, :], bare[r][:, :, n], ACT.Copy, scale=gt[:, bass.ds(b * OH + n, 1)])
                    last.then_inc(act_scaled, 1)

                def copy(t, b, r):
                    for x in range(2):
                        act.wait_ge(w_made, 32 * t + 2 * b + x + 1 + 4)
                        act.activation(tile_w[:, :, bass.ds(b * OH + 4 * x, 4)].rearrange("p j n -> p n j"),
                                       kp[2 * r + x][:, :].rearrange("p (n j) -> p n j", n=4), ACT.Copy).then_inc(w_copied, 1)

                def spread(t):
                    act.wait_ge(above_ready, t + 1)
                    act.activation(above[:, :, :], above[:, :, :], ACT.Exp).then_inc(e_ready, 1)
                    act.wait_ge(p_turned, t + 1)
                    act.activation(key1t[:, :], tp[:, 0, :], ACT.Copy)
                    act.activation(key2t[:, :], tp[:, 1, :], ACT.Copy)
                    act.activation(gt[:, :], tp[:, 2, :], ACT.Copy).then_inc(turned_ready, 1)
                    scale(t, 0, 0)
                    act.wait_ge(w_stored, 16 * (t + 1))
                    with act.Fori(0, batches // 2 - 1) as i:
                        for r in range(2):
                            scale(t, i * 2 + r + 1, 1 - r)
                            copy(t, i * 2 + r, r)
                    scale(t, batches - 1, 1)
                    copy(t, batches - 2, 0)
                    copy(t, batches - 1, 1)

                scores(0, 0)
                with act.Fori(0, NT // 2) as i:
                    for s in range(2):
                        scores(i * 2 + s + 1, 1 - s)
                        spread(i * 2 + s)
                spread(NT - 1)

            @block.vector
            def _(dve):
                dve.wait_ge(iotas, 3)
                dve.wait_ge(rooted, 1)
                dve.reciprocal(K["rstd"][:, :], std[:, :]).then_inc(rstd_ready, 1)

                def halves(f):
                    for a in range(2):
                        for h in range(PH):
                            f(a, h)
                    dve.drain()

                def heads(f):
                    for h in range(PH):
                        f(h)
                    dve.drain()

                def choose(t, s):
                    sc = places[s][:, :].rearrange("p (a h n) -> p a h n", a=2, h=PH)
                    cand = places[s][:, :].rearrange("p (h n) -> p h n", h=PH)
                    dve.wait_ge(s_copied, t + 1)
                    dve.memset(carrier[:, :], 0.0)
                    halves(lambda a, h: dve.max(val[:, a, h, 0:8], sc[:, a, h, :]))
                    halves(lambda a, h: dve.max_index(ind[:, a, h, 0:8], val[:, a, h, 0:8], sc[:, a, h, :]))
                    halves(lambda a, h: dve.match_replace(sc2[:, a, h, :], val[:, a, h, 0:8], sc[:, a, h, :], LOW))
                    halves(lambda a, h: dve.max(val[:, a, h, 8:16], sc2[:, a, h, :]))
                    halves(lambda a, h: dve.max_index(ind[:, a, h, 8:16], val[:, a, h, 8:16], sc2[:, a, h, :]))
                    for h in range(PH):
                        dve.tensor_tensor(cand[:, h, :].rearrange("p (a b) -> p a b", a=TOP), along(val[:, 0, h, :], TOP),
                                          over(val[:, 1, h, :], TOP), ALU.add)
                    for a in range(2):
                        dve.tensor_copy(indf[:, a, :, :].rearrange("p j h -> p h j"), ind[:, a, :, :])
                    dve.drain()
                    heads(lambda h: dve.max(best[:, h, 0:8], cand[:, h, :]))
                    heads(lambda h: dve.max_index(pos[:, h, 0:8], best[:, h, 0:8], cand[:, h, :]))
                    heads(lambda h: dve.match_replace(cand2[:, h, :], best[:, h, 0:8], cand[:, h, :], LOW))
                    heads(lambda h: dve.max(best[:, h, 8:16], cand2[:, h, :]))
                    dve.tensor_tensor(above[:, :, :], best[:, :, :], best[:, :, 0:1].to_broadcast([P, PH, TOP]), ALU.subtract)\
                       .then_inc(above_ready, 1)
                    heads(lambda h: dve.max_index(pos[:, h, 8:16], best[:, h, 8:16], cand2[:, h, :]))
                    flat = pos[:, :, :].rearrange("p h k -> p (h k)")
                    dve.tensor_scalar(part[:, 0, :], flat, 4, None, ALU.logical_shift_right)
                    dve.tensor_scalar(part[:, 1, :], flat, 15, None, ALU.bitwise_and)
                    dve.drain()
                    for a in range(2):
                        dve.tensor_copy(partf[:, a, :].rearrange("p (k h) -> p h k", h=PH),
                                        part[:, a, :].rearrange("p (h k) -> p h k", h=PH))
                    for a in range(2):
                        dve.drain()
                        dve.tensor_tensor(hot[:, :, :], over(partf[:, a, :], TOP), place_of[:, :, :], ALU.is_equal)
                        dve.drain()
                        by_head = hot[:, :, :].rearrange("p j (k h) -> p j k h", h=PH)
                        dve.tensor_tensor(by_head, by_head, indf[:, a, :, :].unsqueeze(2).to_broadcast([P, TOP, TOP, PH]), ALU.mult)
                        dve.drain()
                        dve.tensor_reduce(picked[:, a, :], hot[:, :, :].rearrange("p j c -> p c j"), AXX, ALU.add)
                    dve.wait_ge(e_ready, t + 1)
                    dve.tensor_reduce(mass[:, :], above[:, :, :], AXX, ALU.add)
                    dve.drain()
                    dve.reciprocal(rmass[:, :], mass[:, :])
                    dve.drain()
                    dve.tensor_tensor(picked[:, 2, :].rearrange("p (k h) -> p h k", h=PH), above[:, :, :],
                                      along(rmass[:, :], TOP), ALU.mult).then_inc(picked_ready, 1)

                def spread(t):
                    dve.wait_ge(turned_ready, t + 1)
                    dve.memset(carrier[:, :], 0.0)

                    def second_keys(b, r):
                        dve.wait_ge(pool_scaled, batches * t + b - 1 + 2)
                        dve.wait_ge(act_scaled, batches * t + b - 1 + 2)
                        dve.tensor_tensor(bare[r][:, :, :], key_of[:, :, :], over(key2t[:, bass.ds(b * OH, OH)], NKEY),
                                          ALU.is_equal).then_inc(bare_ready, 1)

                    def first_keys(b, r):
                        dve.wait_ge(w_made, 32 * t + 2 * b + 2)
                        dve.tensor_tensor(left[r][:, :, :], over(iota[:, :], OH), along(key1t[:, bass.ds(b * OH, OH)], NKEY),
                                          ALU.is_equal).then_inc(left_ready, 1)

                    second_keys(0, 0)
                    with dve.Fori(0, batches // 2 - 1) as i:
                        for r in range(2):
                            second_keys(i * 2 + r + 1, 1 - r)
                            first_keys(i * 2 + r, r)
                    second_keys(batches - 1, 1)
                    first_keys(batches - 2, 0)
                    first_keys(batches - 1, 1)

                with dve.Fori(0, NT // 2) as i:
                    for s in range(2):
                        choose(i * 2 + s, s)
                        spread(i * 2 + s)
                choose(NT - 1, 0)
                spread(NT - 1)

            @block.tensor
            def _(pe):
                pe.sem_inc(w_made, 4)

                def scores(t, again=True):
                    pe.wait_ge(x_ready, t + 1)
                    for k in range(KD):
                        last = pe.transpose(tp[:, k, :], xn[:, k * P:(k + 1) * P], ident[:, :])
                    last.then_inc(x_turned, 1)
                    if not again:
                        pe.wait_ge(w_in, 32)
                    pe.wait_ge(xt_ready, t + 1)
                    for h in range(PH):
                        for k in range(KD):
                            last = pe.matmul(qp[:, h, :], wq[:, k, h * P:(h + 1) * P], xt[:, k, :],
                                             start=(k == 0), stop=(k == KD - 1))
                    last.then_inc(q_ready, 1)
                    pe.wait_ge(q_copied, t + 1)
                    if again:
                        pe.wait_ge(w_copied, 32 * (t - 1) + 4)
                    for x in range(4):
                        lo = 64 * (x // 2)
                        for h in range(4):
                            hh = 4 * (x % 2) + h
                            last = pe.matmul(kp[x][:, h * P:(h + 1) * P], qt[lo:lo + 64, hh, :], keys[lo:lo + 64, hh, :],
                                             start=True, stop=True)
                    last.then_inc(s_ready, 1)

                def spread(t):
                    pe.wait_ge(picked_ready, t + 1)
                    for x in range(3):
                        last = pe.transpose(tp[:, x, :], picked[:, x, :], ident[:, :])
                    last.then_inc(p_turned, 1)
                    with pe.Fori(0, batches // 2) as i:
                        for r in range(2):
                            b = i * 2 + r
                            pe.wait_ge(left_ready, batches * t + b + 1)
                            pe.wait_ge(pool_scaled, batches * t + b + 1 + 2)
                            pe.wait_ge(act_scaled, batches * t + b + 1 + 2)
                            for n in range(OH):
                                if n % 4 == 0:
                                    pe.wait_ge(w_copied, 32 * t + 2 * b + n // 4 + 1)
                                last = pe.matmul(kp[2 * r + n // 4][:, (n % 4) * P:(n % 4 + 1) * P], left[r][:, n, :],
                                                 right[r][:, n, :], start=True, stop=True)
                                if n % 4 == 3:
                                    last.then_inc(w_made, 1)

                scores(0, again=False)
                with pe.Fori(0, NT - 1) as t:
                    scores(t + 1)
                    spread(t)
                spread(NT - 1)


NH3 = 3
TC = N // NH3
NY = 2 * NT


def phase_experts(nc, sem, K, I, S):
    with ExitStack() as ctx:
        sb, ps = open_phase(nc, ctx, "exp")
        xh, xl = sb("xh", [P, KD, N], F32R), sb("xl", [P, KD, N], F32R)
        u = [sb(f"u{s}", [P, KD, P]) for s in range(2)]
        v = [sb(f"v{s}", [P, D]) for s in range(2)]
        w = [sb(f"w{s}", [P, NT, P]) for s in range(2)]
        uh = [sb(f"uh{s}", [P, KD, P], F32R) for s in range(2)]
        ul = [sb(f"ul{s}", [P, KD, P], F32R) for s in range(2)]
        vh = [sb(f"vh{s}", [P, D], F32R) for s in range(2)]
        vl = [sb(f"vl{s}", [P, D], F32R) for s in range(2)]
        ah = [sb(f"ah{s}", [P, N], F32R) for s in range(2)]
        al = [sb(f"al{s}", [P, N], F32R) for s in range(2)]
        gel = sb("gel", [P, NH3, TC])
        prod = sb("prod", [P, NH3, TC])
        hp = [ps(f"h{x}", [P, CW]) for x in range(NH3)]
        yp = [ps(f"y{x}", [P, CW]) for x in range(4)]

        x_in = [sem("ex_x_in0"), sem("ex_x_in1")]
        xh_ready, xl_ready = sem("ex_xh_ready"), sem("ex_xl_ready")
        u_in = [sem("ex_u_in0"), sem("ex_u_in1")]
        v_in = [sem("ex_v_in0"), sem("ex_v_in1")]
        w_in = [sem("ex_w_in0"), sem("ex_w_in1")]
        uh_ready, ul_ready = sem("ex_uh_ready"), sem("ex_ul_ready")
        vh_ready, vl_ready = sem("ex_vh_ready"), sem("ex_vl_ready")
        h_ready = sem("ex_h_ready")
        h_taken = sem("ex_h_taken")
        p_ready = sem("ex_p_ready")
        ah_ready = sem("ex_ah_ready")
        al_ready = sem("ex_al_ready")
        y_ready = sem("ex_y_ready")
        y_added = sem("ex_y_added")
        H = K["H"]

        with nc.Block() as block:

            @block.sync
            def _(sp):
                def load_u(e, s):
                    sp.dma_start(u[s][:, :, :].rearrange("p k n -> p (k n)"),
                                 I["peer_u"][bass.ds(e, 1)].rearrange("a p n -> (a p) n")).then_inc(u_in[s], 16)

                def load_v(e, s):
                    sp.dma_start(v[s][:, :], I["peer_v"][:, bass.ds(e, 1), :].rearrange("p a n -> p (a n)"))\
                      .then_inc(v_in[s], 16)

                def load_w(e, s):
                    sp.dma_start(w[s][:, :, :], S["w"][:, :, bass.ds(e, 1), :].rearrange("p t a n -> p t (a n)"))\
                      .then_inc(w_in[s], 16)

                load_u(0, 0)
                for t in range(NT):
                    if t >= 2:
                        sp.wait_ge(xl_ready, t - 1)
                    sp.dma_start(v[t % 2][:, :], S["xt"][t].rearrange("p k n -> p (k n)")).then_inc(x_in[t % 2], 16)
                load_w(0, 0)
                load_u(1, 1)
                load_w(1, 1)
                sp.wait_ge(xl_ready, NT)
                load_v(0, 0)
                load_v(1, 1)
                with sp.Fori(0, NKEY // 2 - 1) as i:
                    for s in range(2):
                        e = i * 2 + s
                        sp.wait_ge(ul_ready, e + 1)
                        load_u(e + 2, s)
                        sp.wait_ge(vl_ready, e + 1)
                        load_v(e + 2, s)
                        sp.wait_ge(p_ready, NH3 * (e + 1) + NH3)
                        load_w(e + 2, s)

            @block.scalar
            def _(act):
                act.sem_inc(h_taken, NH3)
                act.sem_inc(ah_ready, NH3)
                def high_u(e, s, turn):
                    act.wait_ge(u_in[s], 16 * (turn + 1))
                    act.activation(uh[s][:, :, :], u[s][:, :, :], ACT.Copy).then_inc(uh_ready, 1)

                def step(e, s, turn, next_turn):
                    if next_turn is not None:
                        act.wait_ge(h_ready, NH3 * e + NH3)
                        high_u(e + 1, 1 - s, next_turn)
                    act.wait_ge(v_in[s], 16 * (turn + 1))
                    act.wait_ge(y_ready, NY * (e + 1))
                    act.activation(vh[s][:, :], v[s][:, :], ACT.Copy).then_inc(vh_ready, 1)

                    def gelu(c):
                        act.wait_ge(h_ready, NH3 * e + c + 1 + NH3)
                        act.wait_ge(p_ready, NH3 * e + c + 1)
                        act.activation(gel[:, c, :], hp[c][:, 0:TC], ACT.Gelu_apprx_tanh).then_inc(h_taken, 1)

                    def high_a(c):
                        act.wait_ge(p_ready, NH3 * e + c + 1 + NH3)
                        act.activation(ah[s][:, c * TC:(c + 1) * TC], prod[:, c, :], ACT.Copy).then_inc(ah_ready, 1)

                    for c in range(NH3):
                        gelu(c)
                        high_a(c)

                high_u(0, 0, 0)
                for t in range(NT):
                    act.wait_ge(x_in[t % 2], 16 * (t // 2 + 1))
                    act.activation(xh[:, :, t * P:(t + 1) * P], v[t % 2][:, :].rearrange("p (k n) -> p k n", k=KD), ACT.Copy).then_inc(xh_ready, 1)
                act.wait_ge(xl_ready, NT)
                step(0, 0, 0, 0)
                with act.Fori(0, NKEY // 2 - 1) as i:
                    step(i * 2 + 1, 1, i, i + 1)
                    step(i * 2 + 2, 0, i + 1, i + 1)
                step(NKEY - 1, 1, NKEY // 2 - 1, None)

            @block.vector
            def _(dve):
                dve.sem_inc(p_ready, NH3)
                dve.sem_inc(y_added, 4)
                def low_u(e, s):
                    dve.wait_ge(uh_ready, e + 1)
                    dve.tensor_tensor(ul[s][:, :, :], u[s][:, :, :], uh[s][:, :, :], ALU.subtract).then_inc(ul_ready, 1)

                def step(e, s, turn, first=False, last=False):
                    dve.drain()
                    if not last:
                        low_u(e + 1, 1 - s)
                    dve.wait_ge(vh_ready, e + 1)
                    dve.tensor_tensor(vl[s][:, :], v[s][:, :], vh[s][:, :], ALU.subtract).then_inc(vl_ready, 1)
                    dve.wait_ge(w_in[s], 16 * (turn + 1))
                    nb = TC // P

                    def weigh(c):
                        dve.wait_ge(h_taken, NH3 * e + c + 1 + NH3)
                        dve.wait_ge(ah_ready, NH3 * e + c + 1)
                        dve.tensor_tensor(prod[:, c, :].rearrange("p (b n) -> p b n", n=P),
                                          gel[:, c, :].rearrange("p (b n) -> p b n", n=P),
                                          w[s][:, c * nb:(c + 1) * nb, :], ALU.mult).then_inc(p_ready, 1)

                    def low_a(c):
                        dve.wait_ge(ah_ready, NH3 * e + c + 1 + NH3)
                        at = slice(c * TC, (c + 1) * TC)
                        dve.tensor_tensor(al[s][:, at], prod[:, c, :], ah[s][:, at], ALU.subtract).then_inc(al_ready, 1)

                    weigh(0)
                    low_a(0)
                    weigh(1)
                    low_a(1)
                    if first:
                        weigh(2)
                        low_a(2)
                    else:
                        add_up(e - 1, 1 - s, 0, 3)
                        weigh(2)
                        add_up(e - 1, 1 - s, 3, 7)
                        low_a(2)
                        add_up(e - 1, 1 - s, 7, NY)

                def add_up(e, s, lo=0, hi=NY):
                    for x in range(lo, hi):
                        dst = H[:, x // 2, (x % 2) * CW:(x % 2 + 1) * CW]
                        dve.wait_ge(y_ready, NY * e + x + 1 + 2 * NY)
                        dve.tensor_tensor(dst, dst, yp[(s * NY + x) % 4][:, :], ALU.add).then_inc(y_added, 1)

                low_u(0, 0)
                for t in range(NT):
                    dve.wait_ge(xh_ready, t + 1)
                    dve.tensor_tensor(xl[:, :, t * P:(t + 1) * P], v[t % 2][:, :].rearrange("p (k n) -> p k n", k=KD), xh[:, :, t * P:(t + 1) * P],
                                      ALU.subtract).then_inc(xl_ready, 1)
                step(0, 0, 0, first=True)
                with dve.Fori(0, NKEY // 2 - 1) as i:
                    step(i * 2 + 1, 1, i)
                    step(i * 2 + 2, 0, i + 1)
                step(NKEY - 1, 1, NKEY // 2 - 1, last=True)
                dve.drain()
                add_up(NKEY - 1, 1)

            @block.tensor
            def _(pe):
                pe.sem_inc(h_ready, NH3)
                pe.sem_inc(y_ready, 2 * NY)

                def hidden(e, s, first=False):
                    pe.wait_ge(ul_ready, e + 1)
                    for c in range(NH3):
                        if first:
                            pe.wait_ge(xl_ready, (c + 1) * NT // NH3)
                        pe.wait_ge(h_taken, NH3 * e + c + 1)
                        at = slice(c * TC, (c + 1) * TC)
                        for k in range(KD):
                            pe.matmul(hp[c][:, 0:TC], uh[s][:, k, :], xh[:, k, at], start=(k == 0), stop=False)
                            pe.matmul(hp[c][:, 0:TC], uh[s][:, k, :], xl[:, k, at], start=False, stop=False)
                            last = pe.matmul(hp[c][:, 0:TC], ul[s][:, k, :], xh[:, k, at], start=False, stop=(k == KD - 1))
                        last.then_inc(h_ready, 1)

                def output(e, s):
                    pe.wait_ge(vl_ready, e + 1)
                    pe.wait_ge(al_ready, NH3 * (e + 1))
                    for x in range(NY):
                        rows, cols = slice(x // 2 * P, (x // 2 + 1) * P), slice(x % 2 * CW, (x % 2 + 1) * CW)
                        y = yp[(s * NY + x) % 4][:, :]
                        pe.wait_ge(y_added, NY * e + x + 1)
                        pe.matmul(y, ah[s][:, rows], vh[s][:, cols], start=True, stop=False)
                        pe.matmul(y, ah[s][:, rows], vl[s][:, cols], start=False, stop=False)
                        pe.matmul(y, al[s][:, rows], vh[s][:, cols], start=False, stop=True).then_inc(y_ready, 1)

                hidden(0, 0, first=True)
                with pe.Fori(0, NKEY // 2 - 1) as i:
                    hidden(i * 2 + 1, 1)
                    output(i * 2, 0)
                    hidden(i * 2 + 2, 0)
                    output(i * 2 + 1, 1)
                hidden(NKEY - 1, 1)
                output(NKEY - 2, 0)
                output(NKEY - 1, 1)


def phase_final(nc, sem, K, I, S):
    with ExitStack() as ctx:
        sb, ps = open_phase(nc, ctx, "fin")
        g = sb("g", [P, D])
        std = sb("std", [P, NT])
        y = sb("y", [P, 3, D])
        junk = sb("junk", [P, D])
        g_in, rooted, y_ready = sem("fin_g_in"), sem("fin_rooted"), sem("fin_y_ready")
        stored = [sem(f"fin_stored{x}") for x in range(3)]
        H = K["H"]

        with nc.Block() as block:

            @block.sync
            def _(sp):
                sp.dma_start(g[:, :], I["final_norm_g"].partition_broadcast(P)).then_inc(g_in, 16)
                for x in range(3):
                    sp.sem_inc(stored[x], 16)
                with sp.Fori(0, 3) as i:
                    for x in range(3):
                        sp.wait_ge(y_ready, i * 3 + x + 1)
                        sp.dma_start(S["y"][bass.ds((i * 3 + x) * P, P), :], y[:, x, :]).then_inc(stored[x], 16)
                for x in range(3):
                    sp.wait_ge(stored[x], 64)

            @block.scalar
            def _(act):
                with act.Fori(0, NT) as t:
                    act.drain()
                    act.activation(junk[:, :], tile_of(H, t), ACT.Square, accum_out=K["ss"][:, bass.ds(t, 1)])
                act.drain()
                act.activation(std[:, :], K["ss"][:, :], ACT.Sqrt, scale=1.0 / D, bias=K["eps"][:, 0:1]).then_inc(rooted, 1)

            @block.vector
            def _(dve):
                dve.wait_ge(g_in, 16)
                dve.wait_ge(rooted, 1)
                dve.reciprocal(K["rstd"][:, :], std[:, :])
                dve.drain()
                with dve.Fori(0, 3) as i:
                    for x in range(3):
                        t = i * 3 + x
                        dve.wait_ge(stored[x], 16 * (i + 1))
                        dve.scalar_tensor_tensor(out=y[:, x, :], in0=tile_of(H, t), scalar=K["rstd"][:, bass.ds(t, 1)],
                                                 in1=g[:, :], op0=ALU.mult, op1=ALU.mult).then_inc(y_ready, 1)


def load_constants(nc, sem, K, I):
    with nc.Block() as block:
        cleared = sem("cleared")

        @block.gpsimd
        def _(pool):
            pool.memset(K["ident"][:, :], 0.0).then_inc(cleared, 1)
            pool.memset(K["eps"][:, :], EPS).then_inc(cleared, 1)
            pool.wait_ge(cleared, 2)
            pool.affine_select(out=K["ident"][:, :], in_=K["ident"][:, :], compare_op=ALU.not_equal, fill=1.0,
                               base=0, pattern=[[-1, P]], channel_multiplier=1)


def build(nc, I, O):
    with ExitStack() as ctx:
        def sem(name):
            return ctx.enter_context(nc.semaphore(name))

        def keep(name, shape, dt=F32):
            return ctx.enter_context(nc.sbuf_tensor(name, shape, dt))

        K = {
            "H": keep("H", [P, NT, D]),
            "ident": keep("ident", [P, P]),
            "eps": keep("eps", [P, 1]),
            "ss": keep("ss", [P, NT]),
            "rstd": keep("rstd", [P, NT]),
        }
        S = {n: nc.dram_tensor(f"s_{n}", shape, F32).ap() for n, shape in SCRATCH.items()}
        S.update(O)
        load_constants(nc, sem, K, I)
        for kept, phases in PHASES:
            with ExitStack() as scope:
                for name, shape in kept.items():
                    K[name] = scope.enter_context(nc.sbuf_tensor(name, shape, F32))
                for phase in phases:
                    phase(nc, sem, K, I, S)


SCRATCH = {
    "xt": (NT, P, KD, P),
    "w": (P, NT, NKEY, P),
    "zt": (ROPED * 4, P, N),
    "skt": (4, P, N),
}
OUTS = {
    "y": (N, D),
    "z": ((ROPED + PLAIN) * N, CW), "skv": (N, 256),
    "mk": (2 * P, CW), "mv": (2 * P, CW),
    "swa_k_sample": (NB, P, P), "swa_v_sample": (NB, P, P),
}


def kernel(**inputs):
    import numpy as _np
    import concourse.bacc as _bacc
    from concourse import mybir as _mybir
    from concourse.bass_utils import run_bass_kernel_spmd as _run

    a = {k: _np.asarray(v) for k, v in inputs.items()}
    arrays = lay_out(a, _np)
    nc = _bacc.Bacc("TRN2", target_bir_lowering=False, num_devices=1)
    ins, feed = {}, {}
    for name, x in arrays.items():
        x = _np.ascontiguousarray(x)
        ins[name] = nc.dram_tensor(f"in_{name}", x.shape, _mybir.dt.from_np(x.dtype), kind="ExternalInput").ap()
        feed[f"in_{name}"] = x
    outs = {n: nc.dram_tensor(f"out_{n}", shape, _mybir.dt.float32, kind="ExternalOutput").ap() for n, shape in OUTS.items()}
    build(nc, ins, outs)
    r = _run(nc, [feed], core_ids=[0]).results[0]
    return give_back({n: r[f"out_{n}"] for n in OUTS})


def rope_tables(np):
    pos = np.concatenate([np.arange(TP), 256 + np.arange(NB * TS) % TS]).astype(np.float32)
    inv = np.float32(10000.0) ** (-np.arange(32, dtype=np.float32) / np.float32(32))
    angle = (pos[:, None] * inv[None, :]).astype(np.float32)
    cos, sin = np.cos(angle), np.sin(angle)
    return np.concatenate([cos, cos], 1).astype(np.float32), np.concatenate([-sin, sin], 1).astype(np.float32)


def lay_out(a, np):
    cols = a["w_in"][0]
    cos, sin = rope_tables(np)
    return {
        "x_prompt": a["x_prompt"][0], "x_sample": a["x_sample"].reshape(N - TP, D),
        "norm_mix_g": a["norm_mix_g"][0].reshape(KD, P).T,
        "w_in": np.concatenate([cols[:, 0:1024], cols[:, 1536:2048], cols[:, 1024:1536], cols[:, 2304:4352],
                                cols[:, 2048:2304]], axis=1),
        "rope_cos": cos, "rope_sin": sin,
        "cache_diff_kt": a["cache_diff_k"][0].reshape(NB, PAST, NH, P).transpose(2, 3, 0, 1).reshape(NH, P, NB * PAST),
        "cache_diff_v": a["cache_diff_v"][0].reshape(NB * PAST, NH * P),
        "lambdas": np.stack([a[f"lambda_{x}"][0] for x in ("q1", "q2", "k1", "k2")]),
        "cache_swa_kt": np.concatenate([a["cache_swa_k"][0].transpose(2, 3, 0, 1).reshape(2, HALF, NB * P)] * 2, axis=1),
        "diff_subln_g": a["diff_subln_g"][0].reshape(P, 1),
        "w_branch_a": a["w_branch_a"][0], "w_branch_b": a["w_branch_b"][0], "w_out": a["w_out"][0],
        "mem_prompt": a["mem_prompt"][0],
        "norm_memkv_g": a["norm_memkv_g"][0].reshape(KD, P).T, "norm_mem_g": a["norm_mem_g"][0].reshape(KD, P).T,
        "w_mem_q": a["w_mem_q"][0], "w_mem_k": a["w_mem_k"][0], "w_mem_v": a["w_mem_v"][0], "w_mem_o": a["w_mem_o"][0],
        "cache_mem_kt": a["cache_mem_k"][0].transpose(2, 3, 0, 1).reshape(4, P, NB * NM),
        "cache_mem_v": a["cache_mem_v"][0].reshape(NB * NM, CW),
        "norm_ffn_g": a["norm_ffn_g"][0].reshape(KD, P).T, "w_peer_q": a["w_peer_q"][0],
        "peer_keys": np.concatenate([a[f"peer_keys{x}"][0].transpose(0, 2, 1) for x in (1, 2)], axis=1),
        "peer_u": a["peer_u"][0].reshape(NKEY, NKEY, KD, P).transpose(1, 3, 2, 0).reshape(NKEY, P, D),
        "peer_v": a["peer_v"][0].reshape(NKEY, NKEY, D),
        "final_norm_g": a["final_norm_g"],
        "swa_sinks": a["swa_sinks"][0],
        "cache_swa_k": a["cache_swa_k"][0].reshape(NB, P, P), "cache_swa_v": a["cache_swa_v"][0].reshape(NB, P, P),
    }



def give_back(o):
    z = o["z"].reshape(ROPED + PLAIN, N, CW)
    dk, dv, skv = z[1], z[3], o["skv"]
    return (
        o["y"][:TP].reshape(1, TP, D), o["y"][TP:].reshape(NB, TS, D),
        dk[:TP].reshape(1, 1, TP, NH, 2, HALF), dv[:TP].reshape(1, 1, TP, NH, P),
        skv[TP - P:TP, 0:P].reshape(1, 1, P, 2, HALF), skv[TP - P:TP, P:2 * P].reshape(1, 1, P, 2, HALF),
        o["mk"].reshape(1, 1, NM, 4, P), o["mv"].reshape(1, 1, NM, 4, P),
        dk[TP:].reshape(1, NB, TS, NH, 2, HALF), dv[TP:].reshape(1, NB, TS, NH, P),
        o["swa_k_sample"].reshape(1, NB, P, 2, HALF), o["swa_v_sample"].reshape(1, NB, P, 2, HALF),
    )


PHASES = [
    ({}, [phase_project]),
    ({"OA": [P, NT, CW], "OB": [P, NT, CW], "sso": [P, NH * NT]}, [phase_diff, phase_window, phase_merge]),
    ({}, [phase_memory, phase_retrieve, phase_experts, phase_final]),
]
```
